# Optimizing a Trainium2 kernel written in Bass

```python
import math
import jax, jax.numpy as jnp
from jax import lax
import numpy as np

D_MODEL = 2048
BATCH = 1
SEQ = 256
DEPTH = 1

SSM_GROUP = 16
SSM_WIDTH = D_MODEL // 2
SSM_GROUPS = SSM_WIDTH // SSM_GROUP
SSM_STATE = 64
DT_MIN = 0.001
DT_MAX = 0.1
N_HEADS = 16
QK_NOPE = 128
QK_ROPE = 64
V_HEAD = 128
Q_LORA = 512
KV_LORA = 512
ROPE_THETA = 10000.0
BLOCK_Q = 128
N_BRANCHES = 2
GATE_WIDTH = N_BRANCHES * D_MODEL
IN_WIDTH = SSM_WIDTH + Q_LORA + KV_LORA + QK_ROPE + GATE_WIDTH
D_FF = -(-8 * D_MODEL // (3 * 256)) * 256
DEEPNORM_ALPHA = (2.0 * DEPTH) ** 0.25
DEEPNORM_BETA = (8.0 * DEPTH) ** -0.25
LN_EPS = 1e-5
RMS_EPS = 1e-6

kernel_name = "hybrid_s5_mla_gated_deepnorm"

def layer_norm(x, g, b):
    x32 = x.astype(jnp.float32)
    mu = jnp.mean(x32, axis=-1, keepdims=True)
    var = jnp.mean(jnp.square(x32 - mu), axis=-1, keepdims=True)
    y = (x32 - mu) * lax.rsqrt(var + LN_EPS) * g.astype(jnp.float32) + b.astype(jnp.float32)
    return y.astype(x.dtype)

def rms_norm(x, g):
    x32 = x.astype(jnp.float32)
    y = x32 * lax.rsqrt(jnp.mean(jnp.square(x32), axis=-1, keepdims=True) + RMS_EPS)
    return (y * g.astype(jnp.float32)).astype(x.dtype)

def rope_tables(positions):
    inv_freq = 1.0 / (ROPE_THETA ** (jnp.arange(0, QK_ROPE, 2, dtype=jnp.float32) / QK_ROPE))
    ang = positions.astype(jnp.float32)[..., None] * inv_freq
    return jnp.cos(ang), jnp.sin(ang)

def apply_rope(t, cos, sin):
    t32 = t.astype(jnp.float32)
    t1, t2 = jnp.split(t32, 2, axis=-1)
    out = jnp.concatenate([t1 * cos - t2 * sin, t1 * sin + t2 * cos], axis=-1)
    return out.astype(t.dtype)

def s5_scan(u, lam_re, lam_im, log_dt, b_re, b_im, c_re, c_im, d_skip):
    f32 = jnp.float32
    bsz, seq, _ = u.shape
    u32 = u.astype(f32).reshape(bsz, seq, SSM_GROUPS, SSM_GROUP)
    lam_re = lam_re.astype(f32)
    lam_im = lam_im.astype(f32)
    dt = jnp.exp(log_dt.astype(f32))[:, None]
    mag = jnp.exp(lam_re * dt)
    ang = lam_im * dt
    abar_re = mag * jnp.cos(ang)
    abar_im = mag * jnp.sin(ang)
    den = jnp.square(lam_re) + jnp.square(lam_im)
    num_re = abar_re - 1.0
    coef_re = (num_re * lam_re + abar_im * lam_im) / den
    coef_im = (abar_im * lam_re - num_re * lam_im) / den
    b_re = b_re.astype(f32)
    b_im = b_im.astype(f32)
    bbar_re = coef_re[..., None] * b_re - coef_im[..., None] * b_im
    bbar_im = coef_re[..., None] * b_im + coef_im[..., None] * b_re
    bu_re = jnp.einsum('bsgp,gnp->bsgn', u32, bbar_re)
    bu_im = jnp.einsum('bsgp,gnp->bsgn', u32, bbar_im)
    a_re = jnp.broadcast_to(abar_re, bu_re.shape)
    a_im = jnp.broadcast_to(abar_im, bu_im.shape)

    def combine(left, right):
        ar1, ai1, br1, bi1 = left
        ar2, ai2, br2, bi2 = right
        ar = ar1 * ar2 - ai1 * ai2
        ai = ar1 * ai2 + ai1 * ar2
        br = ar2 * br1 - ai2 * bi1 + br2
        bi = ar2 * bi1 + ai2 * br1 + bi2
        return ar, ai, br, bi

    _, _, st_re, st_im = lax.associative_scan(combine, (a_re, a_im, bu_re, bu_im), axis=1)
    y = (jnp.einsum('bsgn,gpn->bsgp', st_re, c_re.astype(f32))
         - jnp.einsum('bsgn,gpn->bsgp', st_im, c_im.astype(f32))
         + d_skip.astype(f32) * u32)
    return y.reshape(bsz, seq, SSM_WIDTH).astype(u.dtype)

def mla_attention(q_nope, q_rope, k_nope, k_rope, v):
    bsz, seq = q_nope.shape[:2]
    n_blocks = seq // BLOCK_Q
    scale = 1.0 / math.sqrt(QK_NOPE + QK_ROPE)
    qn_b = q_nope.reshape(bsz, n_blocks, BLOCK_Q, N_HEADS, QK_NOPE).transpose(1, 0, 2, 3, 4)
    qr_b = q_rope.reshape(bsz, n_blocks, BLOCK_Q, N_HEADS, QK_ROPE).transpose(1, 0, 2, 3, 4)
    key_pos = jnp.arange(seq)

    def attend(args):
        blk, qn, qr = args
        s = (jnp.einsum('bqhd,bkhd->bhqk', qn, k_nope)
             + jnp.einsum('bqhr,bkr->bhqk', qr, k_rope)).astype(jnp.float32) * scale
        q_pos = blk * BLOCK_Q + jnp.arange(BLOCK_Q)
        mask = key_pos[None, :] <= q_pos[:, None]
        s = jnp.where(mask[None, None], s, -jnp.inf)
        p = jax.nn.softmax(s, axis=-1).astype(v.dtype)
        return jnp.einsum('bhqk,bkhd->bqhd', p, v)

    o = lax.map(attend, (jnp.arange(n_blocks), qn_b, qr_b))
    return o.transpose(1, 0, 2, 3, 4).reshape(bsz, seq, N_HEADS * V_HEAD)

def setup_inputs(seed: int = 0) -> dict:
    key = jax.random.key(seed)
    ks = jax.random.split(key, 26)
    f32 = jnp.float32
    L = DEPTH

    def nrm(k, shape, scale):
        return jax.random.normal(k, shape, f32) * scale

    x = jax.random.normal(ks[0], (BATCH, SEQ, D_MODEL), f32)
    offset = jax.random.randint(ks[1], (BATCH, 1), 0, 4096, dtype=jnp.int32)
    positions = offset + jnp.arange(SEQ, dtype=jnp.int32)[None, :]

    w_in = nrm(ks[2], (L, D_MODEL, IN_WIDTH), D_MODEL ** -0.5)
    ssm_lambda_re = -0.5 + nrm(ks[3], (L, SSM_GROUPS, SSM_STATE), 0.01)
    ssm_lambda_im = (math.pi * jnp.arange(SSM_STATE, dtype=f32))[None, None, :] + nrm(ks[4], (L, SSM_GROUPS, SSM_STATE), 0.01)
    ssm_log_dt = jax.random.uniform(ks[5], (L, SSM_GROUPS), f32, math.log(DT_MIN), math.log(DT_MAX))
    ssm_b_re = nrm(ks[6], (L, SSM_GROUPS, SSM_STATE, SSM_GROUP), (2.0 * SSM_GROUP) ** -0.5)
    ssm_b_im = nrm(ks[7], (L, SSM_GROUPS, SSM_STATE, SSM_GROUP), (2.0 * SSM_GROUP) ** -0.5)
    ssm_c_re = nrm(ks[8], (L, SSM_GROUPS, SSM_GROUP, SSM_STATE), (2.0 * SSM_STATE) ** -0.5)
    ssm_c_im = nrm(ks[9], (L, SSM_GROUPS, SSM_GROUP, SSM_STATE), (2.0 * SSM_STATE) ** -0.5)
    ssm_d = nrm(ks[10], (L, SSM_GROUPS, SSM_GROUP), 1.0)
    w_glu = nrm(ks[11], (L, SSM_WIDTH, 2 * D_MODEL), SSM_WIDTH ** -0.5)

    q_norm_g = 1.0 + nrm(ks[12], (L, Q_LORA), 0.02)
    w_uq = nrm(ks[13], (L, Q_LORA, N_HEADS * (QK_NOPE + QK_ROPE)), Q_LORA ** -0.5)
    kv_norm_g = 1.0 + nrm(ks[14], (L, KV_LORA), 0.02)
    w_ukv = nrm(ks[15], (L, KV_LORA, N_HEADS * (QK_NOPE + V_HEAD)), KV_LORA ** -0.5)

    w_out = nrm(ks[16], (L, D_MODEL, D_MODEL), DEEPNORM_BETA * D_MODEL ** -0.5)
    ln1_g = 1.0 + nrm(ks[17], (L, D_MODEL), 0.02)
    ln1_b = nrm(ks[18], (L, D_MODEL), 0.02)

    w_ffn_gate = nrm(ks[19], (L, D_MODEL, D_FF), D_MODEL ** -0.5)
    w_ffn_up = nrm(ks[20], (L, D_MODEL, D_FF), D_MODEL ** -0.5)
    w_ffn_down = nrm(ks[21], (L, D_FF, D_MODEL), DEEPNORM_BETA * D_FF ** -0.5)
    ln2_g = 1.0 + nrm(ks[22], (L, D_MODEL), 0.02)
    ln2_b = nrm(ks[23], (L, D_MODEL), 0.02)

    return {
        "x": x, "positions": positions, "w_in": w_in,
        "ssm_lambda_re": ssm_lambda_re, "ssm_lambda_im": ssm_lambda_im, "ssm_log_dt": ssm_log_dt,
        "ssm_b_re": ssm_b_re, "ssm_b_im": ssm_b_im, "ssm_c_re": ssm_c_re, "ssm_c_im": ssm_c_im,
        "ssm_d": ssm_d, "w_glu": w_glu,
        "q_norm_g": q_norm_g, "w_uq": w_uq, "kv_norm_g": kv_norm_g, "w_ukv": w_ukv,
        "w_out": w_out, "ln1_g": ln1_g, "ln1_b": ln1_b,
        "w_ffn_gate": w_ffn_gate, "w_ffn_up": w_ffn_up, "w_ffn_down": w_ffn_down,
        "ln2_g": ln2_g, "ln2_b": ln2_b,
    }

def reference(x, positions, w_in, ssm_lambda_re, ssm_lambda_im, ssm_log_dt, ssm_b_re, ssm_b_im,
              ssm_c_re, ssm_c_im, ssm_d, w_glu, q_norm_g, w_uq, kv_norm_g, w_ukv, w_out,
              ln1_g, ln1_b, w_ffn_gate, w_ffn_up, w_ffn_down, ln2_g, ln2_b):
    bsz, seq, _ = x.shape
    cos, sin = rope_tables(positions)
    cos_h, sin_h = cos[:, :, None, :], sin[:, :, None, :]
    split_at = [SSM_WIDTH, SSM_WIDTH + Q_LORA, SSM_WIDTH + Q_LORA + KV_LORA,
                SSM_WIDTH + Q_LORA + KV_LORA + QK_ROPE]
    h = x
    for l in range(DEPTH):
        z = h @ w_in[l]
        u_ssm, c_q, c_kv, k_rope_raw, gate_logits = jnp.split(z, split_at, axis=-1)

        y_ssm = s5_scan(u_ssm, ssm_lambda_re[l], ssm_lambda_im[l], ssm_log_dt[l], ssm_b_re[l],
                        ssm_b_im[l], ssm_c_re[l], ssm_c_im[l], ssm_d[l])
        glu_a, glu_b = jnp.split(jax.nn.gelu(y_ssm) @ w_glu[l], 2, axis=-1)
        ssm_out = glu_a * jax.nn.sigmoid(glu_b)

        q = (rms_norm(c_q, q_norm_g[l]) @ w_uq[l]).reshape(bsz, seq, N_HEADS, QK_NOPE + QK_ROPE)
        q_nope, q_rope = jnp.split(q, [QK_NOPE], axis=-1)
        q_rope = apply_rope(q_rope, cos_h, sin_h)
        kv = (rms_norm(c_kv, kv_norm_g[l]) @ w_ukv[l]).reshape(bsz, seq, N_HEADS, QK_NOPE + V_HEAD)
        k_nope, v = jnp.split(kv, [QK_NOPE], axis=-1)
        k_rope = apply_rope(k_rope_raw, cos, sin)
        mla_out = mla_attention(q_nope, q_rope, k_nope, k_rope, v)

        g_ssm, g_mla = jnp.split(jax.nn.sigmoid(gate_logits), 2, axis=-1)
        mix = (g_ssm * ssm_out + g_mla * mla_out) @ w_out[l]
        h = layer_norm(DEEPNORM_ALPHA * h + mix, ln1_g[l], ln1_b[l])

        ffn = (jax.nn.silu(h @ w_ffn_gate[l]) * (h @ w_ffn_up[l])) @ w_ffn_down[l]
        h = layer_norm(DEEPNORM_ALPHA * h + ffn, ln2_g[l], ln2_b[l])
    return h


_drawn_inputs = setup_inputs


def setup_inputs(seed=0):
    import zlib

    import numpy as np

    out = dict(_drawn_inputs(seed))
    spreads = {}
    factors = {'ssm_lambda_re': 64.0,
     'ssm_lambda_im': 64.0,
     'ssm_log_dt': 64.0,
     'ssm_b_re': 64.0,
     'ssm_b_im': 64.0,
     'ssm_c_re': 64.0,
     'ssm_c_im': 64.0,
     'q_norm_g': 8.0,
     'kv_norm_g': 8.0,
     'ln1_g': 2.712,
     'ln1_b': 2.727,
     'ln2_g': 7.985,
     'ln2_b': 8.155}
    for name, (base, spread) in spreads.items():
        noise = np.random.default_rng([zlib.crc32(name.encode()), seed]).standard_normal(out[name].shape)
        drawn = base * np.exp(spread * noise) if base else spread * noise
        out[name] = __import__('jax').numpy.asarray(drawn.astype(out[name].dtype))
    for name, factor in factors.items():
        out[name] = (out[name] * factor).astype(out[name].dtype)
    return out
```

```python
from contextlib import ExitStack

import numpy as np
import concourse.bass as bass
from concourse import mybir

P = 128
TOK = 256
D = 2048
SSM_W, LORA, ROPE, HEADS = 1024, 512, 64, 16
GROUP, STATE = 16, 64
D_FF = 5632
ALPHA = 2.0 ** 0.25
LN_EPS, RMS_EPS = 1e-5, 1e-6
SM_SCALE = 1.0 / (192.0 ** 0.5)

KT = D // P
FT = D_FF // P
UT = SSM_W // P
CT = LORA // P
SLAB = 8 * P
RING = 4
HG = HEADS // 4
PAIRS = SSM_W // (2 * GROUP)

FRONT0, FRONT_PER = 0, 4
FRONT_TURNS = 9
HEAD0 = FRONT0 + FRONT_PER * FRONT_TURNS
HEAD_PER, HEAD_HOLE = 24, 5
GLU0 = HEAD0 + HEAD_PER * HG
GLU_PER = 4
OUT0 = GLU0 + GLU_PER * 8
OUT_PER = 8
FFN0 = OUT0 + OUT_PER * 4
FFN_PER, FFN_TURNS = 8, FT // 2
DOWN0 = FFN0 + FFN_PER * FFN_TURNS
DOWN_PER, DOWN_REAL = 24, 22
HEAD_REAL = HEAD_PER - 1
D_HEAD0 = HEAD0
D_GLU0 = D_HEAD0 + HEAD_REAL * HG
D_OUT0 = D_GLU0 + 32
D_FFN0 = D_OUT0 + 32
D_DOWN0 = D_FFN0 + FFN_PER * FFN_TURNS
N_SLABS = D_DOWN0 + DOWN_REAL * 4

C_ID, C_MASK, C_T, C_ONES, C_INVF, C_HALFPI, C_RMSEPS, C_LNEPS = 0, 128, 384, 640, 768, 769, 770, 771
C_N = 772
P_CG, P_D, P_G1, P_B1 = 0, 8, 16, 32
P_N = 48
S_RE, S_IM, S_DT = 0, 1, 2

MAGIC = 12582912.0
TWO_PI = 6.283185
INV_2PI = 0.15915494309189535
PI_A, PI_B, PI_C = 6.28125, 1.93500518798828125e-3, 3.0199159819567e-07
NEG = -1.0e30

F32 = mybir.dt.float32
F32R = mybir.dt.float32r
I32 = mybir.dt.int32
ALU = mybir.AluOpType
ACT = mybir.ActivationFunctionType

DVE_HEAD_STEPS = 87
DVE_GLU_STEPS = 4
DVE_OUT_STEPS = 2
DVE_DOWN_STEPS = 2


class Steps:

    def __init__(self, eng, sem):
        self.eng, self.sem, self.base, self.n = eng, sem, 0, 0

    def __call__(self, ins):
        ins.then_inc(self.sem, 1)
        self.n += 1

    def wait(self):
        self.eng.wait_ge(self.sem, self.base + self.n)

    def enter(self, i, per):
        self.start = self.base + self.n
        self.base, self.n = i * per + self.start, 0

    def leave(self, turns, per):
        assert self.n == per, f"{self.n} steps a turn, not {per}"
        self.base, self.n = self.start + turns * per, 0


def build(nc, slabs, x, pos, consts, cols, ssm, ssm_b, ssm_c, ln_rows, out):
    with ExitStack() as ctx:
        def sem(name):
            return ctx.enter_context(nc.semaphore(name))

        base = 16512

        def at(name, off, shape, dt=F32):
            return nc.alloc_sbuf_tensor_at(name, shape, dt, offset=off)

        o = base
        raw = at("raw", o, [P, RING, SLAB]); o += RING * SLAB * 4
        whi = at("whi", o, [P, RING, SLAB], F32R); o += RING * SLAB * 4
        wlo = at("wlo", o, [P, RING, SLAB], F32R); o += RING * SLAB * 4
        cst = at("cst", o, [P, C_N]); o += 3104
        col = at("col", o, [P, P_N]); o += 192
        stats = at("stats", o, [P, 2, 4, 6]); o += 192
        moments = at("moments", o, [P, 2, 2]); o += 32
        rstd = at("rstd", o, [P, 2]); o += 32
        sm = at("sm", o, [P, 8]); o += 32
        start = at("start", o, [P, 8]); o += 32
        a0 = o
        xT = at("xT", a0, [P, KT, 2, TOK], F32R)
        rows = at("rows", a0, [P, 2, D])
        gb = at("gb", a0 + 16384, [P, 2, D])
        a1 = a0 + 32768
        cT = at("cT", a1, [P, 2 * CT, 2, TOK], F32R)
        cosT = at("cosT", a1 + 16384, [P, 4, TOK])
        sinT = at("sinT", a1 + 20480, [P, 4, TOK])
        prod = at("prod", a1 + 24576, [P, 4, 2 * TOK])
        mixT = at("mixT", a1, [P, KT, 2, TOK], F32R)
        hT = at("hT", a1, [P, KT, 2, TOK], F32R)
        a2 = a1 + 32768
        states = at("states", a2, [P, 2, 2 * TOK])
        tmp = at("tmp", a2, [P, 4, TOK])
        a3 = a2 + 4096
        act = at("act", a3, [P, FT, 2, TOK], F32R)
        o = a3
        mla = at("mla", o, [P, KT, TOK])
        xrow = at("xrow", o, [P, 2, D]); o += 16384
        gate = at("gate", o, [P, KT, TOK]); o += 16384
        zT = at("zT", o, [P, 18, TOK])
        qT = at("qT", o, [P, 4, TOK])
        kT = at("kT", o + 4096, [P, 4, TOK]); o += 18432
        scan = at("scan", o, [P, 2, 2 * TOK])
        yT = at("yT", o, [P, UT, 2, TOK], F32R); o += 4096
        bT = at("bT", o, [P, UT, 2, P]); o += 8192
        cP = at("cP", o, [P, PAIRS, 2, GROUP]); o += 4096
        bslot = at("bslot", o, [P, 2, 2, P])
        tmpB = at("tmpB", o, [P, 6, TOK]); o += 2048
        cslot = at("cslot", o, [P, 8, 2, 2 * GROUP]); o += 2048
        uslot = at("uslot", o, [P, 2, TOK]); o += 2048
        prob = at("prob", o, [P, 384]); o += 1536
        probT = at("probT", o, [P, 384]); o += 1536
        gsum = at("gsum", o, [P, 2, TOK]); o += 2048
        ropecs = at("ropecs", o, [P, 2, TOK]); o += 2048
        sp = at("ssm_small", o, [P, 12, PAIRS]); o += 1536
        vT = at("vT", o, [P, 2, 4 * P]); o += 4096
        qr = at("qr", o, [P, 2, TOK]); o += 2048
        assert o <= a3 + FT * 2 * TOK * 4 and a3 + FT * 2 * TOK * 4 <= nc.sbuf_usable_end
        bpar = at("bpar", a1, [P, 2, PAIRS, GROUP])
        bprod = at("bprod", a1 + 4096, [P, 4, PAIRS * GROUP])
        bpad = at("bpad", a1 + 16384, [P, 2, PAIRS * 2 * GROUP])
        posi = at("posi", a2, [P, TOK], I32)
        ang = at("ang", a2 + 1024, [P, 3, TOK])
        squares = at("squares", a1 + 24576, [P, 8, TOK])
        rinv = at("rinv", a2, [P, 2, TOK])

        ps = ctx.enter_context(nc.psum_tensor("ps", [P, 8, 512], F32))
        GEMM, BU, YP, SC, PT, OP = 0, 2, 4, 5, 6, 7

        ident = cst[:, C_ID:C_ID + P]
        tvals = cst[:, C_T:C_T + TOK]

        raw_ready = [sem(f"raw_ready{s}") for s in range(RING)]
        hi_ready, lo_ready, slab_used = sem("hi_ready"), sem("lo_ready"), sem("slab_used")
        half_done, gemm_free = sem("half_done"), sem("gemm_free")
        in_x = [sem(f"in_x{n}") for n in range(4)]
        in_cst, in_small, in_rows, in_gb = sem("in_cst"), sem("in_small"), sem("in_rows"), sem("in_gb")
        out_stored = sem("out_stored")
        dve_step, act_step = sem("dve_step"), sem("act_step")
        xt_psum, xt_hi, xt_lo = sem("xt_psum"), sem("xt_hi"), sem("xt_lo")
        ssm_exp, ssm_phase, ssm_trig, b_padded, bt_psum, bt_copied = (sem(n) for n in (
            "ssm_exp", "ssm_phase", "ssm_trig", "b_padded", "bt_psum", "bt_copied"))
        rope_phase, rope_trig = sem("rope_phase"), sem("rope_trig")
        sq_ready, ss_psum, rms_root, c_ready, c_hi, c_lo = (sem(n) for n in (
            "sq_ready", "ss_psum", "rms_root", "c_ready", "c_hi", "c_lo"))
        slots_ready, phase_ready, trig_ready, bu_psum, rotated, states_ready, c_done = (
            sem(n) for n in ("slots_ready", "phase_ready", "trig_ready", "bu_psum", "rotated",
                             "states_ready", "c_done"))
        y_free = sem("y_free")
        qk_ready, scores, max_ready, exp_done, prob_ready, pt_psum, pt_copied = (
            sem(n) for n in ("qk_ready", "scores", "max_ready", "exp_done", "prob_ready",
                             "pt_psum", "pt_copied"))
        o_psum, o_read, gate_done = (sem(n) for n in (
            "o_psum", "o_read", "gate_done"))
        y_act, y_hi, y_lo = sem("y_act"), sem("y_hi"), sem("y_lo")
        glu_tanh, mix_sum, mix_hi, mix_lo = (sem(n) for n in (
            "glu_tanh", "mix_sum", "mix_hi", "mix_lo"))
        var_ready, root_ready, normed, h_psum, h_f32, h_hi, h_lo, h_rows = (sem(n) for n in (
            "var_ready", "root_ready", "normed", "h_psum", "h_f32", "h_hi", "h_lo", "h_rows"))
        ffn_silu, ffn_prod, act_hi, act_lo, out_ready = (sem(n) for n in (
            "ffn_silu", "ffn_prod", "act_hi", "act_lo", "out_ready"))

        block = ctx.enter_context(nc.Block())

        @block.sync
        def _(sy):
            def load(v, at_dram, s):
                sy.wait_ge(lo_ready, v - (RING - 1))
                sy.dma_start(raw[:, s:s + 1, :], slabs[bass.ds(at_dram, 1)].rearrange("a p n -> p a n")
                             ).then_inc(raw_ready[s], 16)

            def skip(v, s):
                sy.wait_ge(lo_ready, v - (RING - 1))
                sy.sem_inc(raw_ready[s], 16)

            x_v = x.rearrange("(t p) d -> p t d", p=P)

            def load_x(n):
                cut = slice(n * 512, (n + 1) * 512)
                sy.dma_start(xrow[:, :, cut], x_v[:, :, cut]).then_inc(in_x[n], 16)

            def first_slab(s):
                sy.dma_start(raw[:, s:s + 1, :], slabs[s:s + 1].rearrange("a p n -> p a n")
                             ).then_inc(raw_ready[s], 16)
            load_x(0)
            sy.dma_start(cst[:], consts).then_inc(in_cst, 16)
            load_x(1)
            first_slab(0)
            load_x(2)
            load_x(3)
            first_slab(1)
            sy.dma_start(sp[:, 0:3, :], ssm).then_inc(in_small, 16)
            first_slab(2)
            first_slab(3)
            sy.dma_start(col[:], cols).then_inc(in_small, 16)
            sy.dma_start(bpar[:], ssm_b).then_inc(in_small, 16)
            sy.dma_start(cP[:], ssm_c).then_inc(in_small, 16)
            sy.dma_start(posi[:], pos.to_broadcast([P, TOK])).then_inc(in_small, 16)
            with sy.Fori(1, FRONT_TURNS) as i:
                for k in range(FRONT_PER):
                    load(i * FRONT_PER + k, i * FRONT_PER + k, k)
            with sy.Fori(0, HG) as i:
                for k in range(HEAD_PER):
                    v = i * HEAD_PER + HEAD0 + k
                    if k == HEAD_HOLE:
                        skip(v, k % RING)
                    else:
                        load(v, i * HEAD_REAL + D_HEAD0 + k - (k > HEAD_HOLE), k % RING)
            with sy.Fori(0, 4) as i:
                for k in range(4):
                    load(i * 4 + GLU0 + k, i * 4 + D_GLU0 + k, k)
                sy.wait_ge(slab_used, GLU0)
                sy.dma_start(rows[:, :, bass.ds(i * 512, 512)],
                             x_v[:, :, bass.ds(i * 512, 512)]).then_inc(in_rows, 16)
            with sy.Fori(0, 4) as i:
                for k in range(4):
                    load(i * 4 + (GLU0 + 16) + k, i * 4 + (D_GLU0 + 16) + k, k)
                sy.dma_start(gb[:, :, bass.ds(i * 512, 512)],
                             ln_rows[0:1, :, bass.ds(i * 512, 512)].to_broadcast([P, 2, 512])).then_inc(in_gb, 16)
            with sy.Fori(0, 8) as i:
                for k in range(4):
                    load(i * 4 + OUT0 + k, i * 4 + D_OUT0 + k, k)
            for k in range(FFN_PER):
                load(FFN0 + k, D_FFN0 + k, k % RING)
            with sy.Fori(1, FFN_TURNS) as i:
                for k in range(FFN_PER):
                    load(i * FFN_PER + FFN0 + k, i * FFN_PER + D_FFN0 + k, k % RING)
            sy.wait_ge(h_rows, 4)
            sy.dma_start(gb[:], ln_rows[1:2].rearrange("a b n -> a (b n)").to_broadcast([P, 2 * D])
                         .rearrange("p (b n) -> p b n", b=2)).then_inc(in_gb, 16)
            with sy.Fori(0, 4) as i:
                for k in range(DOWN_PER):
                    v = i * DOWN_PER + DOWN0 + k
                    if k >= DOWN_REAL:
                        skip(v, k % RING)
                    else:
                        load(v, i * DOWN_REAL + D_DOWN0 + k, k % RING)
            out_v = out.rearrange("(t p) d -> p t d", p=P)
            for k in range(4):
                sy.wait_ge(out_ready, k + 1)
                t, h = k // 2, k % 2
                sy.dma_start(out_v[:, t, h * 1024:(h + 1) * 1024],
                             rows[:, t, h * 1024:(h + 1) * 1024]).then_inc(out_stored, 16)
            sy.wait_ge(out_stored, 64)

        def low_part(eng, unit, v, s, empty_after=0):
            eng.wait_ge(hi_ready, v + 1)
            unit.tensor_tensor(wlo[:, s, :], raw[:, s, :], whi[:, s, :].bitcast(F32), ALU.subtract
                               ).then_inc(lo_ready, 1 + empty_after)

        @block.gpsimd
        def _(po):
            nc.gpsimd.memset(bpad[:], 0.0).then_inc(b_padded, 1)
            nc.gpsimd.memset(cslot[:], 0.0).then_inc(b_padded, 1)
            with po.Fori(0, FRONT_TURNS) as i:
                for k in range(FRONT_PER):
                    low_part(po, nc.gpsimd, i * FRONT_PER + FRONT0 + k, k)
            with po.Fori(0, HG) as i:
                for k in range(HEAD_PER):
                    if k != HEAD_HOLE:
                        low_part(po, nc.gpsimd, i * HEAD_PER + HEAD0 + k, k % RING, int(k + 1 == HEAD_HOLE))
            with po.Fori(0, 8) as i:
                for k in range(GLU_PER):
                    low_part(po, nc.gpsimd, i * GLU_PER + GLU0 + k, k)
            for k in range(RING):
                low_part(po, nc.gpsimd, OUT0 + k, k)
            po.wait_ge(in_gb, 64)
            for t in range(2):
                po.wait_ge(h_psum, 8)
                nc.gpsimd.tensor_tensor(rows[:, t, :], rows[:, t, :], gb[:, 0, :], ALU.mult).then_inc(h_rows, 1)
                po.wait_ge(h_rows, 2 * t + 1)
                nc.gpsimd.tensor_tensor(rows[:, t, :], rows[:, t, :], gb[:, 1, :], ALU.add).then_inc(h_rows, 1)

        @block.scalar
        def _(ac):
            st = Steps(ac, act_step)

            def high(i, start, per, k, hole=()):
                if k % per in hole:
                    return
                s = (start + k) % RING
                v = i * per + (start + k)
                if isinstance(i, int) and i == 0 and start + k < RING:
                    ac.wait_ge(raw_ready[s], 16)
                else:
                    ac.wait_ge(raw_ready[s], i * (16 * per // RING) + 16 * ((start + k) // RING + 1))
                    ac.wait_ge(slab_used, v - (RING - 1))
                empty = 0
                while (k + 1 + empty) % per in hole:
                    empty += 1
                nc.scalar.activation(whi[:, s, :], raw[:, s, :], ACT.Copy).then_inc(hi_ready, 1 + empty)

            for k in range(8):
                ac.wait_ge(xt_psum, k + 1)
                nc.scalar.activation(xT[:, 2 * k:2 * k + 2, 0, :],
                                     ps[:, 2 + k % 6, :].rearrange("p (a t) -> p a t", a=2), ACT.Copy).then_inc(xt_hi, 1)
                if k < RING:
                    high(0, 0, FRONT_PER, k)
            ac.wait_ge(in_small, 80)
            ac.wait_ge(in_cst, 16)
            nc.scalar.activation(sp[:, 2, :], sp[:, 2, :], ACT.Exp).then_inc(ssm_exp, 1)
            high(0, FRONT0, FRONT_PER, RING)
            ac.wait_ge(ssm_phase, 1)
            nc.scalar.activation(sp[:, 3, :], sp[:, 3, :], ACT.Exp).then_inc(ssm_exp, 1)
            high(0, FRONT0, FRONT_PER, RING + 1)
            ac.wait_ge(ssm_phase, 2)
            nc.scalar.activation(sp[:, 5, :], sp[:, 4, :], ACT.Sin, scale=TWO_PI).then_inc(ssm_trig, 1)
            st(nc.scalar.activation(sp[:, 6, :], sp[:, 4, :], ACT.Abs))
            st.wait()
            nc.scalar.activation(sp[:, 6, :], sp[:, 6, :], ACT.Sin, scale=-TWO_PI,
                                 bias=cst[:, C_HALFPI:C_HALFPI + 1]).then_inc(ssm_trig, 1)
            high(0, FRONT0, FRONT_PER, RING + 2)
            high(0, FRONT0, FRONT_PER, RING + 3)

            with ac.Fori(1, 5) as i:
                for k in range(FRONT_PER):
                    high(i, FRONT0, FRONT_PER, k + RING)
            ac.wait_ge(rope_phase, 1)
            nc.scalar.activation(ropecs[:, 1, :], ang[:, 0, :], ACT.Sin).then_inc(rope_trig, 1)
            st(nc.scalar.activation(ropecs[:, 0, :], ang[:, 0, :], ACT.Abs))
            st.wait()
            nc.scalar.activation(ropecs[:, 0, :], ropecs[:, 0, :], ACT.Sin, scale=-1.0,
                                 bias=cst[:, C_HALFPI:C_HALFPI + 1]).then_inc(rope_trig, 1)
            for m in range(8):
                ac.wait_ge(gemm_free, m + 1)
                nc.scalar.activation(squares[:, m, :], zT[:, m, :], ACT.Square).then_inc(sq_ready, 1)
            for k in range(FRONT_PER):
                high(5, FRONT0, FRONT_PER, k + RING)
            for n in range(2):
                ac.wait_ge(ss_psum, n + 1)
                nc.scalar.activation(rinv[:, n, :], ps[:, SC + n, 0:TOK], ACT.Sqrt, scale=1.0 / LORA,
                                     bias=cst[:, C_RMSEPS:C_RMSEPS + 1]).then_inc(rms_root, 1)
            for m in range(8):
                ac.wait_ge(c_ready, m + 1)
                nc.scalar.activation(cT[:, m, 0, :], zT[:, m, :], ACT.Copy).then_inc(c_hi, 1)
            with ac.Fori(6, FRONT_TURNS) as i:
                for k in range(FRONT_PER):
                    high(i, FRONT0, FRONT_PER, k + RING)

            with ac.Fori(0, HG) as i:
                def hp(k):
                    high(i, HEAD0, HEAD_PER, k, (HEAD_HOLE,))

                ac.wait_ge(y_free, i * 2 + 1)
                nc.scalar.activation(bslot[:], bT[:, bass.ds(i * 2, 2)], ACT.Copy).then_inc(slots_ready, 1)
                for g in range(2):
                    nc.scalar.activation(cslot[g * 64:(g + 1) * 64, :, :, g * GROUP:(g + 1) * GROUP],
                                         cP[g * 64:(g + 1) * 64, bass.ds(i * 8, 8)], ACT.Copy).then_inc(slots_ready, 1)
                nc.scalar.activation(uslot[:], zT[:, bass.ds(i * 2 + 10, 2), :], ACT.Copy).then_inc(slots_ready, 1)

                def trig(n, part):
                    if part == 0:
                        ac.wait_ge(phase_ready, i * 2 + n + 1)
                        nc.scalar.activation(sinT[:], cosT[:], ACT.Sin, scale=TWO_PI).then_inc(trig_ready, 1)
                        return
                    ac.wait_ge(trig_ready, i * 6 + 3 * n + 1)
                    nc.scalar.activation(cosT[:], cosT[:], ACT.Abs).then_inc(trig_ready, 1)
                    ac.wait_ge(trig_ready, i * 6 + 3 * n + 2)
                    nc.scalar.activation(cosT[:], cosT[:], ACT.Sin, scale=-TWO_PI,
                                         bias=cst[:, C_HALFPI:C_HALFPI + 1]).then_inc(trig_ready, 1)

                def exps(h):
                    ac.wait_ge(max_ready, i * 4 + h + 1)
                    nc.scalar.activation(prob[:, 0:P], prob[:, 0:P], ACT.Exp, bias=sm[:, 2:3], scale=SM_SCALE,
                                         accum_out=sm[:, 4:5]).then_inc(exp_done, 1)
                    nc.scalar.activation(prob[:, P:384], prob[:, P:384], ACT.Exp, bias=sm[:, 3:4], scale=SM_SCALE,
                                         accum_out=sm[:, 5:6]).then_inc(exp_done, 1)

                def tanh_gate(g):
                    ac.wait_ge(gemm_free, i * 20 + 18 + 12 + g + 1)
                    to = mla[:, bass.ds(i * 4 + g, 1), :] if g < 4 else gate[:, bass.ds(i * 4 + g - 4, 1), :]
                    nc.scalar.activation(to, gsum[:, g % 2:g % 2 + 1, :], ACT.Tanh, scale=0.5).then_inc(gate_done, 1)

                def copy_pt(h):
                    ac.wait_ge(pt_psum, i * 4 + h + 1)
                    nc.scalar.activation(probT[:], ps[:, PT, 0:384], ACT.Copy).then_inc(pt_copied, 1)

                trig(0, 0)
                hp(4)
                trig(0, 1)
                for k in range(6, 12):
                    hp(k)
                for g in range(8):
                    if g < 4:
                        exps(g)
                    if g == 3:
                        trig(1, 0)
                        trig(1, 1)
                    hp(12 + 2 * g), hp(13 + 2 * g)
                    tanh_gate(g)
                    if g < 4:
                        copy_pt(g)

            for m in range(UT):
                ac.wait_ge(y_free, m + 2)
                nc.scalar.activation(zT[:, 10 + m, :], zT[:, 10 + m, :], ACT.Gelu_apprx_tanh).then_inc(y_act, 1)
            for m in range(UT):
                ac.wait_ge(y_act, m + 1)
                nc.scalar.activation(yT[:, m, 0, :], zT[:, 10 + m, :], ACT.Copy).then_inc(y_hi, 1)

            with ac.Fori(0, 8) as i:
                for e in range(2):
                    high(i, GLU0, GLU_PER, 2 * e + RING)
                    high(i, GLU0, GLU_PER, 2 * e + 1 + RING)
                    ac.wait_ge(gemm_free, i * 4 + 98 + 2 * e + 2)
                    nc.scalar.activation(tmpB[:, 1, :], tmpB[:, 1, :], ACT.Tanh, scale=0.5).then_inc(glu_tanh, 1)
                    ac.wait_ge(mix_sum, i * 2 + e + 1)
                    nc.scalar.activation(mixT[:, bass.ds(i * 2 + e, 1), 0, :], tmpB[:, 4:5, :], ACT.Copy,
                                         scale=0.5).then_inc(mix_hi, 1)
            with ac.Fori(0, 4) as i:
                for k in range(OUT_PER):
                    high(i, OUT0, OUT_PER, k + RING)

            nc.scalar.activation(start[:, 5:6], cst[:, C_ONES:C_ONES + 1], ACT.Sqrt)
            ac.wait_ge(var_ready, 1)
            nc.scalar.activation(rstd[:], moments[:, :, 1], ACT.Sqrt, bias=cst[:, C_LNEPS:C_LNEPS + 1]).then_inc(root_ready, 1)
            for k in range(KT):
                ac.wait_ge(h_f32, k + 1)
                nc.scalar.activation(hT[:, k, 0, :], tmp[:, k % 4, :], ACT.Copy).then_inc(h_hi, 1)

            with ac.Fori(0, FFN_TURNS) as i:
                for e in range(2):
                    high(i, FFN0, FFN_PER, 4 * e + RING)
                    high(i, FFN0, FFN_PER, 4 * e + 1 + RING)
                    ac.wait_ge(gemm_free, i * 4 + 138 + 2 * e + 1)
                    nc.scalar.activation(tmp[:, 1, :], tmp[:, 0, :], ACT.Silu).then_inc(ffn_silu, 1)
                    high(i, FFN0, FFN_PER, 4 * e + 2 + RING)
                    high(i, FFN0, FFN_PER, 4 * e + 3 + RING)
                    ac.wait_ge(ffn_prod, i * 2 + e + 1)
                    nc.scalar.activation(act[:, bass.ds(i * 2 + e, 1), 0, :], tmp[:, 3:4, :], ACT.Copy).then_inc(act_hi, 1)
            hole = tuple(range(DOWN_REAL, DOWN_PER))
            with ac.Fori(0, 3) as i:
                for k in range(DOWN_PER):
                    high(i, DOWN0, DOWN_PER, k + RING, hole)
            for k in range(DOWN_REAL - RING):
                high(3, DOWN0, DOWN_PER, k + RING, hole)
            nc.scalar.activation(start[:, 6:7], cst[:, C_ONES:C_ONES + 1], ACT.Sqrt)
            ac.wait_ge(var_ready, 2)
            nc.scalar.activation(rstd[:], moments[:, :, 1], ACT.Sqrt, bias=cst[:, C_LNEPS:C_LNEPS + 1]).then_inc(root_ready, 1)

        @block.tensor
        def _(pe):
            mm = nc.tensor.matmul

            def weights_in(v):
                pe.wait_ge(lo_ready, v + 1)

            def bank_free(m):
                if not (isinstance(m, int) and m < 2):
                    pe.wait_ge(gemm_free, m - 1)

            def feature_tile(bank, s, b, src, kts, first, last, inc):
                for n, kt in enumerate(kts):
                    hi = whi[:, s, (b + n) * P:(b + n + 1) * P]
                    lo = wlo[:, s, (b + n) * P:(b + n + 1) * P]
                    mm(ps[:, bank, :], hi, src[:, kt].rearrange("p a t -> p (a t)"),
                       start=(first and n == 0), stop=False)
                    done = last and n == len(kts) - 1
                    ins = mm(ps[:, bank, TOK:512], lo, src[:, kt, 0, :], start=False, stop=done)
                return ins

            def row_tile(bank, s, t, src, kts, first, last):
                for n, kt in enumerate(kts):
                    hi, lo = whi[:, s, n * 512:(n + 1) * 512], wlo[:, s, n * 512:(n + 1) * 512]
                    xh, xl = src[:, kt, 0, t * P:(t + 1) * P], src[:, kt, 1, t * P:(t + 1) * P]
                    mm(ps[:, bank, :], xh, hi, start=(first and n == 0), stop=False)
                    mm(ps[:, bank, :], xh, lo, start=False, stop=False)
                    ins = mm(ps[:, bank, :], xl, hi, start=False, stop=(last and n == len(kts) - 1))
                return ins

            pe.wait_ge(in_cst, 16)
            for k in range(8):
                pe.wait_ge(in_x[k // 2], 16)
                if k >= 6:
                    pe.wait_ge(xt_lo, k - 5)
                for a in range(2):
                    for t in range(2):
                        kt = 2 * k + a
                        ins = nc.tensor.transpose(ps[:, 2 + k % 6, a * TOK + t * P:a * TOK + (t + 1) * P],
                                                  xrow[:, t, kt * P:(kt + 1) * P], ident)
                ins.then_inc(xt_psum, 1)

            def front_turn(i, first):
                for e in range(2):
                    bank_free(i * 2 + e)
                    for h in range(2):
                        v = i * 4 + 2 * e + h
                        weights_in(v)
                        if first and e == 0:
                            pe.wait_ge(xt_lo, 4 * h + 4)
                        ins = feature_tile(e, 2 * e + h, 0, xT, range(8 * h, 8 * h + 8), h == 0, h == 1, None)
                        ins.then_inc(slab_used, 1)

            front_turn(0, True)
            with pe.Fori(1, 6) as i:
                front_turn(i, False)
            for n in range(2):
                for m in range(CT):
                    pe.wait_ge(sq_ready, CT * n + m + 1)
                    ins = mm(ps[:, SC + n, 0:TOK], cst[:, C_ONES:C_ONES + P], squares[:, CT * n + m, :],
                             start=(m == 0), stop=(m == CT - 1))
                ins.then_inc(ss_psum, 1)
            pe.wait_ge(b_padded, 6)
            for c in range(2):
                for q in range(2):
                    for n in range(4):
                        ins = nc.tensor.transpose(ps[:, 2 + q, n * P:(n + 1) * P],
                                                  bpad[:, c, (4 * q + n) * P:(4 * q + n + 1) * P], ident)
                    ins.then_inc(bt_psum, 1)
                if c == 0:
                    pe.wait_ge(bt_copied, 2)
            with pe.Fori(6, FRONT_TURNS) as i:
                front_turn(i, False)

            with pe.Fori(0, HG) as i:
                v0, m0 = i * HEAD_PER + HEAD0, i * 20 + 18

                def latent_tiles(k, m, n_tiles, src0, extra=0):
                    weights_in(v0 + k)
                    for b in range(n_tiles):
                        bank_free(m0 + m + b)
                        ins = feature_tile((m + b) % 2, k % RING, CT * b, cT, range(src0, src0 + CT), True, True, None)
                        if b < n_tiles - 1:
                            ins.then_inc(half_done, 1)
                    ins.then_inc(slab_used, 1 + extra)

                def b_product(b):
                    if b == 0:
                        pe.wait_ge(slots_ready, i * 4 + 4)
                    pe.wait_ge(rotated, i * 4 + b + 1)
                    for e in range(2):
                        q = 2 * (b % 2) + e
                        for c in range(2):
                            ins = mm(ps[:, BU + e, c * TOK:(c + 1) * TOK], bslot[32 * q:32 * q + 32, b // 2, c, :],
                                     uslot[32 * q:32 * q + 32, b // 2, :], start=True, stop=True)
                    ins.then_inc(bu_psum, 1)

                def c_product(b):
                    pe.wait_ge(states_ready, i * 4 + b + 1)
                    if b % 2 == 0:
                        pe.wait_ge(y_free, i * 2 + b // 2 + 1)
                    for e in range(2):
                        q = 2 * (b % 2) + e
                        for c in range(2):
                            ins = mm(ps[32 * q:32 * q + 32, YP, 0:TOK], cslot[:, 2 * b + e, c, :],
                                     states[:, c, e * TOK:(e + 1) * TOK], start=(c == 0), stop=(c == 1))
                    ins.then_inc(c_done, 1)

                def score(h):
                    if h == 0:
                        pe.wait_ge(qk_ready, i + 1)
                    else:
                        pe.wait_ge(max_ready, i * 4 + h)
                    r = 32 * h
                    for q, (c0, n) in enumerate(((0, P), (P, 2 * P))):
                        o_ = ps[:, SC, c0:c0 + n]
                        mm(o_, qT[:, h, q * P:(q + 1) * P], kT[:, h, 0:n], start=True, stop=False)
                        mm(o_, qr[r:r + 32, 0, q * P:(q + 1) * P], zT[r:r + 32, 8, 0:n], start=False, stop=False)
                        ins = mm(o_, qr[r:r + 32, 1, q * P:(q + 1) * P], zT[r:r + 32, 9, 0:n], start=False, stop=True)
                    ins.then_inc(scores, 1)

                def turn_probs(h):
                    pe.wait_ge(prob_ready, i * 4 + h + 1)
                    nc.tensor.transpose(ps[:, PT, 0:P], prob[:, 0:P], ident)
                    nc.tensor.transpose(ps[:, PT, P:2 * P], prob[:, P:2 * P], ident)
                    nc.tensor.transpose(ps[:, PT, 2 * P:3 * P], prob[:, 2 * P:3 * P], ident).then_inc(pt_psum, 1)

                def values(h):
                    pe.wait_ge(pt_copied, i * 4 + h + 1)
                    if h == 0:
                        pe.wait_ge(gemm_free, m0 + 12)
                    pe.wait_ge(o_read, i * 4 + h + 1)
                    mm(ps[:, OP, 0:TOK], vT[:, 0, h * P:(h + 1) * P], probT[:, 0:TOK], start=True, stop=False)
                    mm(ps[:, OP, P:TOK], vT[:, 1, h * P:(h + 1) * P], probT[:, TOK:384], start=False,
                       stop=True).then_inc(o_psum, 1)

                def gate_tile(g):
                    bank_free(m0 + 12 + g)
                    for h in range(2):
                        k = 8 + 2 * g + h
                        weights_in(v0 + k)
                        ins = feature_tile(g % 2, k % RING, 0, xT, range(8 * h, 8 * h + 8), h == 0, h == 1, None)
                        ins.then_inc(slab_used, 1)

                pe.wait_ge(c_lo, 8)
                latent_tiles(0, 0, 2, 0)
                latent_tiles(1, 2, 2, 0)
                b_product(0)
                latent_tiles(2, 4, 2, CT)
                latent_tiles(3, 6, 2, CT)
                latent_tiles(4, 8, 2, 0, extra=1)
                for h in range(2):
                    weights_in(v0 + 6 + h)
                    for t in range(2):
                        if h == 0:
                            bank_free(m0 + 10 + t)
                        ins = row_tile(t, (6 + h) % RING, t, cT, range(CT + 2 * h, CT + 2 * h + 2), h == 0, h == 1)
                        if h == 1 and t == 0:
                            ins.then_inc(half_done, 1)
                    ins.then_inc(slab_used, 1)
                b_product(1)
                score(0)
                gate_tile(0)
                turn_probs(0)
                score(1)
                c_product(0)
                gate_tile(1)
                values(0)
                turn_probs(1)
                score(2)
                gate_tile(2)
                values(1)
                turn_probs(2)
                score(3)
                gate_tile(3)
                c_product(1)
                values(2)
                turn_probs(3)
                b_product(2)
                gate_tile(4)
                values(3)
                b_product(3)
                gate_tile(5)
                gate_tile(6)
                c_product(2)
                gate_tile(7)
                c_product(3)

            def glu_turn(i):
                for e in range(4):
                    bank_free(i * 4 + (98 + e))
                    weights_in(i * GLU_PER + (GLU0 + e))
                    for kt in range(UT):
                        if isinstance(i, int) and e == 0:
                            pe.wait_ge(y_lo, kt + 1)
                        ins = feature_tile(e % 2, e, kt, yT, (kt,), kt == 0, kt == UT - 1, None)
                    ins.then_inc(slab_used, 1)
            glu_turn(0)
            with pe.Fori(1, 8) as i:
                glu_turn(i)

            with pe.Fori(0, 4) as i:
                for k in range(OUT_PER):
                    pe.wait_ge(mix_lo, 2 * k + 2)
                    weights_in(i * OUT_PER + OUT0 + k)
                    for t in range(2):
                        if k == 0:
                            bank_free(i * 2 + 130 + t)
                        ins = row_tile(t, k % RING, t, mixT, (2 * k, 2 * k + 1), k == 0, k == OUT_PER - 1)
                        if k == OUT_PER - 1 and t == 0:
                            ins.then_inc(half_done, 1)
                    ins.then_inc(slab_used, 1)

            for k in range(8):
                for t in range(2):
                    pe.wait_ge(normed, t + 1)
                    if k >= 6 and t == 0:
                        pe.wait_ge(h_f32, 2 * (k - 6) + 2)
                    for a in range(2):
                        ins = nc.tensor.transpose(ps[:, 2 + k % 6, a * TOK + t * P:a * TOK + (t + 1) * P],
                                                  rows[:, t, (2 * k + a) * P:(2 * k + a + 1) * P], ident)
                ins.then_inc(h_psum, 1)

            def ffn_turn(i, first):
                for e in range(4):
                    bank_free(i * 4 + 138 + e)
                    for h in range(2):
                        k = 2 * e + h
                        weights_in(i * FFN_PER + FFN0 + k)
                        for n in range(8):
                            if first and e == 0:
                                pe.wait_ge(h_lo, 8 * h + n + 1)
                            ins = feature_tile(e % 2, k % RING, n, hT, (8 * h + n,), h == 0 and n == 0,
                                               h == 1 and n == 7, None)
                        ins.then_inc(slab_used, 1)
            ffn_turn(0, True)
            with pe.Fori(1, FFN_TURNS) as i:
                ffn_turn(i, False)

            with pe.Fori(0, 4) as i:
                for k in range(DOWN_REAL):
                    pe.wait_ge(act_lo, 2 * k + 2)
                    weights_in(i * DOWN_PER + DOWN0 + k)
                    for t in range(2):
                        if k == 0:
                            bank_free(i * 2 + (138 + 2 * FT) + t)
                        ins = row_tile(t, k % RING, t, act, (2 * k, 2 * k + 1), k == 0, k == DOWN_REAL - 1)
                        if k == DOWN_REAL - 1 and t == 0:
                            ins.then_inc(half_done, 1)
                    ins.then_inc(slab_used, 1 + (DOWN_PER - DOWN_REAL) * (k == DOWN_REAL - 1))

        @block.vector
        def _(ve):
            st = Steps(ve, dve_step)
            V = nc.vector

            def tile_sum(out_, bank, slab=None, half=None):
                if slab is not None:
                    ve.wait_ge(slab_used, slab + 1)
                else:
                    ve.wait_ge(half_done, half + 1)
                V.tensor_reduce(out_, ps[:, bank, :].rearrange("p (a t) -> p t a", a=2), mybir.AxisListType.X, ALU.add
                                ).then_inc(gemm_free, 1)

            for k in range(8):
                ve.wait_ge(xt_hi, k + 1)
                V.tensor_tensor(xT[:, 2 * k:2 * k + 2, 1, :], ps[:, 2 + k % 6, :].rearrange("p (a t) -> p a t", a=2),
                                xT[:, 2 * k:2 * k + 2, 0, :].bitcast(F32), ALU.subtract).then_inc(xt_lo, 1)

            re, im, dt = sp[:, 0, :], sp[:, 1, :], sp[:, 2, :]
            mag, theta, sn, cs = sp[:, 3, :], sp[:, 4, :], sp[:, 5, :], sp[:, 6, :]
            w = [sp[:, 7 + n, :] for n in range(5)]
            ve.wait_ge(ssm_exp, 1)
            V.tensor_tensor(mag, re, dt, ALU.mult).then_inc(ssm_phase, 1)
            st(V.tensor_tensor(w[0], im, dt, ALU.mult)); st.wait()
            st(V.tensor_scalar(w[0], w[0], INV_2PI, None, ALU.mult)); st.wait()
            st(V.tensor_scalar(w[1], w[0], MAGIC, None, ALU.add)); st.wait()
            st(V.tensor_scalar(w[1], w[1], MAGIC, None, ALU.subtract)); st.wait()
            V.tensor_tensor(theta, w[0], w[1], ALU.subtract).then_inc(ssm_phase, 1)
            st(V.tensor_tensor(w[2], re, re, ALU.mult))
            st(V.tensor_tensor(w[3], im, im, ALU.mult)); st.wait()
            st(V.tensor_tensor(w[2], w[2], w[3], ALU.add)); st.wait()
            st(V.reciprocal(w[2], w[2]))
            ve.wait_ge(ssm_trig, 2)
            st(V.tensor_tensor(cs, mag, cs, ALU.mult))
            st(V.tensor_tensor(sn, mag, sn, ALU.mult)); st.wait()
            st(V.tensor_scalar(cs, cs, -1.0, None, ALU.add)); st.wait()
            st(V.tensor_tensor(w[0], cs, re, ALU.mult))
            st(V.tensor_tensor(w[1], sn, im, ALU.mult)); st.wait()
            st(V.tensor_tensor(w[0], w[0], w[1], ALU.add))
            st(V.tensor_tensor(w[4], sn, re, ALU.mult))
            st(V.tensor_tensor(w[3], cs, im, ALU.mult)); st.wait()
            st(V.tensor_tensor(w[1], w[4], w[3], ALU.subtract))
            st(V.tensor_tensor(w[0], w[0], w[2], ALU.mult)); st.wait()
            st(V.tensor_tensor(w[1], w[1], w[2], ALU.mult)); st.wait()
            def wide(a):
                return a.rearrange("p (n o) -> p n o", o=1).to_broadcast([P, PAIRS, GROUP])
            pr = [bprod[:, n, :].rearrange("p (a b) -> p a b", a=PAIRS) for n in range(4)]
            st(V.tensor_tensor(pr[0], bpar[:, 0], wide(w[0]), ALU.mult))
            st(V.tensor_tensor(pr[1], bpar[:, 1], wide(w[1]), ALU.mult))
            st(V.tensor_tensor(pr[2], bpar[:, 1], wide(w[0]), ALU.mult))
            st(V.tensor_tensor(pr[3], bpar[:, 0], wide(w[1]), ALU.mult)); st.wait()
            ve.wait_ge(b_padded, 2)
            for g in range(2):
                half = slice(64 * g, 64 * g + 64)
                for c, (one, two, op) in enumerate(((0, 1, ALU.subtract), (2, 3, ALU.add))):
                    V.tensor_tensor(bpad[half, c].rearrange("p (a b) -> p a b", a=PAIRS)[:, :, g * GROUP:(g + 1) * GROUP],
                                    pr[one][half], pr[two][half], op).then_inc(b_padded, 1)
            st(V.tensor_scalar(cP[:, :, 1, :], cP[:, :, 1, :], -1.0, None, ALU.mult))

            st(V.tensor_copy(ang[:, 0, :], posi[:])); st.wait()
            st(V.tensor_scalar(ang[:, 0, :], ang[:, 0, :], cst[:, C_INVF:C_INVF + 1], None, ALU.mult)); st.wait()
            st(V.tensor_scalar(ang[:, 1, :], ang[:, 0, :], INV_2PI, MAGIC, ALU.mult, ALU.add)); st.wait()
            st(V.tensor_scalar(ang[:, 1, :], ang[:, 1, :], MAGIC, None, ALU.subtract)); st.wait()
            for part in (PI_A, PI_B, PI_C):
                st(V.scalar_tensor_tensor(ang[:, 0, :], ang[:, 1, :], -part, ang[:, 0, :], ALU.mult, ALU.add)); st.wait()
            V.tensor_scalar(ang[:, 0, :], ang[:, 0, :], 3.1415925, -3.1415925, ALU.min, ALU.max).then_inc(rope_phase, 1)

            with ve.Fori(0, 6) as i:
                for e in range(2):
                    tile_sum(zT[:, bass.ds(i * 2 + e, 1), :].rearrange("p a t -> p (a t)"), e, i * 4 + 2 * e + 1)
            cosr, sinr = ropecs[:, 0, :], ropecs[:, 1, :]

            def rotate(t1, t2, out1, out2, signal):
                a, b, c, d = gsum[:, 0, :], gsum[:, 1, :], states[:, 1, 0:TOK], states[:, 1, TOK:]
                st(V.tensor_tensor(a, t1, cosr, ALU.mult))
                st(V.tensor_tensor(b, t2, sinr, ALU.mult))
                st(V.tensor_tensor(c, t1, sinr, ALU.mult))
                st(V.tensor_tensor(d, t2, cosr, ALU.mult)); st.wait()
                st(V.tensor_tensor(out1, a, b, ALU.subtract))
                ins = V.tensor_tensor(out2, c, d, ALU.add)
                if signal is not None:
                    ins.then_inc(signal, 1)

            for c in range(2):
                for q in range(2):
                    ve.wait_ge(bt_psum, 2 * c + q + 1)
                    V.tensor_copy(bT[:, 4 * q:4 * q + 4, c, :], ps[:, 2 + q, :].rearrange("p (a b) -> p a b", a=4)
                                  ).then_inc(bt_copied, 1)
            for n in range(2):
                ve.wait_ge(rms_root, n + 1)
                st(V.reciprocal(rinv[:, n, :], rinv[:, n, :])); st.wait()
                for m in range(CT * n, CT * n + CT):
                    V.scalar_tensor_tensor(zT[:, m, :], zT[:, m, :], col[:, P_CG + m:P_CG + m + 1], rinv[:, n, :],
                                           ALU.mult, ALU.mult).then_inc(c_ready, 1)
            for m in range(8):
                ve.wait_ge(c_hi, m + 1)
                V.tensor_tensor(cT[:, m, 1, :], zT[:, m, :], cT[:, m, 0, :].bitcast(F32), ALU.subtract).then_inc(c_lo, 1)
            ve.wait_ge(rope_trig, 2)
            rotate(zT[:, 8, :], zT[:, 9, :], zT[:, 8, :], zT[:, 9, :], None)
            with ve.Fori(6, FRONT_TURNS) as i:
                for e in range(2):
                    tile_sum(zT[:, bass.ds(i * 2 + e, 1), :].rearrange("p a t -> p (a t)"), e, i * 4 + 2 * e + 1)
            for n, s_ in enumerate((c_done, rotated, o_read, y_free)):
                V.memset(start[:, n:n + 1], 0.0).then_inc(s_, 1)

            def phases(i, n):
                for e in range(4):
                    th = theta_of(i, 4 * n + e)
                    st(V.tensor_scalar(sinT[:, e, :], tvals, th, MAGIC, ALU.mult, ALU.add))
                st.wait()
                st(V.tensor_scalar(sinT[:], sinT[:], MAGIC, None, ALU.subtract)); st.wait()
                for e in range(4):
                    ins = V.scalar_tensor_tensor(cosT[:, e, :], tvals, theta_of(i, 4 * n + e), sinT[:, e, :],
                                                 ALU.mult, ALU.subtract)
                ins.then_inc(phase_ready, 1)

            def theta_of(i, pair):
                return sp[:, 4:6, :].rearrange("p a b -> p (a b)")[:, bass.ds(i * 8 + pair, 1)]

            st.wait()
            phases(0, 0)
            with ve.Fori(0, HG) as i:
                st.enter(i, DVE_HEAD_STEPS)
                v0, m0 = i * HEAD_PER + HEAD0, i * 20 + 18
                xR, xI = scan[:, 0], scan[:, 1]
                sR, sI = states[:, 0], states[:, 1]

                def trig_of(b):
                    return cosT[:, 2 * (b % 2):2 * (b % 2) + 2, :], sinT[:, 2 * (b % 2):2 * (b % 2) + 2, :]

                def of_pairs(a):
                    return a.rearrange("p (a t) -> p a t", a=2)

                def turn_back(b, half):
                    c_, s_ = trig_of(b)
                    uR, uI = ps[:, BU:BU + 2, 0:TOK], ps[:, BU:BU + 2, TOK:512]
                    if half == 0:
                        if b % 2 == 0:
                            ve.wait_ge(trig_ready, i * 6 + 3 * (b // 2) + 3)
                        else:
                            ve.wait_ge(states_ready, i * 4 + b)
                        ve.wait_ge(bu_psum, i * 4 + b + 1)
                        st(V.tensor_tensor(of_pairs(prod[:, 0]), uR, c_, ALU.mult))
                        st(V.tensor_tensor(of_pairs(prod[:, 1]), uI, s_, ALU.mult))
                    else:
                        st(V.tensor_tensor(of_pairs(prod[:, 2]), uI, c_, ALU.mult))
                        V.tensor_tensor(of_pairs(prod[:, 3]), uR, s_, ALU.mult).then_inc(rotated, 1)

                def combine(b):
                    ve.wait_ge(rotated, i * 4 + b + 2)
                    st(V.tensor_tensor(prod[:, 0], prod[:, 0], prod[:, 1], ALU.add))
                    st(V.tensor_tensor(prod[:, 2], prod[:, 2], prod[:, 3], ALU.subtract))

                def recur(b, e):
                    if e == 0:
                        st.wait()
                    a_ = sp[:, 3, bass.ds(i * 8 + (2 * b + e), 1)].to_broadcast([P, TOK])
                    cut = slice(e * TOK, (e + 1) * TOK)
                    st(V.tensor_tensor_scan(xR[:, cut], a_, prod[:, 0, cut], 0.0, ALU.mult, ALU.add))
                    st(V.tensor_tensor_scan(xI[:, cut], a_, prod[:, 2, cut], 0.0, ALU.mult, ALU.add))

                def turn_forward(b, half):
                    c_, s_ = trig_of(b)
                    if half == 0:
                        st.wait()
                        st(V.tensor_tensor(of_pairs(prod[:, 0]), of_pairs(xR), c_, ALU.mult))
                        st(V.tensor_tensor(of_pairs(prod[:, 1]), of_pairs(xI), s_, ALU.mult))
                        st(V.tensor_tensor(of_pairs(prod[:, 2]), of_pairs(xI), c_, ALU.mult))
                    else:
                        st(V.tensor_tensor(of_pairs(prod[:, 3]), of_pairs(xR), s_, ALU.mult)); st.wait()
                        ve.wait_ge(c_done, i * 4 + b + 1)
                        st(V.tensor_tensor(sR, prod[:, 0], prod[:, 1], ALU.subtract))
                        V.tensor_tensor(sI, prod[:, 2], prod[:, 3], ALU.add).then_inc(states_ready, 1)

                def y_tile(n):
                    ve.wait_ge(c_done, i * 4 + 2 * n + 3)
                    ins = V.scalar_tensor_tensor(zT[:, bass.ds(i * 2 + (10 + n), 1), :].rearrange("p a t -> p (a t)"),
                                                 uslot[:, n, :], col[:, bass.ds(i * 2 + (P_D + n), 1)],
                                                 ps[:, YP, 0:TOK], ALU.mult, ALU.add)
                    ins.then_inc(y_free, 1)

                def softmax_max(h):
                    ve.wait_ge(scores, i * 4 + h + 1)
                    V.memset(start[:, 4:5], 0.0)
                    st(V.tensor_tensor_reduce(prob[:, 0:P], ps[:, SC, 0:P], cst[:, C_MASK + P:C_MASK + 2 * P], 1.0,
                                              NEG, ALU.add, ALU.max, sm[:, 0:1]))
                    st(V.tensor_tensor_reduce(prob[:, P:384], ps[:, SC, P:384], cst[:, C_MASK:C_MASK + 2 * P], 1.0,
                                              NEG, ALU.add, ALU.max, sm[:, 1:2])); st.wait()
                    V.tensor_scalar(sm[:, 2:4], sm[:, 0:2], -SM_SCALE, None, ALU.mult).then_inc(max_ready, 1)

                def normalise(h):
                    ve.wait_ge(exp_done, i * 8 + 2 * h + 2)
                    st(V.reciprocal(sm[:, 4:6], sm[:, 4:6])); st.wait()
                    st(V.tensor_scalar(prob[:, 0:P], prob[:, 0:P], sm[:, 4:5], None, ALU.mult))
                    V.tensor_scalar(prob[:, P:384], prob[:, P:384], sm[:, 5:6], None, ALU.mult).then_inc(prob_ready, 1)

                def gate_sum(g):
                    if g >= 2:
                        ve.wait_ge(gate_done, i * 8 + g - 1)
                    tile_sum(gsum[:, g % 2, :], g % 2, v0 + 9 + 2 * g)

                def head_out(h):
                    ve.wait_ge(o_psum, i * 4 + h + 1)
                    ve.wait_ge(gate_done, i * 8 + h + 1)
                    g_ = mla[:, bass.ds(i * 4 + h, 1), :].rearrange("p a t -> p (a t)")
                    V.scalar_tensor_tensor(g_, g_, 1.0, ps[:, OP, 0:TOK], ALU.add, ALU.mult).then_inc(o_read, 1)

                def latent_pair(k, to, h):
                    tile_sum(to[:, h, :], 0, half=i * 6 + k + h // 2)
                    tile_sum(to[:, h + 1, :], 1, slab=v0 + k + h // 2)

                latent_pair(0, qT, 0)
                latent_pair(0, qT, 2)
                latent_pair(2, kT, 0)
                turn_back(0, 0)
                latent_pair(2, kT, 2)
                turn_back(0, 1)
                tile_sum(states[:, 0, 0:TOK], 0, half=i * 6 + 4)
                tile_sum(states[:, 0, TOK:], 1, slab=v0 + 4)
                ve.wait_ge(gemm_free, m0 + 10)
                rotate(states[:, 0, 0:TOK], states[:, 0, TOK:], qr[:, 0, :], qr[:, 1, :], qk_ready)
                combine(0)
                recur(0, 0)
                ve.wait_ge(half_done, i * 6 + 6)
                V.tensor_copy(vT[:, 0, :], ps[:, 0, :]).then_inc(gemm_free, 1)
                ve.wait_ge(slab_used, v0 + 8)
                V.tensor_copy(vT[:, 1, :], ps[:, 1, :]).then_inc(gemm_free, 1)
                recur(0, 1)
                softmax_max(0)
                turn_forward(0, 0)
                normalise(0)
                turn_forward(0, 1)
                gate_sum(0)
                softmax_max(1)
                turn_back(1, 0)
                turn_back(1, 1)
                normalise(1)
                combine(1)
                gate_sum(1)
                recur(1, 0)
                head_out(0)
                softmax_max(2)
                recur(1, 1)
                normalise(2)
                turn_forward(1, 0)
                gate_sum(2)
                turn_forward(1, 1)
                head_out(1)
                softmax_max(3)
                phases(i, 1)
                normalise(3)
                gate_sum(3)
                y_tile(0)
                head_out(2)
                turn_back(2, 0)
                turn_back(2, 1)
                combine(2)
                gate_sum(4)
                recur(2, 0)
                recur(2, 1)
                head_out(3)
                turn_forward(2, 0)
                gate_sum(5)
                turn_forward(2, 1)
                turn_back(3, 0)
                turn_back(3, 1)
                gate_sum(6)
                combine(3)
                recur(3, 0)
                recur(3, 1)
                turn_forward(3, 0)
                turn_forward(3, 1)
                gate_sum(7)
                ve.wait_ge(states_ready, i * 4 + 4)
                phases(i, 2)
                y_tile(1)
            st.leave(HG, DVE_HEAD_STEPS)

            for m in range(UT):
                ve.wait_ge(y_hi, m + 1)
                V.tensor_tensor(yT[:, m, 1, :], zT[:, 10 + m, :], yT[:, m, 0, :].bitcast(F32), ALU.subtract).then_inc(y_lo, 1)

            with ve.Fori(0, 8) as i:
                st.enter(i, DVE_GLU_STEPS)
                v = i * GLU_PER + GLU0

                def mix_tile(e):
                    kt = i * 2 + e
                    ve.wait_ge(glu_tanh, kt + 1)
                    st(V.scalar_tensor_tensor(tmpB[:, 2, :], tmpB[:, 1, :], 1.0, tmpB[:, 5 * e, :], ALU.add, ALU.mult)); st.wait()
                    st(V.scalar_tensor_tensor(tmpB[:, 3:4, :], gate[:, bass.ds(kt, 1), :], 1.0, tmpB[:, 2:3, :],
                                              ALU.add, ALU.mult)); st.wait()
                    ins = V.scalar_tensor_tensor(tmpB[:, 4:5, :], tmpB[:, 3:4, :], 0.5, mla[:, bass.ds(kt, 1), :],
                                                 ALU.mult, ALU.add)
                    ins.then_inc(mix_sum, 1)
                    ve.wait_ge(mix_hi, kt + 1)
                    ins = V.scalar_tensor_tensor(mixT[:, bass.ds(kt, 1), 1, :], tmpB[:, 4:5, :], 0.5,
                                                 mixT[:, bass.ds(kt, 1), 0, :].bitcast(F32), ALU.mult, ALU.subtract)
                    ins.then_inc(mix_lo, 1)
                    ve.wait_ge(mix_lo, kt + 1)

                tile_sum(tmpB[:, 0, :], 0, v)
                tile_sum(tmpB[:, 1, :], 1, v + 1)
                tile_sum(tmpB[:, 5, :], 0, v + 2)
                mix_tile(0)
                tile_sum(tmpB[:, 1, :], 1, v + 3)
                mix_tile(1)
            st.leave(8, DVE_GLU_STEPS)

            def residual_panel(i, m, half0, v_last):
                for t in range(2):
                    if t == 0:
                        ve.wait_ge(half_done, i + half0 + 1)
                    else:
                        ve.wait_ge(slab_used, v_last + 1)
                    r_ = rows[:, t, bass.ds(i * 512, 512)]
                    ins = V.scalar_tensor_tensor(r_, r_, ALPHA, ps[:, t, :], ALU.mult, ALU.add)
                    ins.then_inc(gemm_free, 1)
                    ve.wait_ge(gemm_free, m + t + 1)
                    st(V.bn_stats(stats[:, t, bass.ds(i, 1), :].rearrange("p a b -> p (a b)"), r_))

            def statistics():
                st.wait()
                for t in range(2):
                    ins = V.bn_aggr(moments[:, t, :], stats[:, t, :, :].rearrange("p a b -> p (a b)"))
                ins.then_inc(var_ready, 1)

            ve.wait_ge(in_rows, 64)
            ve.wait_ge(lo_ready, OUT0 + RING)
            with ve.Fori(0, 4) as i:
                st.enter(i, DVE_OUT_STEPS)
                for k in range(OUT_PER - 1):
                    low_part(ve, V, i * OUT_PER + OUT0 + RING + k, k % RING)
                residual_panel(i, i * 2 + 130, 6 * HG, i * OUT_PER + OUT0 + OUT_PER - 1)
                low_part(ve, V, i * OUT_PER + OUT0 + RING + OUT_PER - 1, RING - 1)
            st.leave(4, DVE_OUT_STEPS)
            statistics()
            ve.wait_ge(root_ready, 1)
            st(V.reciprocal(rstd[:], rstd[:])); st.wait()
            for t in range(2):
                V.tensor_scalar(rows[:, t, :], rows[:, t, :], moments[:, t, 0:1], rstd[:, t:t + 1], ALU.subtract,
                                ALU.mult).then_inc(normed, 1)

            def h_low(k):
                ve.wait_ge(h_hi, k + 1)
                V.tensor_tensor(hT[:, k, 1, :], tmp[:, k % 4, :], hT[:, k, 0, :].bitcast(F32), ALU.subtract).then_inc(h_lo, 1)

            for k in range(KT):
                if k % 2 == 0:
                    ve.wait_ge(h_psum, k // 2 + 1)
                if k >= 4:
                    ve.wait_ge(h_lo, k - 3)
                V.tensor_scalar(tmp[:, k % 4, :], ps[:, 2 + (k // 2) % 6, (k % 2) * TOK:(k % 2 + 1) * TOK],
                                col[:, P_G1 + k:P_G1 + k + 1], col[:, P_B1 + k:P_B1 + k + 1], ALU.mult, ALU.add
                                ).then_inc(h_f32, 1)
                if k >= 2:
                    h_low(k - 2)
            h_low(KT - 2)
            h_low(KT - 1)

            with ve.Fori(0, FFN_TURNS) as i:
                for e in range(2):
                    n = i * 2 + e
                    m = i * 4 + 138 + 2 * e
                    v = i * FFN_PER + FFN0 + 4 * e
                    for k in range(2):
                        low_part(ve, V, i * FFN_PER + FFN0 + RING + 4 * e + k, k)
                    tile_sum(tmp[:, 0, :], 0, v + 1)
                    for k in range(2, 4):
                        low_part(ve, V, i * FFN_PER + FFN0 + RING + 4 * e + k, k)
                    tile_sum(tmp[:, 2, :], 1, v + 3)
                    ve.wait_ge(gemm_free, m + 2)
                    ve.wait_ge(ffn_silu, n + 1)
                    ins = V.tensor_tensor(tmp[:, 3, :], tmp[:, 1, :], tmp[:, 2, :], ALU.mult)
                    ins.then_inc(ffn_prod, 1)
                    ve.wait_ge(act_hi, n + 1)
                    ins = V.tensor_tensor(act[:, bass.ds(n, 1), 1, :], tmp[:, 3:4, :],
                                          act[:, bass.ds(n, 1), 0, :].bitcast(F32), ALU.subtract)
                    ins.then_inc(act_lo, 1)
                    ve.wait_ge(act_lo, n + 1)

            ve.wait_ge(h_rows, 4)

            def down_turn(i, last):
                for k in range(DOWN_REAL - RING):
                    low_part(ve, V, i * DOWN_PER + DOWN0 + RING + k, k % RING, 2 * (k == DOWN_REAL - RING - 1))
                if not last:
                    low_part(ve, V, i * DOWN_PER + DOWN0 + DOWN_PER, 0)
                residual_panel(i, i * 2 + (138 + 2 * FT), 6 * HG + 4, i * DOWN_PER + DOWN0 + DOWN_REAL - 1)
                if not last:
                    for k in range(1, RING):
                        low_part(ve, V, i * DOWN_PER + DOWN0 + DOWN_PER + k, k)
            with ve.Fori(0, 3) as i:
                st.enter(i, DVE_DOWN_STEPS)
                down_turn(i, False)
            st.leave(3, DVE_DOWN_STEPS)
            down_turn(3, True)
            statistics()
            ve.wait_ge(root_ready, 2)
            st(V.reciprocal(rstd[:], rstd[:])); st.wait()
            ve.wait_ge(in_gb, 80)
            for t in range(2):
                for h in range(2):
                    r_, cut = rows[:, t, h * 1024:(h + 1) * 1024], slice(h * 1024, (h + 1) * 1024)
                    st(V.scalar_tensor_tensor(r_, r_, moments[:, t, 0:1], gb[:, 0, cut], ALU.subtract, ALU.mult)); st.wait()
                    V.scalar_tensor_tensor(r_, r_, rstd[:, t:t + 1], gb[:, 1, cut], ALU.mult, ALU.add).then_inc(out_ready, 1)


def blocks_for_features(w):
    k, m = w.shape
    t = w.reshape(k // P, P, m // P, P).transpose(2, 1, 0, 3).reshape(m // P, P, k)
    if k >= SLAB:
        return t.reshape(m // P, P, k // SLAB, SLAB).transpose(0, 2, 1, 3).reshape(-1, P, SLAB)
    n = SLAB // k
    return t.reshape(m // P // n, n, P, k).transpose(0, 2, 1, 3).reshape(-1, P, SLAB)


def blocks_for_rows(w):
    return w.reshape(-1, 2, P, 512).transpose(0, 2, 1, 3).reshape(-1, P, SLAB)


def pack_slabs(w_in, w_uq, w_ukv, w_glu, w_out, w_gate, w_up, w_down):
    o_q, o_kv = SSM_W, SSM_W + LORA
    o_kr = o_kv + LORA
    o_gs = o_kr + ROPE
    o_gm = o_gs + D
    half = ROPE // 2
    kr1 = np.concatenate([w_in[:, o_kr:o_kr + half]] * 4, axis=1)
    kr2 = np.concatenate([w_in[:, o_kr + half:o_kr + ROPE]] * 4, axis=1)
    parts = [blocks_for_features(np.concatenate([w_in[:, o_q:o_kr], kr1, kr2, w_in[:, :SSM_W]], axis=1))]
    uq = w_uq.reshape(LORA, HEADS, P + ROPE)
    ukv = w_ukv.reshape(LORA, HEADS, 2 * P)
    for g in range(HG):
        hs = slice(4 * g, 4 * g + 4)
        parts.append(blocks_for_features(uq[:, hs, :P].reshape(LORA, 512)))
        parts.append(blocks_for_features(ukv[:, hs, :P].reshape(LORA, 512)))
        parts.append(blocks_for_features(np.concatenate([uq[:, hs, P:P + half].reshape(LORA, P),
                                                         uq[:, hs, P + half:].reshape(LORA, P)], axis=1)))
        parts.append(blocks_for_rows(ukv[:, hs, P:].reshape(LORA, 512)))
        parts.append(blocks_for_features(w_in[:, o_gm + 512 * g:o_gm + 512 * (g + 1)]))
        parts.append(blocks_for_features(w_in[:, o_gs + 512 * g:o_gs + 512 * (g + 1)]))

    def alternate(a, b):
        k, m = a.shape
        return np.stack([a.reshape(k, m // P, P), b.reshape(k, m // P, P)], axis=2).reshape(k, 2 * m)
    parts.append(blocks_for_features(alternate(w_glu[:, :D], w_glu[:, D:])))
    for n in range(4):
        parts.append(blocks_for_rows(w_out[:, 512 * n:512 * (n + 1)]))
    parts.append(blocks_for_features(alternate(w_gate, w_up)))
    for n in range(4):
        parts.append(blocks_for_rows(w_down[:, 512 * n:512 * (n + 1)]))
    return np.concatenate(parts, axis=0)


def shape_constants():
    c = np.zeros((P, C_N), np.float32)
    c[:, C_ID:C_ID + P] = np.eye(P)
    c[:, C_MASK + P:C_MASK + 2 * P] = np.where(np.arange(P)[None, :] <= np.arange(P)[:, None], 0.0, NEG)
    c[:, C_T:C_T + TOK] = np.arange(TOK)[None, :]
    c[:, C_ONES:C_ONES + P] = 1.0
    inv = (1.0 / (np.float32(10000.0) ** (np.arange(0, ROPE, 2, dtype=np.float32) / ROPE))).astype(np.float32)
    c[:, C_INVF] = np.tile(inv, 4)
    c[:, C_HALFPI] = np.float32(np.pi / 2)
    c[:, C_RMSEPS] = RMS_EPS
    c[:, C_LNEPS] = LN_EPS
    return c


def kernel(**inputs):
    import concourse.bacc as _bacc
    from concourse.bass_utils import run_bass_kernel_spmd as _run

    a = {k: np.asarray(v)[0] for k, v in inputs.items()}

    def by_state(v):
        v = v.reshape(PAIRS, P, *v.shape[2:])
        return np.moveaxis(v, 0, 1)

    log_dt = np.broadcast_to(a["ssm_log_dt"][:, None], (2 * PAIRS, STATE))
    c_of = [by_state(a[n].transpose(0, 2, 1)) for n in ("ssm_c_re", "ssm_c_im")]
    arrays = {
        "slabs": pack_slabs(a["w_in"], a["w_uq"], a["w_ukv"], a["w_glu"], a["w_out"], a["w_ffn_gate"],
                            a["w_ffn_up"], a["w_ffn_down"]),
        "x": a["x"],
        "pos": a["positions"][None, :],
        "consts": shape_constants(),
        "cols": np.concatenate([a[n].reshape(-1, P).T for n in ("q_norm_g", "kv_norm_g", "ssm_d", "ln1_g", "ln1_b")],
                               axis=1),
        "ssm": np.stack([by_state(v) for v in (a["ssm_lambda_re"], a["ssm_lambda_im"], log_dt)], axis=1),
        "ssm_b": np.stack([by_state(a[n]) for n in ("ssm_b_re", "ssm_b_im")], axis=1),
        "ssm_c": np.stack(c_of, axis=2),
        "ln_rows": np.stack([np.stack([a["ln1_g"], a["ln1_b"]]), np.stack([a["ln2_g"], a["ln2_b"]])]),
    }
    nc = _bacc.Bacc("TRN2", target_bir_lowering=False, num_devices=1)
    args, given = [], {}
    for name, v in arrays.items():
        v = np.ascontiguousarray(v)
        given[name] = v
        args.append(nc.dram_tensor(name, v.shape, mybir.dt.from_np(v.dtype), kind="ExternalInput").ap())
    out = nc.dram_tensor("out", (TOK, D), F32, kind="ExternalOutput").ap()
    build(nc, *args, out)
    r = _run(nc, [given], core_ids=[0])
    return r.results[0]["out"].reshape(1, TOK, D)
```

```python
from contextlib import ExitStack

import numpy as np
import concourse.bass as bass
from concourse import mybir

P = 128
TOK = 256
D = 2048
SSM_W, LORA, ROPE, HEADS = 1024, 512, 64, 16
GROUP, STATE = 16, 64
D_FF = 5632
ALPHA = 2.0 ** 0.25
LN_EPS, RMS_EPS = 1e-5, 1e-6
SM_SCALE = 1.0 / (192.0 ** 0.5)

KT = D // P
FT = D_FF // P
UT = SSM_W // P
CT = LORA // P
SLAB = 8 * P
RING = 4
HG = HEADS // 4
PAIRS = SSM_W // (2 * GROUP)

FRONT0, FRONT_PER = 0, 4
FRONT_TURNS = 9
HEAD0 = FRONT0 + FRONT_PER * FRONT_TURNS
HEAD_PER, HEAD_HOLE = 24, 5
GLU0 = HEAD0 + HEAD_PER * HG
GLU_PER = 4
OUT0 = GLU0 + GLU_PER * 8
OUT_PER = 8
FFN0 = OUT0 + OUT_PER * 4
FFN_PER, FFN_TURNS = 8, FT // 2
DOWN0 = FFN0 + FFN_PER * FFN_TURNS
DOWN_PER = 22
HEAD_REAL = HEAD_PER - 1
D_HEAD0 = HEAD0
D_GLU0 = D_HEAD0 + HEAD_REAL * HG
D_OUT0 = D_GLU0 + 32
D_FFN0 = D_OUT0 + 32
D_DOWN0 = D_FFN0 + FFN_PER * FFN_TURNS

C_ID, C_MASK, C_T, C_ONES, C_INVF, C_HALFPI, C_RMSEPS, C_LNEPS = 0, 128, 384, 640, 768, 769, 770, 771
C_N = 772
P_CG, P_D, P_G1, P_B1 = 0, 8, 16, 32
P_N = 48
S_RE, S_IM, S_DT = 0, 1, 2

MAGIC = 12582912.0
TWO_PI = 6.283185
INV_2PI = 0.15915494309189535
PI_A, PI_B, PI_C = 6.28125, 1.93500518798828125e-3, 3.0199159819567e-07
NEG = -1.0e30

F32 = mybir.dt.float32
F32R = mybir.dt.float32r
I32 = mybir.dt.int32
ALU = mybir.AluOpType
ACT = mybir.ActivationFunctionType

DVE_HEAD_STEPS = 87
DVE_GLU_STEPS = 4
DVE_OUT_STEPS = 2


class Steps:

    def __init__(self, eng, sem):
        self.eng, self.sem, self.base, self.n = eng, sem, 0, 0

    def __call__(self, ins):
        ins.then_inc(self.sem, 1)
        self.n += 1

    def wait(self):
        self.eng.wait_ge(self.sem, self.base + self.n)

    def enter(self, i, per):
        self.start = self.base + self.n
        self.base, self.n = i * per + self.start, 0

    def leave(self, turns, per):
        assert self.n == per, f"{self.n} steps a turn, not {per}"
        self.base, self.n = self.start + turns * per, 0


def build(nc, slabs, x, pos, consts, cols, ssm, ssm_b, ssm_c, ln_rows, out):
    with ExitStack() as ctx:
        def sem(name):
            return ctx.enter_context(nc.semaphore(name))

        base = 16512

        def at(name, off, shape, dt=F32):
            return nc.alloc_sbuf_tensor_at(name, shape, dt, offset=off)

        o = base
        raw = at("raw", o, [P, RING, SLAB]); o += RING * SLAB * 4
        whi = at("whi", o, [P, RING, SLAB], F32R); o += RING * SLAB * 4
        wlo = at("wlo", o, [P, RING, SLAB], F32R); o += RING * SLAB * 4
        cst = at("cst", o, [P, C_N]); o += 3104
        col = at("col", o, [P, P_N]); o += 192
        stats = at("stats", o, [P, 2, 4, 6]); o += 192
        moments = at("moments", o, [P, 2, 2]); o += 32
        rstd = at("rstd", o, [P, 2]); o += 32
        sm = at("sm", o, [P, 8]); o += 32
        start = at("start", o, [P, 8]); o += 32
        a0 = o
        xT = at("xT", a0, [P, KT, 2, TOK], F32R)
        rows = at("rows", a0, [P, 2, D])
        gb = at("gb", a0 + 16384, [P, 2, D])
        a1 = a0 + 32768
        cT = at("cT", a1, [P, 2 * CT, 2, TOK], F32R)
        cosT = at("cosT", a1 + 16384, [P, 4, TOK])
        sinT = at("sinT", a1 + 20480, [P, 4, TOK])
        prod = at("prod", a1 + 24576, [P, 4, 2 * TOK])
        mixT = at("mixT", a1, [P, KT, 2, TOK], F32R)
        hT = at("hT", a1, [P, KT, 2, TOK], F32R)
        a2 = a1 + 32768
        states = at("states", a2, [P, 2, 2 * TOK])
        tmp = at("tmp", a2, [P, 4, TOK])
        a3 = a2 + 4096
        act = at("act", a3, [P, FT, 2, TOK], F32R)
        o = a3
        mla = at("mla", o, [P, KT, TOK])
        xrow = at("xrow", o, [P, 2, D]); o += 16384
        gate = at("gate", o, [P, KT, TOK]); o += 16384
        zT = at("zT", o, [P, 18, TOK])
        qT = at("qT", o, [P, 4, TOK])
        kT = at("kT", o + 4096, [P, 4, TOK]); o += 18432
        scan = at("scan", o, [P, 2, 2 * TOK])
        yT = at("yT", o, [P, UT, 2, TOK], F32R); o += 4096
        bT = at("bT", o, [P, UT, 2, P]); o += 8192
        cP = at("cP", o, [P, PAIRS, 2, GROUP]); o += 4096
        bslot = at("bslot", o, [P, 2, 2, P])
        tmpB = at("tmpB", o, [P, 7, TOK]); o += 2048
        cslot = at("cslot", o, [P, 8, 2, 2 * GROUP]); o += 2048
        uslot = at("uslot", o, [P, 2, TOK]); o += 2048
        prob = at("prob", o, [P, 384]); o += 1536
        probT = at("probT", o, [P, 384]); o += 1536
        gsum = at("gsum", o, [P, 2, TOK]); o += 2048
        ropecs = at("ropecs", o, [P, 2, TOK]); o += 2048
        sp = at("ssm_small", o, [P, 12, PAIRS]); o += 1536
        vT = at("vT", o, [P, 2, 4 * P]); o += 4096
        qr = at("qr", o, [P, 2, TOK]); o += 2048
        assert o <= a3 + FT * 2 * TOK * 4 and a3 + FT * 2 * TOK * 4 <= nc.sbuf_usable_end
        bpar = at("bpar", a1, [P, 2, PAIRS, GROUP])
        bprod = at("bprod", a1 + 4096, [P, 4, PAIRS * GROUP])
        bpad = at("bpad", a1 + 16384, [P, 2, PAIRS * 2 * GROUP])
        posi = at("posi", a2, [P, TOK], I32)
        ang = at("ang", a2 + 1024, [P, 3, TOK])
        squares = at("squares", a1 + 24576, [P, 8, TOK])
        rinv = at("rinv", a2, [P, 2, TOK])

        ps = ctx.enter_context(nc.psum_tensor("ps", [P, 8, 512], F32))
        GEMM, BU, YP, SC, PT, OP = 0, 2, 4, 5, 6, 7
        BT_BANKS = (2, 3, 4, 7)

        ident = cst[:, C_ID:C_ID + P]
        tvals = cst[:, C_T:C_T + TOK]

        raw_ready = [sem(f"raw_ready{s}") for s in range(RING)]
        hi_ready, lo_ready, slab_used = sem("hi_ready"), sem("lo_ready"), sem("slab_used")
        half_done, gemm_free = sem("half_done"), sem("gemm_free")
        in_x = [sem(f"in_x{n}") for n in range(4)]
        in_cst, in_ssm, in_small, in_rows, in_gb = sem("in_cst"), sem("in_ssm"), sem("in_small"), sem("in_rows"), sem("in_gb")
        out_stored = sem("out_stored")
        dve_step, act_step = sem("dve_step"), sem("act_step")
        xt_psum, xt_hi, xt_lo = sem("xt_psum"), sem("xt_hi"), sem("xt_lo")
        ssm_exp, ssm_phase, ssm_trig, b_padded, bt_psum = (sem(n) for n in (
            "ssm_exp", "ssm_phase", "ssm_trig", "b_padded", "bt_psum"))
        rope_phase, rope_trig = sem("rope_phase"), sem("rope_trig")
        sq_ready, ss_psum, rms_root, c_ready, c_hi, c_lo = (sem(n) for n in (
            "sq_ready", "ss_psum", "rms_root", "c_ready", "c_hi", "c_lo"))
        slots_ready, phase_ready, trig_ready, bu_psum, rotated, states_ready, c_done = (
            sem(n) for n in ("slots_ready", "phase_ready", "trig_ready", "bu_psum", "rotated",
                             "states_ready", "c_done"))
        y_free = sem("y_free")
        qk_ready, scores, max_ready, exp_done, prob_ready, pt_psum, pt_copied = (
            sem(n) for n in ("qk_ready", "scores", "max_ready", "exp_done", "prob_ready",
                             "pt_psum", "pt_copied"))
        o_psum, o_read, gate_done = (sem(n) for n in (
            "o_psum", "o_read", "gate_done"))
        y_act, y_hi, y_lo = sem("y_act"), sem("y_hi"), sem("y_lo")
        glu_tanh, mix_sum, mix_hi, mix_lo = (sem(n) for n in (
            "glu_tanh", "mix_sum", "mix_hi", "mix_lo"))
        var_ready, root_ready, normed, h_psum, h_f32, h_hi, h_lo, h_rows = (sem(n) for n in (
            "var_ready", "root_ready", "normed", "h_psum", "h_f32", "h_hi", "h_lo", "h_rows"))
        ffn_silu, ffn_prod, act_hi, act_lo, out_ready = (sem(n) for n in (
            "ffn_silu", "ffn_prod", "act_hi", "act_lo", "out_ready"))

        block = ctx.enter_context(nc.Block())

        @block.sync
        def _(sy):
            def load(v, at_dram, s):
                sy.wait_ge(lo_ready, v - (RING - 1))
                sy.dma_start(raw[:, s:s + 1, :], slabs[bass.ds(at_dram, 1)].rearrange("a p n -> p a n")
                             ).then_inc(raw_ready[s], 16)

            def skip(v, s):
                sy.wait_ge(lo_ready, v - (RING - 1))
                sy.sem_inc(raw_ready[s], 16)

            x_v = x.rearrange("(t p) d -> p t d", p=P)

            def load_x(n):
                cut = slice(n * 512, (n + 1) * 512)
                sy.dma_start(xrow[:, :, cut], x_v[:, :, cut]).then_inc(in_x[n], 16)

            def first_slab(s):
                sy.dma_start(raw[:, s:s + 1, :], slabs[s:s + 1].rearrange("a p n -> p a n")
                             ).then_inc(raw_ready[s], 16)
            load_x(0)
            sy.dma_start(cst[:], consts).then_inc(in_cst, 16)
            load_x(1)
            first_slab(0)
            load_x(2)
            first_slab(1)
            load_x(3)
            sy.dma_start(sp[:, 0:3, :], ssm).then_inc(in_ssm, 16)
            first_slab(2)
            first_slab(3)
            load(4, 4, 0)
            load(5, 5, 1)
            sy.dma_start(bpar[:], ssm_b).then_inc(in_small, 16)
            load(6, 6, 2)
            sy.dma_start(cP[:], ssm_c).then_inc(in_small, 16)
            sy.dma_start(col[:], cols).then_inc(in_small, 16)
            sy.dma_start(posi[:], pos.to_broadcast([P, TOK])).then_inc(in_small, 16)
            load(7, 7, 3)
            with sy.Fori(2, FRONT_TURNS) as i:
                for k in range(FRONT_PER):
                    load(i * FRONT_PER + k, i * FRONT_PER + k, k)
            with sy.Fori(0, HG) as i:
                for k in range(HEAD_PER):
                    v = i * HEAD_PER + HEAD0 + k
                    if k == HEAD_HOLE:
                        skip(v, k % RING)
                    else:
                        load(v, i * HEAD_REAL + D_HEAD0 + k - (k > HEAD_HOLE), k % RING)
            with sy.Fori(0, 4) as i:
                for k in range(4):
                    load(i * 4 + GLU0 + k, i * 4 + D_GLU0 + k, k)
                sy.wait_ge(slab_used, GLU0)
                sy.dma_start(rows[:, :, bass.ds(i * 512, 512)],
                             x_v[:, :, bass.ds(i * 512, 512)]).then_inc(in_rows, 16)
            with sy.Fori(0, 4) as i:
                for k in range(4):
                    load(i * 4 + (GLU0 + 16) + k, i * 4 + (D_GLU0 + 16) + k, k)
                sy.dma_start(gb[:, :, bass.ds(i * 512, 512)],
                             ln_rows[0:1, :, bass.ds(i * 512, 512)].to_broadcast([P, 2, 512])).then_inc(in_gb, 16)
            with sy.Fori(0, 8) as i:
                for k in range(4):
                    load(i * 4 + OUT0 + k, i * 4 + D_OUT0 + k, k)
            for k in range(FFN_PER):
                load(FFN0 + k, D_FFN0 + k, k % RING)
            with sy.Fori(1, FFN_TURNS) as i:
                for k in range(FFN_PER):
                    load(i * FFN_PER + FFN0 + k, i * FFN_PER + D_FFN0 + k, k % RING)
            sy.wait_ge(h_rows, 4)
            sy.dma_start(gb[:], ln_rows[1:2].rearrange("a b n -> a (b n)").to_broadcast([P, 2 * D])
                         .rearrange("p (b n) -> p b n", b=2)).then_inc(in_gb, 16)
            with sy.Fori(0, DOWN_PER) as i:
                for k in range(4):
                    load(i * 4 + DOWN0 + k, i * 4 + D_DOWN0 + k, k)
            out_v = out.rearrange("(t p) d -> p t d", p=P)
            for k in range(4):
                sy.wait_ge(out_ready, k + 1)
                t, h = k // 2, k % 2
                sy.dma_start(out_v[:, t, h * 1024:(h + 1) * 1024],
                             rows[:, t, h * 1024:(h + 1) * 1024]).then_inc(out_stored, 16)
            sy.wait_ge(out_stored, 64)

        def low_part(eng, unit, v, s, empty_after=0):
            eng.wait_ge(hi_ready, v + 1)
            unit.tensor_tensor(wlo[:, s, :], raw[:, s, :], whi[:, s, :].bitcast(F32), ALU.subtract
                               ).then_inc(lo_ready, 1 + empty_after)

        @block.gpsimd
        def _(po):
            nc.gpsimd.memset(bpad[:], 0.0).then_inc(b_padded, 1)
            nc.gpsimd.memset(cslot[:], 0.0).then_inc(b_padded, 1)
            with po.Fori(0, FRONT_TURNS) as i:
                for k in range(FRONT_PER):
                    low_part(po, nc.gpsimd, i * FRONT_PER + FRONT0 + k, k)
            with po.Fori(0, HG) as i:
                for k in range(HEAD_PER):
                    if k != HEAD_HOLE:
                        low_part(po, nc.gpsimd, i * HEAD_PER + HEAD0 + k, k % RING, int(k + 1 == HEAD_HOLE))
            with po.Fori(0, 8) as i:
                for k in range(GLU_PER):
                    low_part(po, nc.gpsimd, i * GLU_PER + GLU0 + k, k)
            for k in range(RING):
                low_part(po, nc.gpsimd, OUT0 + k, k)
            po.wait_ge(lo_ready, FFN0)
            for k in range(2 * RING):
                low_part(po, nc.gpsimd, FFN0 + k, k % RING)
            po.wait_ge(in_gb, 64)
            for t in range(2):
                po.wait_ge(h_psum, 8)
                nc.gpsimd.tensor_tensor(rows[:, t, :], rows[:, t, :], gb[:, 0, :], ALU.mult).then_inc(h_rows, 1)
                po.wait_ge(h_rows, 2 * t + 1)
                nc.gpsimd.tensor_tensor(rows[:, t, :], rows[:, t, :], gb[:, 1, :], ALU.add).then_inc(h_rows, 1)

        @block.scalar
        def _(ac):
            st = Steps(ac, act_step)

            def high(i, start, per, k, hole=()):
                if k % per in hole:
                    return
                s = (start + k) % RING
                v = i * per + (start + k)
                if isinstance(i, int) and i == 0 and start + k < RING:
                    ac.wait_ge(raw_ready[s], 16)
                else:
                    ac.wait_ge(raw_ready[s], i * (16 * per // RING) + 16 * ((start + k) // RING + 1))
                    ac.wait_ge(slab_used, v - (RING - 1))
                empty = 0
                while (k + 1 + empty) % per in hole:
                    empty += 1
                nc.scalar.activation(whi[:, s, :], raw[:, s, :], ACT.Copy).then_inc(hi_ready, 1 + empty)

            for k in range(8):
                ac.wait_ge(xt_psum, k + 1)
                nc.scalar.activation(xT[:, 2 * k:2 * k + 2, 0, :],
                                     ps[:, 2 + k % 6, :].rearrange("p (a t) -> p a t", a=2), ACT.Copy).then_inc(xt_hi, 1)
                if k in (3, 5):
                    high(0, 0, FRONT_PER, (k - 3) // 2)
            high(0, 0, FRONT_PER, 2)
            high(0, 0, FRONT_PER, 3)
            ac.wait_ge(in_ssm, 16)
            ac.wait_ge(in_cst, 16)
            nc.scalar.activation(sp[:, 2, :], sp[:, 2, :], ACT.Exp).then_inc(ssm_exp, 1)
            high(0, FRONT0, FRONT_PER, RING)
            high(0, FRONT0, FRONT_PER, RING + 1)
            ac.wait_ge(ssm_phase, 1)
            nc.scalar.activation(sp[:, 3, :], sp[:, 3, :], ACT.Exp).then_inc(ssm_exp, 1)
            high(0, FRONT0, FRONT_PER, RING + 2)
            ac.wait_ge(ssm_phase, 2)
            nc.scalar.activation(sp[:, 5, :], sp[:, 4, :], ACT.Sin, scale=TWO_PI).then_inc(ssm_trig, 1)
            st(nc.scalar.activation(sp[:, 6, :], sp[:, 4, :], ACT.Abs))
            st.wait()
            nc.scalar.activation(sp[:, 6, :], sp[:, 6, :], ACT.Sin, scale=-TWO_PI,
                                 bias=cst[:, C_HALFPI:C_HALFPI + 1]).then_inc(ssm_trig, 1)
            high(0, FRONT0, FRONT_PER, RING + 3)

            with ac.Fori(1, 5) as i:
                for k in range(FRONT_PER):
                    high(i, FRONT0, FRONT_PER, k + RING)
            ac.wait_ge(rope_phase, 1)
            nc.scalar.activation(ropecs[:, 1, :], ang[:, 0, :], ACT.Sin).then_inc(rope_trig, 1)
            st(nc.scalar.activation(ropecs[:, 0, :], ang[:, 0, :], ACT.Abs))
            st.wait()
            nc.scalar.activation(ropecs[:, 0, :], ropecs[:, 0, :], ACT.Sin, scale=-1.0,
                                 bias=cst[:, C_HALFPI:C_HALFPI + 1]).then_inc(rope_trig, 1)
            for m in range(8):
                ac.wait_ge(gemm_free, m + 1)
                nc.scalar.activation(squares[:, m, :], zT[:, m, :], ACT.Square).then_inc(sq_ready, 1)
            for k in range(FRONT_PER):
                high(5, FRONT0, FRONT_PER, k + RING)
            for n in range(2):
                ac.wait_ge(ss_psum, n + 1)
                nc.scalar.activation(rinv[:, n, :], ps[:, SC + n, 0:TOK], ACT.Sqrt, scale=1.0 / LORA,
                                     bias=cst[:, C_RMSEPS:C_RMSEPS + 1]).then_inc(rms_root, 1)
            for m in range(8):
                ac.wait_ge(c_ready, m + 1)
                nc.scalar.activation(cT[:, m, 0, :], zT[:, m, :], ACT.Copy).then_inc(c_hi, 1)
            with ac.Fori(6, FRONT_TURNS) as i:
                for k in range(FRONT_PER):
                    high(i, FRONT0, FRONT_PER, k + RING)

            with ac.Fori(0, HG) as i:
                def hp(k):
                    high(i, HEAD0, HEAD_PER, k, (HEAD_HOLE,))

                ac.wait_ge(y_free, i * 2 + 1)
                nc.scalar.activation(bslot[:], bT[:, bass.ds(i * 2, 2)], ACT.Copy).then_inc(slots_ready, 1)
                for g in range(2):
                    nc.scalar.activation(cslot[g * 64:(g + 1) * 64, :, :, g * GROUP:(g + 1) * GROUP],
                                         cP[g * 64:(g + 1) * 64, bass.ds(i * 8, 8)], ACT.Copy).then_inc(slots_ready, 1)
                nc.scalar.activation(uslot[:], zT[:, bass.ds(i * 2 + 10, 2), :], ACT.Copy).then_inc(slots_ready, 1)

                def trig(n, part):
                    if part == 0:
                        ac.wait_ge(phase_ready, i * 2 + n + 1)
                        nc.scalar.activation(sinT[:], cosT[:], ACT.Sin, scale=TWO_PI).then_inc(trig_ready, 1)
                        return
                    ac.wait_ge(trig_ready, i * 6 + 3 * n + 1)
                    nc.scalar.activation(cosT[:], cosT[:], ACT.Abs).then_inc(trig_ready, 1)
                    ac.wait_ge(trig_ready, i * 6 + 3 * n + 2)
                    nc.scalar.activation(cosT[:], cosT[:], ACT.Sin, scale=-TWO_PI,
                                         bias=cst[:, C_HALFPI:C_HALFPI + 1]).then_inc(trig_ready, 1)

                def exps(h):
                    ac.wait_ge(max_ready, i * 4 + h + 1)
                    nc.scalar.activation(prob[:, 0:P], prob[:, 0:P], ACT.Exp, bias=sm[:, 2:3], scale=SM_SCALE,
                                         accum_out=sm[:, 4:5]).then_inc(exp_done, 1)
                    nc.scalar.activation(prob[:, P:384], prob[:, P:384], ACT.Exp, bias=sm[:, 3:4], scale=SM_SCALE,
                                         accum_out=sm[:, 5:6]).then_inc(exp_done, 1)

                def tanh_gate(g):
                    ac.wait_ge(gemm_free, i * 20 + 18 + 12 + g + 1)
                    to = mla[:, bass.ds(i * 4 + g, 1), :] if g < 4 else gate[:, bass.ds(i * 4 + g - 4, 1), :]
                    nc.scalar.activation(to, gsum[:, g % 2:g % 2 + 1, :], ACT.Tanh, scale=0.5).then_inc(gate_done, 1)

                def copy_pt(h):
                    ac.wait_ge(pt_psum, i * 4 + h + 1)
                    nc.scalar.activation(probT[:], ps[:, PT, 0:384], ACT.Copy).then_inc(pt_copied, 1)

                trig(0, 0)
                hp(4)
                trig(0, 1)
                for k in range(6, 12):
                    hp(k)
                for g in range(8):
                    if g < 4:
                        exps(g)
                    if g == 3:
                        trig(1, 0)
                        trig(1, 1)
                    hp(12 + 2 * g), hp(13 + 2 * g)
                    tanh_gate(g)
                    if g < 4:
                        copy_pt(g)

            def gelu_high(m):
                ac.wait_ge(y_act, m + 1)
                nc.scalar.activation(yT[:, m, 0, :], zT[:, 10 + m, :], ACT.Copy).then_inc(y_hi, 1)

            for m in range(UT):
                if m == UT - 1:
                    gelu_high(UT - 2)
                ac.wait_ge(y_free, m + 2)
                nc.scalar.activation(zT[:, 10 + m, :], zT[:, 10 + m, :], ACT.Gelu_apprx_tanh).then_inc(y_act, 1)
                if 1 <= m < UT - 1:
                    gelu_high(m - 1)
            gelu_high(UT - 1)

            def glu_high(i, k):
                high(i, GLU0, GLU_PER, k + RING)

            def gate_tanh(i, e):
                ac.wait_ge(gemm_free, i * 4 + 98 + 2 * e + 2)
                nc.scalar.activation(tmpB[:, 2 * e + 1, :], tmpB[:, 2 * e + 1, :], ACT.Tanh, scale=0.5).then_inc(glu_tanh, 1)

            def mix_high(kt):
                ac.wait_ge(mix_sum, kt + 1)
                nc.scalar.activation(mixT[:, bass.ds(kt, 1), 0, :], tmpB[:, 6:7, :], ACT.Copy, scale=0.5).then_inc(mix_hi, 1)

            def glu_turn(i, first):
                glu_high(i, 0)
                if not first:
                    mix_high(i * 2 - 1)
                glu_high(i, 1)
                gate_tanh(i, 0)
                glu_high(i, 2)
                mix_high(i * 2)
                glu_high(i, 3)
                gate_tanh(i, 1)
            glu_turn(0, True)
            with ac.Fori(1, 8) as i:
                glu_turn(i, False)
            mix_high(KT - 1)
            def norm_root(t, count):
                ac.wait_ge(var_ready, count)
                nc.scalar.activation(rstd[:, t:t + 1], moments[:, t, 1:2], ACT.Sqrt, bias=cst[:, C_LNEPS:C_LNEPS + 1]
                                     ).then_inc(root_ready, 1)

            def first_root():
                nc.scalar.activation(start[:, 5:6], cst[:, C_ONES:C_ONES + 1], ACT.Sqrt)

            with ac.Fori(0, 3) as i:
                for k in range(OUT_PER):
                    high(i, OUT0, OUT_PER, k + RING)
            for k in range(RING):
                high(3, OUT0, OUT_PER, k + RING)
            first_root()
            norm_root(0, 1)
            for k in range(RING, OUT_PER):
                high(3, OUT0, OUT_PER, k + RING)
            norm_root(1, 2)
            for k in range(KT):
                ac.wait_ge(h_f32, k + 1)
                nc.scalar.activation(hT[:, k, 0, :], tmp[:, k % 4, :], ACT.Copy).then_inc(h_hi, 1)
                if k == 12:
                    high(0, FFN0, FFN_PER, RING)

            def ffn_turn(i, first):
                for e in range(2):
                    if not (first and e == 0):
                        high(i, FFN0, FFN_PER, 4 * e + RING)
                    high(i, FFN0, FFN_PER, 4 * e + 1 + RING)
                    ac.wait_ge(gemm_free, i * 4 + 138 + 2 * e + 1)
                    nc.scalar.activation(tmp[:, 1, :], tmp[:, 0, :], ACT.Silu).then_inc(ffn_silu, 1)
                    high(i, FFN0, FFN_PER, 4 * e + 2 + RING)
                    high(i, FFN0, FFN_PER, 4 * e + 3 + RING)
                    ac.wait_ge(ffn_prod, i * 2 + e + 1)
                    nc.scalar.activation(act[:, bass.ds(i * 2 + e, 1), 0, :], tmp[:, 3:4, :], ACT.Copy).then_inc(act_hi, 1)
            ffn_turn(0, True)
            with ac.Fori(1, FFN_TURNS) as i:
                ffn_turn(i, False)
            with ac.Fori(0, DOWN_PER - 1) as i:
                for k in range(4):
                    high(i, DOWN0, 4, k + RING)
            first_root()
            for t in range(2):
                norm_root(t, 3 + t)

        @block.tensor
        def _(pe):
            mm = nc.tensor.matmul

            def weights_in(v):
                pe.wait_ge(lo_ready, v + 1)

            def bank_free(m):
                if not (isinstance(m, int) and m < 2):
                    pe.wait_ge(gemm_free, m - 1)

            def feature_tile(bank, s, b, src, kts, first, last):
                for n, kt in enumerate(kts):
                    hi = whi[:, s, (b + n) * P:(b + n + 1) * P]
                    lo = wlo[:, s, (b + n) * P:(b + n + 1) * P]
                    mm(ps[:, bank, :], hi, src[:, kt].rearrange("p a t -> p (a t)"),
                       start=(first and n == 0), stop=False)
                    done = last and n == len(kts) - 1
                    ins = mm(ps[:, bank, TOK:512], lo, src[:, kt, 0, :], start=False, stop=done)
                return ins

            def row_tile(bank, s, t, src, kts, first, last):
                for n, kt in enumerate(kts):
                    hi, lo = whi[:, s, n * 512:(n + 1) * 512], wlo[:, s, n * 512:(n + 1) * 512]
                    xh, xl = src[:, kt, 0, t * P:(t + 1) * P], src[:, kt, 1, t * P:(t + 1) * P]
                    mm(ps[:, bank, :], xh, hi, start=(first and n == 0), stop=False)
                    mm(ps[:, bank, :], xh, lo, start=False, stop=False)
                    ins = mm(ps[:, bank, :], xl, hi, start=False, stop=(last and n == len(kts) - 1))
                return ins

            pe.wait_ge(in_cst, 16)

            def turn_x(k):
                pe.wait_ge(in_x[k // 2], 16)
                if k >= 6:
                    pe.wait_ge(xt_lo, k - 5)
                for a in range(2):
                    for t in range(2):
                        kt = 2 * k + a
                        ins = nc.tensor.transpose(ps[:, 2 + k % 6, a * TOK + t * P:a * TOK + (t + 1) * P],
                                                  xrow[:, t, kt * P:(kt + 1) * P], ident)
                ins.then_inc(xt_psum, 1)

            def front_half(i, e, h):
                weights_in(i * 4 + 2 * e + h)
                feature_tile(e, 2 * e + h, 0, xT, range(8 * h, 8 * h + 8), h == 0, h == 1).then_inc(slab_used, 1)

            def front_turn(i):
                for e in range(2):
                    bank_free(i * 2 + e)
                    front_half(i, e, 0)
                    front_half(i, e, 1)

            for k in range(6):
                turn_x(k)
            pe.wait_ge(xt_lo, 4)
            front_half(0, 0, 0)
            turn_x(6)
            turn_x(7)
            pe.wait_ge(xt_lo, 8)
            front_half(0, 0, 1)
            front_half(0, 1, 0)
            front_half(0, 1, 1)
            with pe.Fori(1, 6) as i:
                front_turn(i)
            for n in range(2):
                for m in range(CT):
                    pe.wait_ge(sq_ready, CT * n + m + 1)
                    ins = mm(ps[:, SC + n, 0:TOK], cst[:, C_ONES:C_ONES + P], squares[:, CT * n + m, :],
                             start=(m == 0), stop=(m == CT - 1))
                ins.then_inc(ss_psum, 1)
            pe.wait_ge(b_padded, 6)
            for c in range(2):
                for q in range(2):
                    for n in range(4):
                        ins = nc.tensor.transpose(ps[:, BT_BANKS[2 * c + q], n * P:(n + 1) * P],
                                                  bpad[:, c, (4 * q + n) * P:(4 * q + n + 1) * P], ident)
                    ins.then_inc(bt_psum, 1)
            with pe.Fori(6, FRONT_TURNS) as i:
                front_turn(i)

            with pe.Fori(0, HG) as i:
                v0, m0 = i * HEAD_PER + HEAD0, i * 20 + 18

                def latent_tiles(k, m, n_tiles, src0, extra=0):
                    weights_in(v0 + k)
                    for b in range(n_tiles):
                        bank_free(m0 + m + b)
                        ins = feature_tile((m + b) % 2, k % RING, CT * b, cT, range(src0, src0 + CT), True, True)
                        if b < n_tiles - 1:
                            ins.then_inc(half_done, 1)
                    ins.then_inc(slab_used, 1 + extra)

                def b_product(b):
                    if b == 0:
                        pe.wait_ge(slots_ready, i * 4 + 4)
                    pe.wait_ge(rotated, i * 4 + b + 1)
                    for e in range(2):
                        q = 2 * (b % 2) + e
                        for c in range(2):
                            ins = mm(ps[:, BU + e, c * TOK:(c + 1) * TOK], bslot[32 * q:32 * q + 32, b // 2, c, :],
                                     uslot[32 * q:32 * q + 32, b // 2, :], start=True, stop=True)
                    ins.then_inc(bu_psum, 1)

                def c_product(b):
                    pe.wait_ge(states_ready, i * 4 + b + 1)
                    if b % 2 == 0:
                        pe.wait_ge(y_free, i * 2 + b // 2 + 1)
                    for e in range(2):
                        q = 2 * (b % 2) + e
                        for c in range(2):
                            ins = mm(ps[32 * q:32 * q + 32, YP, 0:TOK], cslot[:, 2 * b + e, c, :],
                                     states[:, c, e * TOK:(e + 1) * TOK], start=(c == 0), stop=(c == 1))
                    ins.then_inc(c_done, 1)

                def score(h):
                    if h == 0:
                        pe.wait_ge(qk_ready, i + 1)
                    else:
                        pe.wait_ge(max_ready, i * 4 + h)
                    r = 32 * h
                    for q, (c0, n) in enumerate(((0, P), (P, 2 * P))):
                        o_ = ps[:, SC, c0:c0 + n]
                        mm(o_, qT[:, h, q * P:(q + 1) * P], kT[:, h, 0:n], start=True, stop=False)
                        mm(o_, qr[r:r + 32, 0, q * P:(q + 1) * P], zT[r:r + 32, 8, 0:n], start=False, stop=False)
                        ins = mm(o_, qr[r:r + 32, 1, q * P:(q + 1) * P], zT[r:r + 32, 9, 0:n], start=False, stop=True)
                    ins.then_inc(scores, 1)

                def turn_probs(h):
                    pe.wait_ge(prob_ready, i * 4 + h + 1)
                    nc.tensor.transpose(ps[:, PT, 0:P], prob[:, 0:P], ident)
                    nc.tensor.transpose(ps[:, PT, P:2 * P], prob[:, P:2 * P], ident)
                    nc.tensor.transpose(ps[:, PT, 2 * P:3 * P], prob[:, 2 * P:3 * P], ident).then_inc(pt_psum, 1)

                def values(h):
                    pe.wait_ge(pt_copied, i * 4 + h + 1)
                    if h == 0:
                        pe.wait_ge(gemm_free, m0 + 12)
                    pe.wait_ge(o_read, i * 4 + h + 1)
                    mm(ps[:, OP, 0:TOK], vT[:, 0, h * P:(h + 1) * P], probT[:, 0:TOK], start=True, stop=False)
                    mm(ps[:, OP, P:TOK], vT[:, 1, h * P:(h + 1) * P], probT[:, TOK:384], start=False,
                       stop=True).then_inc(o_psum, 1)

                def gate_tile(g):
                    bank_free(m0 + 12 + g)
                    for h in range(2):
                        k = 8 + 2 * g + h
                        weights_in(v0 + k)
                        ins = feature_tile(g % 2, k % RING, 0, xT, range(8 * h, 8 * h + 8), h == 0, h == 1)
                        ins.then_inc(slab_used, 1)

                pe.wait_ge(c_lo, 8)
                latent_tiles(0, 0, 2, 0)
                latent_tiles(1, 2, 2, 0)
                b_product(0)
                latent_tiles(2, 4, 2, CT)
                latent_tiles(3, 6, 2, CT)
                latent_tiles(4, 8, 2, 0, extra=1)
                for h in range(2):
                    weights_in(v0 + 6 + h)
                    for t in range(2):
                        if h == 0:
                            bank_free(m0 + 10 + t)
                        ins = row_tile(t, (6 + h) % RING, t, cT, range(CT + 2 * h, CT + 2 * h + 2), h == 0, h == 1)
                        if h == 1 and t == 0:
                            ins.then_inc(half_done, 1)
                    ins.then_inc(slab_used, 1)
                b_product(1)
                score(0)
                gate_tile(0)
                turn_probs(0)
                score(1)
                c_product(0)
                gate_tile(1)
                values(0)
                turn_probs(1)
                score(2)
                gate_tile(2)
                values(1)
                turn_probs(2)
                score(3)
                gate_tile(3)
                c_product(1)
                values(2)
                turn_probs(3)
                b_product(2)
                gate_tile(4)
                values(3)
                b_product(3)
                gate_tile(5)
                gate_tile(6)
                c_product(2)
                gate_tile(7)
                c_product(3)

            def glu_turn(i):
                for e in range(4):
                    bank_free(i * 4 + (98 + e))
                    weights_in(i * GLU_PER + (GLU0 + e))
                    for kt in range(UT):
                        if isinstance(i, int) and e == 0:
                            pe.wait_ge(y_lo, kt + 1)
                        ins = feature_tile(e % 2, e, kt, yT, (kt,), kt == 0, kt == UT - 1)
                    ins.then_inc(slab_used, 1)
            glu_turn(0)
            with pe.Fori(1, 8) as i:
                glu_turn(i)

            def panel(src, src_ready, n_slabs, slot0, v, m):
                def part(k, t):
                    if t == 0:
                        pe.wait_ge(src_ready, 2 * k + 2)
                        weights_in(v + k)
                    if k == 0:
                        bank_free(m + t)
                    ins = row_tile(t, (slot0 + k) % RING, t, src, (2 * k, 2 * k + 1), k == 0, k == n_slabs - 1)
                    if t == 0 and k == n_slabs - 1:
                        ins.then_inc(half_done, 1)
                    if t == 1:
                        ins.then_inc(slab_used, 1)

                for k in range(n_slabs - RING):
                    part(k, 0)
                    part(k, 1)
                for t in range(2):
                    for k in range(n_slabs - RING, n_slabs):
                        part(k, t)

            with pe.Fori(0, 4) as i:
                panel(mixT, mix_lo, OUT_PER, 0, i * OUT_PER + OUT0, i * 2 + 130)

            def turn_h(k, t):
                for a in range(2):
                    ins = nc.tensor.transpose(ps[:, 2 + k % 6, a * TOK + t * P:a * TOK + (t + 1) * P],
                                              rows[:, t, (2 * k + a) * P:(2 * k + a + 1) * P], ident)
                if t == 1:
                    ins.then_inc(h_psum, 1)
            for t in range(2):
                pe.wait_ge(normed, t + 1)
                for k in range(6):
                    turn_h(k, t)
            for k in (6, 7):
                pe.wait_ge(h_f32, 2 * (k - 6) + 2)
                for t in range(2):
                    turn_h(k, t)

            for k in range(KT):
                h, n = k // 8, k % 8
                if k == 0:
                    bank_free(138)
                    bank_free(139)
                pe.wait_ge(h_lo, k + 1)
                for e in range(2):
                    if n == 0:
                        weights_in(FFN0 + 2 * e + h)
                    ins = feature_tile(e, 2 * e + h, n, hT, (k,), k == 0, k == KT - 1)
                    if e == 0 and n == 7:
                        ins.then_inc(slab_used, 1)
                    if e == 1 and k == KT - 1:
                        ins.then_inc(slab_used, 2)

            def ffn_tiles(i, e0):
                for e in range(e0, 4):
                    bank_free(i * 4 + 138 + e)
                    for h in range(2):
                        k = 2 * e + h
                        weights_in(i * FFN_PER + FFN0 + k)
                        feature_tile(e % 2, k % RING, 0, hT, range(8 * h, 8 * h + 8), h == 0, h == 1
                                     ).then_inc(slab_used, 1)
            ffn_tiles(0, 2)
            with pe.Fori(1, FFN_TURNS) as i:
                ffn_tiles(i, 0)

            with pe.Fori(0, 2) as i:
                for p in range(2):
                    panel(act, act_lo, DOWN_PER, DOWN_PER * p, i * (2 * DOWN_PER) + DOWN0 + DOWN_PER * p,
                          i * 4 + (138 + 2 * FT) + 2 * p)

        @block.vector
        def _(ve):
            st = Steps(ve, dve_step)
            V = nc.vector

            def tile_sum(out_, bank, slab=None, half=None):
                if slab is not None:
                    ve.wait_ge(slab_used, slab + 1)
                else:
                    ve.wait_ge(half_done, half + 1)
                V.tensor_reduce(out_, ps[:, bank, :].rearrange("p (a t) -> p t a", a=2), mybir.AxisListType.X, ALU.add
                                ).then_inc(gemm_free, 1)

            for k in range(8):
                ve.wait_ge(xt_hi, k + 1)
                V.tensor_tensor(xT[:, 2 * k:2 * k + 2, 1, :], ps[:, 2 + k % 6, :].rearrange("p (a t) -> p a t", a=2),
                                xT[:, 2 * k:2 * k + 2, 0, :].bitcast(F32), ALU.subtract).then_inc(xt_lo, 1)

            def front_sums(i, e):
                to = zT[:, bass.ds(i * 2 + e, 1), :].rearrange("p a t -> p (a t)")
                tile_sum(to, e, i * 4 + 2 * e + 1)

            re, im, dt = sp[:, 0, :], sp[:, 1, :], sp[:, 2, :]
            mag, theta, sn, cs = sp[:, 3, :], sp[:, 4, :], sp[:, 5, :], sp[:, 6, :]
            w = [sp[:, 7 + n, :] for n in range(5)]

            def s5_angle():
                ve.wait_ge(ssm_exp, 1)
                V.tensor_tensor(mag, re, dt, ALU.mult).then_inc(ssm_phase, 1)
                st(V.tensor_tensor(w[0], im, dt, ALU.mult)); st.wait()
                st(V.tensor_scalar(w[0], w[0], INV_2PI, None, ALU.mult)); st.wait()
                st(V.tensor_scalar(w[1], w[0], MAGIC, None, ALU.add)); st.wait()
                st(V.tensor_scalar(w[1], w[1], MAGIC, None, ALU.subtract)); st.wait()
                V.tensor_tensor(theta, w[0], w[1], ALU.subtract).then_inc(ssm_phase, 1)
                st(V.tensor_tensor(w[2], re, re, ALU.mult))
                st(V.tensor_tensor(w[3], im, im, ALU.mult)); st.wait()
                st(V.tensor_tensor(w[2], w[2], w[3], ALU.add)); st.wait()
                st(V.reciprocal(w[2], w[2]))

            def s5_coefficient():
                ve.wait_ge(ssm_trig, 2)
                st(V.tensor_tensor(cs, mag, cs, ALU.mult))
                st(V.tensor_tensor(sn, mag, sn, ALU.mult)); st.wait()
                st(V.tensor_scalar(cs, cs, -1.0, None, ALU.add)); st.wait()
                st(V.tensor_tensor(w[0], cs, re, ALU.mult))
                st(V.tensor_tensor(w[1], sn, im, ALU.mult)); st.wait()
                st(V.tensor_tensor(w[0], w[0], w[1], ALU.add))
                st(V.tensor_tensor(w[4], sn, re, ALU.mult))
                st(V.tensor_tensor(w[3], cs, im, ALU.mult)); st.wait()
                st(V.tensor_tensor(w[1], w[4], w[3], ALU.subtract))
                st(V.tensor_tensor(w[0], w[0], w[2], ALU.mult)); st.wait()
                st(V.tensor_tensor(w[1], w[1], w[2], ALU.mult))

            def wide(a):
                return a.rearrange("p (n o) -> p n o", o=1).to_broadcast([P, PAIRS, GROUP])
            pr = [bprod[:, n, :].rearrange("p (a b) -> p a b", a=PAIRS) for n in range(4)]

            def bbar_products():
                st.wait()
                ve.wait_ge(in_small, 64)
                st(V.tensor_tensor(pr[0], bpar[:, 0], wide(w[0]), ALU.mult))
                st(V.tensor_tensor(pr[1], bpar[:, 1], wide(w[1]), ALU.mult))
                st(V.tensor_tensor(pr[2], bpar[:, 1], wide(w[0]), ALU.mult))
                st(V.tensor_tensor(pr[3], bpar[:, 0], wide(w[1]), ALU.mult))

            def bbar():
                st.wait()
                ve.wait_ge(b_padded, 2)
                for g in range(2):
                    half = slice(64 * g, 64 * g + 64)
                    for c, (one, two, op) in enumerate(((0, 1, ALU.subtract), (2, 3, ALU.add))):
                        V.tensor_tensor(bpad[half, c].rearrange("p (a b) -> p a b", a=PAIRS)[:, :, g * GROUP:(g + 1) * GROUP],
                                        pr[one][half], pr[two][half], op).then_inc(b_padded, 1)
                st(V.tensor_scalar(cP[:, :, 1, :], cP[:, :, 1, :], -1.0, None, ALU.mult))

            def rope_angle():
                st(V.tensor_copy(ang[:, 0, :], posi[:])); st.wait()
                st(V.tensor_scalar(ang[:, 0, :], ang[:, 0, :], cst[:, C_INVF:C_INVF + 1], None, ALU.mult)); st.wait()
                st(V.tensor_scalar(ang[:, 1, :], ang[:, 0, :], INV_2PI, MAGIC, ALU.mult, ALU.add)); st.wait()
                st(V.tensor_scalar(ang[:, 1, :], ang[:, 1, :], MAGIC, None, ALU.subtract)); st.wait()
                for part in (PI_A, PI_B, PI_C):
                    st(V.scalar_tensor_tensor(ang[:, 0, :], ang[:, 1, :], -part, ang[:, 0, :], ALU.mult, ALU.add)); st.wait()
                V.tensor_scalar(ang[:, 0, :], ang[:, 0, :], 3.1415925, -3.1415925, ALU.min, ALU.max).then_inc(rope_phase, 1)

            for n, set_up in enumerate((s5_angle, s5_coefficient, bbar_products, bbar, rope_angle)):
                tile_sum(zT[:, n, :], n % 2, 2 * n + 1)
                set_up()
            tile_sum(zT[:, 5, :], 1, 11)

            with ve.Fori(3, 6) as i:
                for e in range(2):
                    front_sums(i, e)
            cosr, sinr = ropecs[:, 0, :], ropecs[:, 1, :]

            def rotate(t1, t2, out1, out2, signal):
                a, b, c, d = gsum[:, 0, :], gsum[:, 1, :], states[:, 1, 0:TOK], states[:, 1, TOK:]
                st(V.tensor_tensor(a, t1, cosr, ALU.mult))
                st(V.tensor_tensor(b, t2, sinr, ALU.mult))
                st(V.tensor_tensor(c, t1, sinr, ALU.mult))
                st(V.tensor_tensor(d, t2, cosr, ALU.mult)); st.wait()
                st(V.tensor_tensor(out1, a, b, ALU.subtract))
                ins = V.tensor_tensor(out2, c, d, ALU.add)
                if signal is not None:
                    ins.then_inc(signal, 1)

            for c in range(2):
                for q in range(2):
                    ve.wait_ge(bt_psum, 2 * c + q + 1)
                    st(V.tensor_copy(bT[:, 4 * q:4 * q + 4, c, :],
                                     ps[:, BT_BANKS[2 * c + q], :].rearrange("p (a b) -> p a b", a=4)))
            for n in range(2):
                ve.wait_ge(rms_root, n + 1)
                st(V.reciprocal(rinv[:, n, :], rinv[:, n, :])); st.wait()
                for m in range(CT * n, CT * n + CT):
                    V.scalar_tensor_tensor(zT[:, m, :], zT[:, m, :], col[:, P_CG + m:P_CG + m + 1], rinv[:, n, :],
                                           ALU.mult, ALU.mult).then_inc(c_ready, 1)
            front_sums(6, 0)
            for m in range(8):
                ve.wait_ge(c_hi, m + 1)
                V.tensor_tensor(cT[:, m, 1, :], zT[:, m, :], cT[:, m, 0, :].bitcast(F32), ALU.subtract).then_inc(c_lo, 1)
            ve.wait_ge(rope_trig, 2)
            rotate(zT[:, 8, :], zT[:, 9, :], zT[:, 8, :], zT[:, 9, :], None)
            front_sums(6, 1)

            def phases(i, n):
                for e in range(4):
                    th = theta_of(i, 4 * n + e)
                    st(V.tensor_scalar(sinT[:, e, :], tvals, th, MAGIC, ALU.mult, ALU.add))
                st.wait()
                st(V.tensor_scalar(sinT[:], sinT[:], MAGIC, None, ALU.subtract)); st.wait()
                for e in range(4):
                    ins = V.scalar_tensor_tensor(cosT[:, e, :], tvals, theta_of(i, 4 * n + e), sinT[:, e, :],
                                                 ALU.mult, ALU.subtract)
                ins.then_inc(phase_ready, 1)

            def theta_of(i, pair):
                return sp[:, 4:6, :].rearrange("p a b -> p (a b)")[:, bass.ds(i * 8 + pair, 1)]

            st.wait()
            phases(0, 0)
            with ve.Fori(7, FRONT_TURNS) as i:
                for e in range(2):
                    front_sums(i, e)
            for n, s_ in enumerate((c_done, rotated, o_read, y_free)):
                V.memset(start[:, n:n + 1], 0.0).then_inc(s_, 1)
            with ve.Fori(0, HG) as i:
                st.enter(i, DVE_HEAD_STEPS)
                v0, m0 = i * HEAD_PER + HEAD0, i * 20 + 18
                xR, xI = scan[:, 0], scan[:, 1]
                sR, sI = states[:, 0], states[:, 1]

                def trig_of(b):
                    return cosT[:, 2 * (b % 2):2 * (b % 2) + 2, :], sinT[:, 2 * (b % 2):2 * (b % 2) + 2, :]

                def of_pairs(a):
                    return a.rearrange("p (a t) -> p a t", a=2)

                def turn_back(b, half):
                    c_, s_ = trig_of(b)
                    uR, uI = ps[:, BU:BU + 2, 0:TOK], ps[:, BU:BU + 2, TOK:512]
                    if half == 0:
                        if b % 2 == 0:
                            ve.wait_ge(trig_ready, i * 6 + 3 * (b // 2) + 3)
                        else:
                            ve.wait_ge(states_ready, i * 4 + b)
                        ve.wait_ge(bu_psum, i * 4 + b + 1)
                        st(V.tensor_tensor(of_pairs(prod[:, 0]), uR, c_, ALU.mult))
                        st(V.tensor_tensor(of_pairs(prod[:, 1]), uI, s_, ALU.mult))
                    else:
                        st(V.tensor_tensor(of_pairs(prod[:, 2]), uI, c_, ALU.mult))
                        V.tensor_tensor(of_pairs(prod[:, 3]), uR, s_, ALU.mult).then_inc(rotated, 1)

                def combine(b):
                    ve.wait_ge(rotated, i * 4 + b + 2)
                    st(V.tensor_tensor(prod[:, 0], prod[:, 0], prod[:, 1], ALU.add))
                    st(V.tensor_tensor(prod[:, 2], prod[:, 2], prod[:, 3], ALU.subtract))

                def recur(b, e):
                    if e == 0:
                        st.wait()
                    a_ = sp[:, 3, bass.ds(i * 8 + (2 * b + e), 1)].to_broadcast([P, TOK])
                    cut = slice(e * TOK, (e + 1) * TOK)
                    st(V.tensor_tensor_scan(xR[:, cut], a_, prod[:, 0, cut], 0.0, ALU.mult, ALU.add))
                    st(V.tensor_tensor_scan(xI[:, cut], a_, prod[:, 2, cut], 0.0, ALU.mult, ALU.add))

                def turn_forward(b, half):
                    c_, s_ = trig_of(b)
                    if half == 0:
                        st.wait()
                        st(V.tensor_tensor(of_pairs(prod[:, 0]), of_pairs(xR), c_, ALU.mult))
                        st(V.tensor_tensor(of_pairs(prod[:, 1]), of_pairs(xI), s_, ALU.mult))
                        st(V.tensor_tensor(of_pairs(prod[:, 2]), of_pairs(xI), c_, ALU.mult))
                    else:
                        st(V.tensor_tensor(of_pairs(prod[:, 3]), of_pairs(xR), s_, ALU.mult)); st.wait()
                        ve.wait_ge(c_done, i * 4 + b + 1)
                        st(V.tensor_tensor(sR, prod[:, 0], prod[:, 1], ALU.subtract))
                        V.tensor_tensor(sI, prod[:, 2], prod[:, 3], ALU.add).then_inc(states_ready, 1)

                def y_tile(n):
                    ve.wait_ge(c_done, i * 4 + 2 * n + 3)
                    ins = V.scalar_tensor_tensor(zT[:, bass.ds(i * 2 + (10 + n), 1), :].rearrange("p a t -> p (a t)"),
                                                 uslot[:, n, :], col[:, bass.ds(i * 2 + (P_D + n), 1)],
                                                 ps[:, YP, 0:TOK], ALU.mult, ALU.add)
                    ins.then_inc(y_free, 1)

                def softmax_max(h):
                    ve.wait_ge(scores, i * 4 + h + 1)
                    V.memset(start[:, 4:5], 0.0)
                    st(V.tensor_tensor_reduce(prob[:, 0:P], ps[:, SC, 0:P], cst[:, C_MASK + P:C_MASK + 2 * P], 1.0,
                                              NEG, ALU.add, ALU.max, sm[:, 0:1]))
                    st(V.tensor_tensor_reduce(prob[:, P:384], ps[:, SC, P:384], cst[:, C_MASK:C_MASK + 2 * P], 1.0,
                                              NEG, ALU.add, ALU.max, sm[:, 1:2])); st.wait()
                    V.tensor_scalar(sm[:, 2:4], sm[:, 0:2], -SM_SCALE, None, ALU.mult).then_inc(max_ready, 1)

                def normalise(h):
                    ve.wait_ge(exp_done, i * 8 + 2 * h + 2)
                    st(V.reciprocal(sm[:, 4:6], sm[:, 4:6])); st.wait()
                    st(V.tensor_scalar(prob[:, 0:P], prob[:, 0:P], sm[:, 4:5], None, ALU.mult))
                    V.tensor_scalar(prob[:, P:384], prob[:, P:384], sm[:, 5:6], None, ALU.mult).then_inc(prob_ready, 1)

                def gate_sum(g):
                    if g >= 2:
                        ve.wait_ge(gate_done, i * 8 + g - 1)
                    tile_sum(gsum[:, g % 2, :], g % 2, v0 + 9 + 2 * g)

                def head_out(h):
                    ve.wait_ge(o_psum, i * 4 + h + 1)
                    ve.wait_ge(gate_done, i * 8 + h + 1)
                    g_ = mla[:, bass.ds(i * 4 + h, 1), :].rearrange("p a t -> p (a t)")
                    V.scalar_tensor_tensor(g_, g_, 1.0, ps[:, OP, 0:TOK], ALU.add, ALU.mult).then_inc(o_read, 1)

                def latent_pair(k, to, h):
                    tile_sum(to[:, h, :], 0, half=i * 6 + k + h // 2)
                    tile_sum(to[:, h + 1, :], 1, slab=v0 + k + h // 2)

                latent_pair(0, qT, 0)
                latent_pair(0, qT, 2)
                latent_pair(2, kT, 0)
                turn_back(0, 0)
                latent_pair(2, kT, 2)
                turn_back(0, 1)
                tile_sum(states[:, 0, 0:TOK], 0, half=i * 6 + 4)
                tile_sum(states[:, 0, TOK:], 1, slab=v0 + 4)
                ve.wait_ge(gemm_free, m0 + 10)
                rotate(states[:, 0, 0:TOK], states[:, 0, TOK:], qr[:, 0, :], qr[:, 1, :], qk_ready)
                combine(0)
                recur(0, 0)
                ve.wait_ge(half_done, i * 6 + 6)
                V.tensor_copy(vT[:, 0, :], ps[:, 0, :]).then_inc(gemm_free, 1)
                ve.wait_ge(slab_used, v0 + 8)
                V.tensor_copy(vT[:, 1, :], ps[:, 1, :]).then_inc(gemm_free, 1)
                recur(0, 1)
                softmax_max(0)
                turn_forward(0, 0)
                normalise(0)
                turn_forward(0, 1)
                gate_sum(0)
                softmax_max(1)
                turn_back(1, 0)
                turn_back(1, 1)
                normalise(1)
                combine(1)
                gate_sum(1)
                recur(1, 0)
                head_out(0)
                softmax_max(2)
                recur(1, 1)
                normalise(2)
                turn_forward(1, 0)
                gate_sum(2)
                turn_forward(1, 1)
                head_out(1)
                softmax_max(3)
                phases(i, 1)
                normalise(3)
                gate_sum(3)
                y_tile(0)
                head_out(2)
                turn_back(2, 0)
                turn_back(2, 1)
                combine(2)
                gate_sum(4)
                recur(2, 0)
                recur(2, 1)
                head_out(3)
                turn_forward(2, 0)
                gate_sum(5)
                turn_forward(2, 1)
                turn_back(3, 0)
                turn_back(3, 1)
                gate_sum(6)
                combine(3)
                recur(3, 0)
                recur(3, 1)
                turn_forward(3, 0)
                turn_forward(3, 1)
                gate_sum(7)
                ve.wait_ge(states_ready, i * 4 + 4)
                phases(i, 2)
                y_tile(1)
            st.leave(HG, DVE_HEAD_STEPS)

            for m in range(UT):
                ve.wait_ge(y_hi, m + 1)
                V.tensor_tensor(yT[:, m, 1, :], zT[:, 10 + m, :], yT[:, m, 0, :].bitcast(F32), ALU.subtract).then_inc(y_lo, 1)

            def mix_tile(kt, e):
                ve.wait_ge(glu_tanh, kt + 1)
                st(V.scalar_tensor_tensor(tmpB[:, 4, :], tmpB[:, 2 * e + 1, :], 1.0, tmpB[:, 2 * e, :], ALU.add, ALU.mult)); st.wait()
                st(V.scalar_tensor_tensor(tmpB[:, 5:6, :], gate[:, bass.ds(kt, 1), :], 1.0, tmpB[:, 4:5, :],
                                          ALU.add, ALU.mult)); st.wait()
                V.scalar_tensor_tensor(tmpB[:, 6:7, :], tmpB[:, 5:6, :], 0.5, mla[:, bass.ds(kt, 1), :],
                                       ALU.mult, ALU.add).then_inc(mix_sum, 1)
                ve.wait_ge(mix_hi, kt + 1)
                V.scalar_tensor_tensor(mixT[:, bass.ds(kt, 1), 1, :], tmpB[:, 6:7, :], 0.5,
                                       mixT[:, bass.ds(kt, 1), 0, :].bitcast(F32), ALU.mult, ALU.subtract
                                       ).then_inc(mix_lo, 1)
                ve.wait_ge(mix_lo, kt + 1)

            def glu_turn(i, first):
                v = i * GLU_PER + GLU0
                tile_sum(tmpB[:, 0, :], 0, v)
                if not first:
                    mix_tile(i * 2 - 1, 1)
                tile_sum(tmpB[:, 1, :], 1, v + 1)
                tile_sum(tmpB[:, 2, :], 0, v + 2)
                mix_tile(i * 2, 0)
                tile_sum(tmpB[:, 3, :], 1, v + 3)
            glu_turn(0, True)
            with ve.Fori(1, 8) as i:
                st.enter(i - 1, DVE_GLU_STEPS)
                glu_turn(i, False)
            st.leave(7, DVE_GLU_STEPS)
            mix_tile(KT - 1, 1)

            def residual(n, t, m, half, v_last):
                if t == 0:
                    ve.wait_ge(half_done, half + 1)
                else:
                    ve.wait_ge(slab_used, v_last + 1)
                r_ = rows[:, t, bass.ds(n * 512, 512)]
                V.scalar_tensor_tensor(r_, r_, ALPHA, ps[:, t, :], ALU.mult, ALU.add).then_inc(gemm_free, 1)
                ve.wait_ge(gemm_free, m + t + 1)
                st(V.bn_stats(stats[:, t, bass.ds(n, 1), :].rearrange("p a b -> p (a b)"), r_))

            def statistics(t):
                st.wait()
                V.bn_aggr(moments[:, t, :], stats[:, t, :, :].rearrange("p a b -> p (a b)")).then_inc(var_ready, 1)

            def inverse_root(t, count):
                ve.wait_ge(root_ready, count)
                st(V.reciprocal(rstd[:, t:t + 1], rstd[:, t:t + 1])); st.wait()

            ve.wait_ge(in_rows, 64)
            ve.wait_ge(lo_ready, OUT0 + RING)

            def out_low(i, k):
                low_part(ve, V, i * OUT_PER + OUT0 + RING + k, k % RING)

            def out_residual(i, t):
                residual(i, t, i * 2 + 130, i + 6 * HG, i * OUT_PER + OUT0 + OUT_PER - 1)

            with ve.Fori(0, 3) as i:
                st.enter(i, DVE_OUT_STEPS)
                for k in range(RING):
                    out_low(i, k)
                out_residual(i, 0)
                out_low(i, 4)
                out_low(i, 5)
                out_residual(i, 1)
                out_low(i, 6)
                out_low(i, 7)
            st.leave(3, DVE_OUT_STEPS)
            for k in range(RING):
                out_low(3, k)
            for t in range(2):
                out_residual(3, t)
                statistics(t)
                inverse_root(t, 1 + t)
                V.tensor_scalar(rows[:, t, :], rows[:, t, :], moments[:, t, 0:1], rstd[:, t:t + 1], ALU.subtract,
                                ALU.mult).then_inc(normed, 1)

            def h_low(k):
                ve.wait_ge(h_hi, k + 1)
                V.tensor_tensor(hT[:, k, 1, :], tmp[:, k % 4, :], hT[:, k, 0, :].bitcast(F32), ALU.subtract).then_inc(h_lo, 1)

            for k in range(KT):
                if k % 2 == 0:
                    ve.wait_ge(h_psum, k // 2 + 1)
                if k >= 4:
                    ve.wait_ge(h_lo, k - 3)
                V.tensor_scalar(tmp[:, k % 4, :], ps[:, 2 + (k // 2) % 6, (k % 2) * TOK:(k % 2 + 1) * TOK],
                                col[:, P_G1 + k:P_G1 + k + 1], col[:, P_B1 + k:P_B1 + k + 1], ALU.mult, ALU.add
                                ).then_inc(h_f32, 1)
                if k >= 2:
                    h_low(k - 2)
            h_low(KT - 2)
            h_low(KT - 1)

            def ffn_turn(i, first):
                for e in range(2):
                    n = i * 2 + e
                    m = i * 4 + 138 + 2 * e
                    v = i * FFN_PER + FFN0 + 4 * e

                    def lows(k0):
                        if first and e == 0:
                            return
                        if first and k0 == 0:
                            ve.wait_ge(lo_ready, FFN0 + 2 * RING)
                        for k in (k0, k0 + 1):
                            low_part(ve, V, i * FFN_PER + FFN0 + RING + 4 * e + k, k)
                    lows(0)
                    tile_sum(tmp[:, 0, :], 0, v + 1)
                    lows(2)
                    tile_sum(tmp[:, 2, :], 1, v + 3)
                    ve.wait_ge(gemm_free, m + 2)
                    ve.wait_ge(ffn_silu, n + 1)
                    V.tensor_tensor(tmp[:, 3, :], tmp[:, 1, :], tmp[:, 2, :], ALU.mult).then_inc(ffn_prod, 1)
                    ve.wait_ge(act_hi, n + 1)
                    V.tensor_tensor(act[:, bass.ds(n, 1), 1, :], tmp[:, 3:4, :],
                                    act[:, bass.ds(n, 1), 0, :].bitcast(F32), ALU.subtract).then_inc(act_lo, 1)
                    ve.wait_ge(act_lo, n + 1)
            ffn_turn(0, True)
            with ve.Fori(1, FFN_TURNS) as i:
                ffn_turn(i, False)

            ve.wait_ge(h_rows, 4)

            def down_low(n, k):
                low_part(ve, V, DOWN0 + n * DOWN_PER + k, (n * DOWN_PER + k) % RING)

            def down_residual(n, t):
                residual(n, t, n * 2 + (138 + 2 * FT), n + 6 * HG + 4, n * DOWN_PER + DOWN0 + DOWN_PER - 1)

            for n in range(4):
                for k in range(RING, DOWN_PER):
                    down_low(n, k)
                if n < 3:
                    down_residual(n, 0)
                    down_low(n + 1, 0)
                    down_low(n + 1, 1)
                    down_residual(n, 1)
                    down_low(n + 1, 2)
                    down_low(n + 1, 3)
            for t in range(2):
                down_residual(3, t)
                statistics(t)
                inverse_root(t, 3 + t)
                if t == 0:
                    ve.wait_ge(in_gb, 80)
                for h in range(2):
                    r_, cut = rows[:, t, h * 1024:(h + 1) * 1024], slice(h * 1024, (h + 1) * 1024)
                    st(V.scalar_tensor_tensor(r_, r_, moments[:, t, 0:1], gb[:, 0, cut], ALU.subtract, ALU.mult)); st.wait()
                    V.scalar_tensor_tensor(r_, r_, rstd[:, t:t + 1], gb[:, 1, cut], ALU.mult, ALU.add).then_inc(out_ready, 1)


def blocks_for_features(w):
    k, m = w.shape
    t = w.reshape(k // P, P, m // P, P).transpose(2, 1, 0, 3).reshape(m // P, P, k)
    if k >= SLAB:
        return t.reshape(m // P, P, k // SLAB, SLAB).transpose(0, 2, 1, 3).reshape(-1, P, SLAB)
    n = SLAB // k
    return t.reshape(m // P // n, n, P, k).transpose(0, 2, 1, 3).reshape(-1, P, SLAB)


def blocks_for_rows(w):
    return w.reshape(-1, 2, P, 512).transpose(0, 2, 1, 3).reshape(-1, P, SLAB)


def pack_slabs(w_in, w_uq, w_ukv, w_glu, w_out, w_gate, w_up, w_down):
    o_q, o_kv = SSM_W, SSM_W + LORA
    o_kr = o_kv + LORA
    o_gs = o_kr + ROPE
    o_gm = o_gs + D
    half = ROPE // 2
    kr1 = np.concatenate([w_in[:, o_kr:o_kr + half]] * 4, axis=1)
    kr2 = np.concatenate([w_in[:, o_kr + half:o_kr + ROPE]] * 4, axis=1)
    parts = [blocks_for_features(np.concatenate([w_in[:, o_q:o_kr], kr1, kr2, w_in[:, :SSM_W]], axis=1))]
    uq = w_uq.reshape(LORA, HEADS, P + ROPE)
    ukv = w_ukv.reshape(LORA, HEADS, 2 * P)
    for g in range(HG):
        hs = slice(4 * g, 4 * g + 4)
        parts.append(blocks_for_features(uq[:, hs, :P].reshape(LORA, 512)))
        parts.append(blocks_for_features(ukv[:, hs, :P].reshape(LORA, 512)))
        parts.append(blocks_for_features(np.concatenate([uq[:, hs, P:P + half].reshape(LORA, P),
                                                         uq[:, hs, P + half:].reshape(LORA, P)], axis=1)))
        parts.append(blocks_for_rows(ukv[:, hs, P:].reshape(LORA, 512)))
        parts.append(blocks_for_features(w_in[:, o_gm + 512 * g:o_gm + 512 * (g + 1)]))
        parts.append(blocks_for_features(w_in[:, o_gs + 512 * g:o_gs + 512 * (g + 1)]))

    def alternate(a, b):
        k, m = a.shape
        return np.stack([a.reshape(k, m // P, P), b.reshape(k, m // P, P)], axis=2).reshape(k, 2 * m)
    parts.append(blocks_for_features(alternate(w_glu[:, :D], w_glu[:, D:])))
    for n in range(4):
        parts.append(blocks_for_rows(w_out[:, 512 * n:512 * (n + 1)]))
    parts.append(blocks_for_features(alternate(w_gate, w_up)))
    for n in range(4):
        parts.append(blocks_for_rows(w_down[:, 512 * n:512 * (n + 1)]))
    return np.concatenate(parts, axis=0)


def shape_constants():
    c = np.zeros((P, C_N), np.float32)
    c[:, C_ID:C_ID + P] = np.eye(P)
    c[:, C_MASK + P:C_MASK + 2 * P] = np.where(np.arange(P)[None, :] <= np.arange(P)[:, None], 0.0, NEG)
    c[:, C_T:C_T + TOK] = np.arange(TOK)[None, :]
    c[:, C_ONES:C_ONES + P] = 1.0
    inv = (1.0 / (np.float32(10000.0) ** (np.arange(0, ROPE, 2, dtype=np.float32) / ROPE))).astype(np.float32)
    c[:, C_INVF] = np.tile(inv, 4)
    c[:, C_HALFPI] = np.float32(np.pi / 2)
    c[:, C_RMSEPS] = RMS_EPS
    c[:, C_LNEPS] = LN_EPS
    return c


def kernel(**inputs):
    import concourse.bacc as _bacc
    from concourse.bass_utils import run_bass_kernel_spmd as _run

    a = {k: np.asarray(v)[0] for k, v in inputs.items()}

    def by_state(v):
        v = v.reshape(PAIRS, P, *v.shape[2:])
        return np.moveaxis(v, 0, 1)

    log_dt = np.broadcast_to(a["ssm_log_dt"][:, None], (2 * PAIRS, STATE))
    c_of = [by_state(a[n].transpose(0, 2, 1)) for n in ("ssm_c_re", "ssm_c_im")]
    arrays = {
        "slabs": pack_slabs(a["w_in"], a["w_uq"], a["w_ukv"], a["w_glu"], a["w_out"], a["w_ffn_gate"],
                            a["w_ffn_up"], a["w_ffn_down"]),
        "x": a["x"],
        "pos": a["positions"][None, :],
        "consts": shape_constants(),
        "cols": np.concatenate([a[n].reshape(-1, P).T for n in ("q_norm_g", "kv_norm_g", "ssm_d", "ln1_g", "ln1_b")],
                               axis=1),
        "ssm": np.stack([by_state(v) for v in (a["ssm_lambda_re"], a["ssm_lambda_im"], log_dt)], axis=1),
        "ssm_b": np.stack([by_state(a[n]) for n in ("ssm_b_re", "ssm_b_im")], axis=1),
        "ssm_c": np.stack(c_of, axis=2),
        "ln_rows": np.stack([np.stack([a["ln1_g"], a["ln1_b"]]), np.stack([a["ln2_g"], a["ln2_b"]])]),
    }
    nc = _bacc.Bacc("TRN2", target_bir_lowering=False, num_devices=1)
    args, given = [], {}
    for name, v in arrays.items():
        v = np.ascontiguousarray(v)
        given[name] = v
        args.append(nc.dram_tensor(name, v.shape, mybir.dt.from_np(v.dtype), kind="ExternalInput").ap())
    out = nc.dram_tensor("out", (TOK, D), F32, kind="ExternalOutput").ap()
    build(nc, *args, out)
    r = _run(nc, [given], core_ids=[0])
    return r.results[0]["out"].reshape(1, TOK, D)
```

```python
from contextlib import ExitStack

import numpy as np
import concourse.bass as bass
from concourse import mybir

P = 128
TOK = 256
D = 2048
SSM_W, LORA, ROPE, HEADS = 1024, 512, 64, 16
GROUP, STATE = 16, 64
D_FF = 5632
ALPHA = 2.0 ** 0.25
LN_EPS, RMS_EPS = 1e-5, 1e-6
SM_SCALE = 1.0 / (192.0 ** 0.5)

KT = D // P
FT = D_FF // P
UT = SSM_W // P
CT = LORA // P
SLAB = 8 * P
RING = 4
HG = HEADS // 4
PAIRS = SSM_W // (2 * GROUP)

FRONT0, FRONT_PER = 0, 4
FRONT_TURNS, FRONT_HOLES = 9, 2
HEAD0 = FRONT0 + FRONT_PER * FRONT_TURNS
HEAD_PER, HEAD_HOLE = 24, 5
GLU0 = HEAD0 + HEAD_PER * HG
GLU_PER = 4
OUT0 = GLU0 + GLU_PER * 8
OUT_PER = 8
FFN0 = OUT0 + OUT_PER * 4
FFN_PER, FFN_TURNS = 8, FT // 2
DOWN0 = FFN0 + FFN_PER * FFN_TURNS
DOWN_PER = 22
HEAD_REAL = HEAD_PER - 1
D_HEAD0 = HEAD0 - FRONT_HOLES
D_GLU0 = D_HEAD0 + HEAD_REAL * HG
D_OUT0 = D_GLU0 + 32
D_FFN0 = D_OUT0 + 32
D_DOWN0 = D_FFN0 + FFN_PER * FFN_TURNS

C_ID, C_MASK, C_T, C_ONES, C_INVF, C_HALFPI, C_RMSEPS, C_LNEPS = 0, 128, 384, 640, 768, 769, 770, 771
C_N = 772
P_CG, P_D, P_G1, P_B1 = 0, 8, 16, 32
P_N = 48

MAGIC = 12582912.0
TWO_PI = 6.283185
INV_2PI = 0.15915494309189535
PI_A, PI_B, PI_C = 6.28125, 1.93500518798828125e-3, 3.0199159819567e-07
NEG = -1.0e30

F32 = mybir.dt.float32
F32R = mybir.dt.float32r
I32 = mybir.dt.int32
ALU = mybir.AluOpType
ACT = mybir.ActivationFunctionType

DVE_HEAD_STEPS = 92
DVE_GLU_STEPS = 4
DVE_OUT_STEPS = 2


class Steps:

    def __init__(self, eng, sem):
        self.eng, self.sem, self.base, self.n = eng, sem, 0, 0

    def __call__(self, ins):
        ins.then_inc(self.sem, 1)
        self.n += 1

    def wait(self):
        self.eng.wait_ge(self.sem, self.base + self.n)

    def enter(self, i, per):
        self.start = self.base + self.n
        self.base, self.n = i * per + self.start, 0

    def leave(self, turns, per):
        assert self.n == per, f"{self.n} steps a turn, not {per}"
        self.base, self.n = self.start + turns * per, 0


def build(nc, slabs, x, pos, consts, cols, ssm, ssm_b, ssm_c, ln_rows, out):
    with ExitStack() as ctx:
        def sem(name):
            return ctx.enter_context(nc.semaphore(name))

        base = 16512

        def at(name, off, shape, dt=F32):
            return nc.alloc_sbuf_tensor_at(name, shape, dt, offset=off)

        o = base
        raw = at("raw", o, [P, RING, SLAB]); o += RING * SLAB * 4
        whi = at("whi", o, [P, RING, SLAB], F32R); o += RING * SLAB * 4
        wlo = at("wlo", o, [P, RING, SLAB], F32R); o += RING * SLAB * 4
        cst = at("cst", o, [P, C_N]); o += 3104
        col = at("col", o, [P, P_N]); o += 192
        stats = at("stats", o, [P, 2, 4, 6]); o += 192
        moments = at("moments", o, [P, 2, 2]); o += 32
        rstd = at("rstd", o, [P, 2]); o += 32
        sm = at("sm", o, [P, 8]); o += 32
        start = at("start", o, [P, 8]); o += 32
        a0 = o
        xT = at("xT", a0, [P, KT, 2, TOK], F32R)
        rows = at("rows", a0, [P, 2, D])
        gb = at("gb", a0 + 16384, [P, 2, D])
        a1 = a0 + 32768
        cT = at("cT", a1, [P, 2 * CT, 2, TOK], F32R)
        cosT = at("cosT", a1 + 16384, [P, 4, TOK])
        sinT = at("sinT", a1 + 20480, [P, 4, TOK])
        prod = at("prod", a1 + 24576, [P, 4, 2 * TOK])
        mixT = at("mixT", a1, [P, KT, 2, TOK], F32R)
        hT = at("hT", a1, [P, KT, 2, TOK], F32R)
        a2 = a1 + 32768
        states = at("states", a2, [P, 2, 2 * TOK])
        tmp = at("tmp", a2, [P, 4, TOK])
        a3 = a2 + 4096
        act = at("act", a3, [P, FT, 2, TOK], F32R)
        o = a3
        mla = at("mla", o, [P, KT, TOK])
        xrow = at("xrow", o, [P, 2, D]); o += 16384
        gate = at("gate", o, [P, KT, TOK]); o += 16384
        zT = at("zT", o, [P, 18, TOK])
        qT = at("qT", o, [P, 4, TOK])
        kT = at("kT", o + 4096, [P, 4, TOK]); o += 18432
        scan = at("scan", o, [P, 2, 2 * TOK])
        yT = at("yT", o, [P, UT, 2, TOK], F32R); o += 4096
        bT = at("bT", o, [P, UT, 2, P]); o += 8192
        cP = at("cP", o, [P, PAIRS, 2, GROUP]); o += 4096
        bslot = at("bslot", o, [P, 2, 2, P])
        tmpB = at("tmpB", o, [P, 7, TOK]); o += 2048
        cslot = at("cslot", o, [P, 8, 2, 2 * GROUP]); o += 2048
        uslot = at("uslot", o, [P, 2, TOK]); o += 2048
        prob = at("prob", o, [P, 384]); o += 1536
        probT = at("probT", o, [P, 384]); o += 1536
        gsum = at("gsum", o, [P, 2, TOK]); o += 2048
        ropecs = at("ropecs", o, [P, 2, TOK]); o += 2048
        sp = at("ssm_small", o, [P, 12, PAIRS]); o += 1536
        vT = at("vT", o, [P, 2, 4 * P]); o += 4096
        qr = at("qr", o, [P, 2, TOK]); o += 2048
        assert o <= a3 + FT * 2 * TOK * 4 and a3 + FT * 2 * TOK * 4 <= nc.sbuf_usable_end
        bpar = at("bpar", a1, [P, 2, PAIRS, GROUP])
        bprod = at("bprod", a1 + 4096, [P, 4, PAIRS * GROUP])
        bpad = at("bpad", a1 + 16384, [P, 2, PAIRS * 2 * GROUP])
        posi = at("posi", a2, [P, TOK], I32)
        ang = at("ang", a2 + 1024, [P, 3, TOK])
        squares = at("squares", a1 + 24576, [P, 8, TOK])
        rinv = at("rinv", a2, [P, 2, TOK])

        ps = ctx.enter_context(nc.psum_tensor("ps", [P, 8, 512], F32))
        GEMM, BU, YP, SC, PT, OP = 0, 2, 4, 5, 6, 7
        Y_ORDER = (0, 2, 4, 6, 1, 3, 5, 7)
        H_POOL = (9, 11, 13)
        BT_BANKS = (2, 3, 4, 7)

        OUT_CUT = ((0, 512, 1024), (0, 768, 1536))

        ident = cst[:, C_ID:C_ID + P]
        tvals = cst[:, C_T:C_T + TOK]

        raw_ready = [sem(f"raw_ready{s}") for s in range(RING)]
        hi_ready, lo_ready, slab_used = sem("hi_ready"), sem("lo_ready"), sem("slab_used")
        half_done, gemm_free = sem("half_done"), sem("gemm_free")
        in_x = [sem(f"in_x{n}") for n in range(4)]
        in_ident, in_cst, in_ssm, in_small, in_rows, in_gb = sem("in_ident"), sem("in_cst"), sem("in_ssm"), sem("in_small"), sem("in_rows"), sem("in_gb")
        out_stored = sem("out_stored")
        dve_step, act_step = sem("dve_step"), sem("act_step")
        xt_psum, xt_hi, xt_lo = sem("xt_psum"), sem("xt_hi"), sem("xt_lo")
        ssm_exp, ssm_phase, ssm_trig, b_padded, bt_psum = (sem(n) for n in (
            "ssm_exp", "ssm_phase", "ssm_trig", "b_padded", "bt_psum"))
        rope_phase, rope_trig = sem("rope_phase"), sem("rope_trig")
        sq_ready, ss_psum, rms_root, c_ready, c_hi, c_lo = (sem(n) for n in (
            "sq_ready", "ss_psum", "rms_root", "c_ready", "c_hi", "c_lo"))
        slots_ready, phase_ready, trig_ready, bu_psum, rotated, states_ready, c_done = (
            sem(n) for n in ("slots_ready", "phase_ready", "trig_ready", "bu_psum", "rotated",
                             "states_ready", "c_done"))
        y_free = sem("y_free")
        qk_ready, scores, max_ready, exp_done, prob_ready, pt_psum, pt_copied = (
            sem(n) for n in ("qk_ready", "scores", "max_ready", "exp_done", "prob_ready",
                             "pt_psum", "pt_copied"))
        o_psum, o_read, gate_done = (sem(n) for n in (
            "o_psum", "o_read", "gate_done"))
        y_act, y_hi, y_lo = sem("y_act"), sem("y_hi"), sem("y_lo")
        glu_tanh, mix_sum, mix_hi, mix_lo = (sem(n) for n in (
            "glu_tanh", "mix_sum", "mix_hi", "mix_lo"))
        var_ready, root_ready, normed, h_psum, h_f32, h_hi, h_lo, h_lo_pool, h_rows = (sem(n) for n in (
            "var_ready", "root_ready", "normed", "h_psum", "h_f32", "h_hi", "h_lo", "h_lo_pool", "h_rows"))
        ffn_silu, ffn_prod, act_hi, act_lo, out_ready = (sem(n) for n in (
            "ffn_silu", "ffn_prod", "act_hi", "act_lo", "out_ready"))
        shift_ready, out_normed, out_scaled, out_ready_pool = (sem(n) for n in (
            "shift_ready", "out_normed", "out_scaled", "out_ready_pool"))

        block = ctx.enter_context(nc.Block())

        @block.sync
        def _(sy):
            def load(v, at_dram, s):
                sy.wait_ge(lo_ready, v - (RING - 1))
                sy.dma_start(raw[:, s:s + 1, :], slabs[bass.ds(at_dram, 1)].rearrange("a p n -> p a n")
                             ).then_inc(raw_ready[s], 16)

            def skip(v, s):
                sy.wait_ge(lo_ready, v - (RING - 1))
                sy.sem_inc(raw_ready[s], 16)

            x_v = x.rearrange("(t p) d -> p t d", p=P)

            def load_x(n):
                cut = slice(n * 512, (n + 1) * 512)
                sy.dma_start(xrow[:, :, cut], x_v[:, :, cut]).then_inc(in_x[n], 16)

            def first_slab(s):
                sy.dma_start(raw[:, s:s + 1, :], slabs[s:s + 1].rearrange("a p n -> p a n")
                             ).then_inc(raw_ready[s], 16)
            sy.dma_start(cst[:, 0:P], consts[:, 0:P]).then_inc(in_ident, 16)
            load_x(0)
            load_x(1)
            first_slab(0)
            load_x(2)
            load_x(3)
            first_slab(1)
            sy.dma_start(sp[:, 0:3, :], ssm).then_inc(in_ssm, 16)
            sy.dma_start(cst[:, P:C_N], consts[:, P:C_N]).then_inc(in_cst, 16)
            first_slab(2)
            first_slab(3)
            load(4, 4, 0)
            load(5, 5, 1)
            sy.dma_start(bpar[:], ssm_b).then_inc(in_small, 16)
            load(6, 6, 2)
            sy.dma_start(cP[:], ssm_c).then_inc(in_small, 16)
            sy.dma_start(col[:], cols).then_inc(in_small, 16)
            sy.dma_start(posi[:], pos.to_broadcast([P, TOK])).then_inc(in_small, 16)
            load(7, 7, 3)
            with sy.Fori(2, FRONT_TURNS - 1) as i:
                for k in range(FRONT_PER):
                    load(i * FRONT_PER + k, i * FRONT_PER + k, k)
            for k in range(FRONT_PER):
                v = (FRONT_TURNS - 1) * FRONT_PER + k
                if k < FRONT_PER - FRONT_HOLES:
                    load(v, v, k)
                else:
                    skip(v, k)
            with sy.Fori(0, HG) as i:
                for k in range(HEAD_PER):
                    v = i * HEAD_PER + HEAD0 + k
                    if k == HEAD_HOLE:
                        skip(v, k % RING)
                    else:
                        load(v, i * HEAD_REAL + D_HEAD0 + k - (k > HEAD_HOLE), k % RING)
            with sy.Fori(0, 4) as i:
                for k in range(4):
                    load(i * 4 + GLU0 + k, i * 4 + D_GLU0 + k, k)
                sy.wait_ge(slab_used, GLU0)
                sy.dma_start(rows[:, :, bass.ds(i * 512, 512)],
                             x_v[:, :, bass.ds(i * 512, 512)]).then_inc(in_rows, 16)
            with sy.Fori(0, 4) as i:
                for k in range(4):
                    load(i * 4 + (GLU0 + 16) + k, i * 4 + (D_GLU0 + 16) + k, k)
                sy.dma_start(gb[:, :, bass.ds(i * 512, 512)],
                             ln_rows[0:1, :, bass.ds(i * 512, 512)].to_broadcast([P, 2, 512])).then_inc(in_gb, 16)
            with sy.Fori(0, 8) as i:
                for k in range(4):
                    load(i * 4 + OUT0 + k, i * 4 + D_OUT0 + k, k)
            for k in range(FFN_PER):
                load(FFN0 + k, D_FFN0 + k, k % RING)
            with sy.Fori(1, FFN_TURNS) as i:
                for k in range(FFN_PER):
                    load(i * FFN_PER + FFN0 + k, i * FFN_PER + D_FFN0 + k, k % RING)
            sy.wait_ge(h_rows, 4)
            sy.dma_start(gb[:], ln_rows[1:2].rearrange("a b n -> a (b n)").to_broadcast([P, 2 * D])
                         .rearrange("p (b n) -> p b n", b=2)).then_inc(in_gb, 16)
            with sy.Fori(0, DOWN_PER) as i:
                for k in range(4):
                    load(i * 4 + DOWN0 + k, i * 4 + D_DOWN0 + k, k)
            out_v = out.rearrange("(t p) d -> p t d", p=P)

            def store(t, c0, c1):
                sy.dma_start(out_v[:, t, c0:c1], rows[:, t, c0:c1]).then_inc(out_stored, 16)
            for t, (c0, c1, c2) in enumerate(OUT_CUT):
                sy.wait_ge(out_ready, 2 * t + 1)
                store(t, c0, c1)
                if t == 0:
                    sy.wait_ge(out_ready, 2)
                    store(0, c1, c2)
                sy.wait_ge(out_ready_pool, t + 1)
                store(t, c2, D)
            sy.wait_ge(out_ready, 4)
            store(1, c1, c2)
            sy.wait_ge(out_stored, 6 * 16)

        def low_part(eng, unit, v, s, empty_after=0):
            eng.wait_ge(hi_ready, v + 1)
            unit.tensor_tensor(wlo[:, s, :], raw[:, s, :], whi[:, s, :].bitcast(F32), ALU.subtract
                               ).then_inc(lo_ready, 1 + empty_after)

        def wait_h_low(eng, k):
            if k in H_POOL:
                eng.wait_ge(h_lo_pool, H_POOL.index(k) + 1)
            else:
                eng.wait_ge(h_lo, k + 1 - sum(j < k for j in H_POOL))

        @block.gpsimd
        def _(po):
            nc.gpsimd.memset(bpad[:], 0.0).then_inc(b_padded, 1)
            nc.gpsimd.memset(cslot[:], 0.0).then_inc(b_padded, 1)
            po.wait_ge(lo_ready, 2)
            low_part(po, nc.gpsimd, 2, 2)
            low_part(po, nc.gpsimd, 3, 3)
            with po.Fori(1, FRONT_TURNS - 1) as i:
                for k in range(FRONT_PER):
                    low_part(po, nc.gpsimd, i * FRONT_PER + FRONT0 + k, k)
            low_part(po, nc.gpsimd, HEAD0 - 4, 0)
            low_part(po, nc.gpsimd, HEAD0 - 3, 1, FRONT_HOLES)
            with po.Fori(0, HG) as i:
                for k in range(HEAD_PER):
                    if k != HEAD_HOLE:
                        low_part(po, nc.gpsimd, i * HEAD_PER + HEAD0 + k, k % RING, int(k + 1 == HEAD_HOLE))
            with po.Fori(0, 8) as i:
                for k in range(GLU_PER):
                    low_part(po, nc.gpsimd, i * GLU_PER + GLU0 + k, k)
            for k in range(RING):
                low_part(po, nc.gpsimd, OUT0 + k, k)
            po.wait_ge(lo_ready, FFN0)
            for k in range(RING):
                low_part(po, nc.gpsimd, FFN0 + k, k)
            for k in H_POOL:
                po.wait_ge(h_hi, k + 1)
                nc.gpsimd.tensor_tensor(hT[:, k, 1, :], tmp[:, k % 4, :], hT[:, k, 0, :].bitcast(F32), ALU.subtract
                                        ).then_inc(h_lo_pool, 1)
            for k in range(RING, 2 * RING):
                low_part(po, nc.gpsimd, FFN0 + k, k % RING)
            po.wait_ge(in_gb, 64)
            for t in range(2):
                po.wait_ge(h_psum, 8)
                nc.gpsimd.tensor_tensor(rows[:, t, :], rows[:, t, :], gb[:, 0, :], ALU.mult).then_inc(h_rows, 1)
                po.wait_ge(h_rows, 2 * t + 1)
                nc.gpsimd.tensor_tensor(rows[:, t, :], rows[:, t, :], gb[:, 1, :], ALU.add).then_inc(h_rows, 1)
            po.wait_ge(in_gb, 80)
            for t in range(2):
                c2 = OUT_CUT[t][2]
                po.wait_ge(out_normed, t + 1)
                nc.gpsimd.tensor_tensor(rows[:, t, c2:], rows[:, t, c2:], gb[:, 0, c2:], ALU.mult).then_inc(out_scaled, 1)
                po.wait_ge(out_scaled, t + 1)
                nc.gpsimd.tensor_tensor(rows[:, t, c2:], rows[:, t, c2:], gb[:, 1, c2:], ALU.add).then_inc(out_ready_pool, 1)

        @block.scalar
        def _(ac):
            st = Steps(ac, act_step)

            def high(i, start, per, k, hole=(), empty=0):
                if k % per in hole:
                    return
                s = (start + k) % RING
                v = i * per + (start + k)
                if isinstance(i, int) and i == 0 and start + k < RING:
                    ac.wait_ge(raw_ready[s], 16)
                else:
                    ac.wait_ge(raw_ready[s], i * (16 * per // RING) + 16 * ((start + k) // RING + 1))
                    ac.wait_ge(slab_used, v - (RING - 1))
                while (k + 1 + empty) % per in hole:
                    empty += 1
                nc.scalar.activation(whi[:, s, :], raw[:, s, :], ACT.Copy).then_inc(hi_ready, 1 + empty)

            for k in range(8):
                ac.wait_ge(xt_psum, k + 1)
                nc.scalar.activation(xT[:, 2 * k:2 * k + 2, 0, :],
                                     ps[:, 2 + k % 6, :].rearrange("p (a t) -> p a t", a=2), ACT.Copy).then_inc(xt_hi, 1)
                if k == 3:
                    high(0, 0, FRONT_PER, 0)
            for k in (1, 2, 3):
                high(0, 0, FRONT_PER, k)
            ac.wait_ge(in_ssm, 16)
            ac.wait_ge(in_cst, 16)
            nc.scalar.activation(sp[:, 2, :], sp[:, 2, :], ACT.Exp).then_inc(ssm_exp, 1)
            high(0, FRONT0, FRONT_PER, RING)
            high(0, FRONT0, FRONT_PER, RING + 1)
            ac.wait_ge(ssm_phase, 1)
            nc.scalar.activation(sp[:, 3, :], sp[:, 3, :], ACT.Exp).then_inc(ssm_exp, 1)
            high(0, FRONT0, FRONT_PER, RING + 2)
            ac.wait_ge(ssm_phase, 2)
            nc.scalar.activation(sp[:, 5, :], sp[:, 4, :], ACT.Sin, scale=TWO_PI).then_inc(ssm_trig, 1)
            st(nc.scalar.activation(sp[:, 6, :], sp[:, 4, :], ACT.Abs))
            st.wait()
            nc.scalar.activation(sp[:, 6, :], sp[:, 6, :], ACT.Sin, scale=-TWO_PI,
                                 bias=cst[:, C_HALFPI:C_HALFPI + 1]).then_inc(ssm_trig, 1)
            high(0, FRONT0, FRONT_PER, RING + 3)

            with ac.Fori(1, 5) as i:
                for k in range(FRONT_PER):
                    high(i, FRONT0, FRONT_PER, k + RING)
            ac.wait_ge(rope_phase, 1)
            nc.scalar.activation(ropecs[:, 1, :], ang[:, 0, :], ACT.Sin).then_inc(rope_trig, 1)
            st(nc.scalar.activation(ropecs[:, 0, :], ang[:, 0, :], ACT.Abs))
            st.wait()
            nc.scalar.activation(ropecs[:, 0, :], ropecs[:, 0, :], ACT.Sin, scale=-1.0,
                                 bias=cst[:, C_HALFPI:C_HALFPI + 1]).then_inc(rope_trig, 1)
            for m in range(8):
                ac.wait_ge(gemm_free, m + 1)
                nc.scalar.activation(squares[:, m, :], zT[:, m, :], ACT.Square).then_inc(sq_ready, 1)
            for k in range(FRONT_PER):
                high(5, FRONT0, FRONT_PER, k + RING)
            for n in range(2):
                ac.wait_ge(ss_psum, n + 1)
                nc.scalar.activation(rinv[:, n, :], ps[:, SC + n, 0:TOK], ACT.Sqrt, scale=1.0 / LORA,
                                     bias=cst[:, C_RMSEPS:C_RMSEPS + 1]).then_inc(rms_root, 1)
            for m in range(8):
                ac.wait_ge(c_ready, m + 1)
                nc.scalar.activation(cT[:, m, 0, :], zT[:, m, :], ACT.Copy).then_inc(c_hi, 1)
                if m == 3:
                    high(6, FRONT0, FRONT_PER, RING)
            for k in range(1, FRONT_PER):
                high(6, FRONT0, FRONT_PER, k + RING)
            high(7, FRONT0, FRONT_PER, RING)
            high(7, FRONT0, FRONT_PER, RING + 1, empty=FRONT_HOLES)
            for k in range(FRONT_PER):
                high(8, FRONT0, FRONT_PER, k + RING)

            with ac.Fori(0, HG) as i:
                def hp(k):
                    high(i, HEAD0, HEAD_PER, k, (HEAD_HOLE,))

                ac.wait_ge(y_free, i * 2 + 1)
                nc.scalar.activation(bslot[:], bT[:, bass.ds(i * 2, 2)], ACT.Copy).then_inc(slots_ready, 1)
                for g in range(2):
                    nc.scalar.activation(cslot[g * 64:(g + 1) * 64, :, :, g * GROUP:(g + 1) * GROUP],
                                         cP[g * 64:(g + 1) * 64, bass.ds(i * 8, 8)], ACT.Copy).then_inc(slots_ready, 1)
                nc.scalar.activation(uslot[:], zT[:, bass.ds(i * 2 + 10, 2), :], ACT.Copy).then_inc(slots_ready, 1)

                def trig(n, part):
                    if part == 0:
                        ac.wait_ge(phase_ready, i * 2 + n + 1)
                        nc.scalar.activation(sinT[:], cosT[:], ACT.Sin, scale=TWO_PI).then_inc(trig_ready, 1)
                        return
                    ac.wait_ge(trig_ready, i * 6 + 3 * n + 1)
                    nc.scalar.activation(cosT[:], cosT[:], ACT.Abs).then_inc(trig_ready, 1)
                    ac.wait_ge(trig_ready, i * 6 + 3 * n + 2)
                    nc.scalar.activation(cosT[:], cosT[:], ACT.Sin, scale=-TWO_PI,
                                         bias=cst[:, C_HALFPI:C_HALFPI + 1]).then_inc(trig_ready, 1)

                def exps(h):
                    ac.wait_ge(max_ready, i * 4 + h + 1)
                    nc.scalar.activation(prob[:, 0:P], prob[:, 0:P], ACT.Exp, bias=sm[:, 2:3], scale=SM_SCALE,
                                         accum_out=sm[:, 4:5]).then_inc(exp_done, 1)
                    nc.scalar.activation(prob[:, P:384], prob[:, P:384], ACT.Exp, bias=sm[:, 3:4], scale=SM_SCALE,
                                         accum_out=sm[:, 5:6]).then_inc(exp_done, 1)

                def tanh_gate(g):
                    ac.wait_ge(gemm_free, i * 20 + 18 + 12 + g + 1)
                    to = mla[:, bass.ds(i * 4 + g, 1), :] if g < 4 else gate[:, bass.ds(i * 4 + g - 4, 1), :]
                    nc.scalar.activation(to, gsum[:, g % 2:g % 2 + 1, :], ACT.Tanh, scale=0.5).then_inc(gate_done, 1)

                def copy_pt(h):
                    ac.wait_ge(pt_psum, i * 4 + h + 1)
                    nc.scalar.activation(probT[:], ps[:, PT, 0:384], ACT.Copy).then_inc(pt_copied, 1)

                hp(4)
                hp(6)
                trig(0, 0)
                hp(7)
                trig(0, 1)
                for k in range(8, 11):
                    hp(k)
                for t in range(2):
                    if t == 0:
                        ac.wait_ge(half_done, i * 6 + 6)
                    else:
                        ac.wait_ge(slab_used, i * HEAD_PER + HEAD0 + 8)
                    nc.scalar.activation(vT[:, t, :], ps[:, t, :], ACT.Copy).then_inc(gemm_free, 1)
                hp(11)
                for g in range(8):
                    if g < 4:
                        exps(g)
                    if g == 3:
                        trig(1, 0)
                        trig(1, 1)
                    if g == 4:
                        ac.wait_ge(y_free, i * 2 + 2)
                    hp(12 + 2 * g), hp(13 + 2 * g)
                    tanh_gate(g)
                    if g < 4:
                        copy_pt(g)
                    if g == 4:
                        y_ = zT[:, bass.ds(i * 2 + 10, 1), :]
                        nc.scalar.activation(y_, y_, ACT.Gelu_apprx_tanh).then_inc(y_act, 1)

            def y_high(n):
                ac.wait_ge(y_act, n + 1)
                nc.scalar.activation(yT[:, Y_ORDER[n], 0, :], zT[:, 10 + Y_ORDER[n], :], ACT.Copy).then_inc(y_hi, 1)

            ac.wait_ge(states_ready, HG * 4)
            for n in range(4):
                y_high(n)
            for n in range(4, UT):
                if n == UT - 1:
                    y_high(UT - 2)
                m = Y_ORDER[n]
                ac.wait_ge(y_free, m + 2)
                nc.scalar.activation(zT[:, 10 + m, :], zT[:, 10 + m, :], ACT.Gelu_apprx_tanh).then_inc(y_act, 1)
                if 4 < n < UT - 1:
                    y_high(n - 1)
            y_high(UT - 1)

            def glu_high(i, k):
                high(i, GLU0, GLU_PER, k + RING)

            def gate_tanh(i, e):
                ac.wait_ge(gemm_free, i * 4 + 98 + 2 * e + 2)
                nc.scalar.activation(tmpB[:, 2 * e + 1, :], tmpB[:, 2 * e + 1, :], ACT.Tanh, scale=0.5).then_inc(glu_tanh, 1)

            def mix_high(kt):
                ac.wait_ge(mix_sum, kt + 1)
                nc.scalar.activation(mixT[:, bass.ds(kt, 1), 0, :], tmpB[:, 6:7, :], ACT.Copy, scale=0.5).then_inc(mix_hi, 1)

            def glu_turn(i, first):
                glu_high(i, 0)
                if not first:
                    mix_high(i * 2 - 1)
                glu_high(i, 1)
                gate_tanh(i, 0)
                glu_high(i, 2)
                mix_high(i * 2)
                glu_high(i, 3)
                gate_tanh(i, 1)
            glu_turn(0, True)
            with ac.Fori(1, 8) as i:
                glu_turn(i, False)
            mix_high(KT - 1)
            def norm_root(t, count):
                ac.wait_ge(var_ready, count)
                nc.scalar.activation(rstd[:, t:t + 1], moments[:, t, 1:2], ACT.Sqrt, bias=cst[:, C_LNEPS:C_LNEPS + 1]
                                     ).then_inc(root_ready, 1)

            def first_root():
                nc.scalar.activation(start[:, 5:6], cst[:, C_ONES:C_ONES + 1], ACT.Sqrt)

            with ac.Fori(0, 3) as i:
                for k in range(OUT_PER):
                    high(i, OUT0, OUT_PER, k + RING)
            for k in range(RING):
                high(3, OUT0, OUT_PER, k + RING)
            first_root()
            norm_root(0, 1)
            for k in range(RING, OUT_PER):
                high(3, OUT0, OUT_PER, k + RING)
            norm_root(1, 2)
            for k in range(KT):
                ac.wait_ge(h_f32, k + 1)
                nc.scalar.activation(hT[:, k, 0, :], tmp[:, k % 4, :], ACT.Copy).then_inc(h_hi, 1)
                if k == 10:
                    high(0, FFN0, FFN_PER, RING)

            def ffn_turn(i, first):
                for e in range(2):
                    if not (first and e == 0):
                        high(i, FFN0, FFN_PER, 4 * e + RING)
                    high(i, FFN0, FFN_PER, 4 * e + 1 + RING)
                    ac.wait_ge(gemm_free, i * 4 + 138 + 2 * e + 1)
                    nc.scalar.activation(tmp[:, 1, :], tmp[:, 0, :], ACT.Silu).then_inc(ffn_silu, 1)
                    high(i, FFN0, FFN_PER, 4 * e + 2 + RING)
                    high(i, FFN0, FFN_PER, 4 * e + 3 + RING)
                    ac.wait_ge(ffn_prod, i * 2 + e + 1)
                    nc.scalar.activation(act[:, bass.ds(i * 2 + e, 1), 0, :], tmp[:, 3:4, :], ACT.Copy).then_inc(act_hi, 1)
            ffn_turn(0, True)
            with ac.Fori(1, FFN_TURNS) as i:
                ffn_turn(i, False)
            with ac.Fori(0, DOWN_PER - 1) as i:
                for k in range(4):
                    high(i, DOWN0, 4, k + RING)
            first_root()
            for t in range(2):
                norm_root(t, 3 + t)
                ac.wait_ge(shift_ready, t + 1)
                c2 = OUT_CUT[t][2]
                nc.scalar.activation(rows[:, t, c2:], rows[:, t, c2:], ACT.Identity, bias=sm[:, t:t + 1],
                                     scale=rstd[:, t:t + 1]).then_inc(out_normed, 1)

        @block.tensor
        def _(pe):
            mm = nc.tensor.matmul

            def weights_in(v):
                pe.wait_ge(lo_ready, v + 1)

            def bank_free(m):
                if not (isinstance(m, int) and m < 2):
                    pe.wait_ge(gemm_free, m - 1)

            def feature_tile(bank, s, b, src, kts, first, last):
                for n, kt in enumerate(kts):
                    hi = whi[:, s, (b + n) * P:(b + n + 1) * P]
                    lo = wlo[:, s, (b + n) * P:(b + n + 1) * P]
                    mm(ps[:, bank, :], hi, src[:, kt].rearrange("p a t -> p (a t)"),
                       start=(first and n == 0), stop=False)
                    done = last and n == len(kts) - 1
                    ins = mm(ps[:, bank, TOK:512], lo, src[:, kt, 0, :], start=False, stop=done)
                return ins

            def row_tile(bank, s, t, src, kts, first, last):
                for n, kt in enumerate(kts):
                    hi, lo = whi[:, s, n * 512:(n + 1) * 512], wlo[:, s, n * 512:(n + 1) * 512]
                    xh, xl = src[:, kt, 0, t * P:(t + 1) * P], src[:, kt, 1, t * P:(t + 1) * P]
                    mm(ps[:, bank, :], xh, hi, start=(first and n == 0), stop=False)
                    mm(ps[:, bank, :], xh, lo, start=False, stop=False)
                    ins = mm(ps[:, bank, :], xl, hi, start=False, stop=(last and n == len(kts) - 1))
                return ins

            pe.wait_ge(in_ident, 16)
            for k in range(8):
                pe.wait_ge(in_x[k // 2], 16)
                if k >= 6:
                    pe.wait_ge(xt_lo, k - 5)
                for a in range(2):
                    for t in range(2):
                        kt = 2 * k + a
                        ins = nc.tensor.transpose(ps[:, 2 + k % 6, a * TOK + t * P:a * TOK + (t + 1) * P],
                                                  xrow[:, t, kt * P:(kt + 1) * P], ident)
                ins.then_inc(xt_psum, 1)

            def front_half(i, e, h, empty_after=0):
                weights_in(i * 4 + 2 * e + h)
                feature_tile(e, 2 * e + h, 0, xT, range(8 * h, 8 * h + 8), h == 0, h == 1
                             ).then_inc(slab_used, 1 + empty_after)

            def front_turn(i):
                for e in range(2):
                    bank_free(i * 2 + e)
                    front_half(i, e, 0)
                    front_half(i, e, 1)

            pe.wait_ge(xt_lo, 4)
            front_half(0, 0, 0)
            pe.wait_ge(xt_lo, 8)
            front_half(0, 0, 1)
            front_half(0, 1, 0)
            front_half(0, 1, 1)
            pe.wait_ge(in_cst, 16)
            with pe.Fori(1, 6) as i:
                front_turn(i)
            for n in range(2):
                for m in range(CT):
                    pe.wait_ge(sq_ready, CT * n + m + 1)
                    ins = mm(ps[:, SC + n, 0:TOK], cst[:, C_ONES:C_ONES + P], squares[:, CT * n + m, :],
                             start=(m == 0), stop=(m == CT - 1))
                ins.then_inc(ss_psum, 1)
            pe.wait_ge(b_padded, 6)
            for c in range(2):
                for q in range(2):
                    for n in range(4):
                        ins = nc.tensor.transpose(ps[:, BT_BANKS[2 * c + q], n * P:(n + 1) * P],
                                                  bpad[:, c, (4 * q + n) * P:(4 * q + n + 1) * P], ident)
                    ins.then_inc(bt_psum, 1)
            with pe.Fori(6, FRONT_TURNS - 1) as i:
                front_turn(i)
            bank_free(2 * (FRONT_TURNS - 1))
            front_half(FRONT_TURNS - 1, 0, 0)
            front_half(FRONT_TURNS - 1, 0, 1, FRONT_HOLES)

            with pe.Fori(0, HG) as i:
                v0, m0 = i * HEAD_PER + HEAD0, i * 20 + 18

                def latent_tiles(k, m, n_tiles, src0, extra=0):
                    weights_in(v0 + k)
                    for b in range(n_tiles):
                        bank_free(m0 + m + b)
                        ins = feature_tile((m + b) % 2, k % RING, CT * b, cT, range(src0, src0 + CT), True, True)
                        if b < n_tiles - 1:
                            ins.then_inc(half_done, 1)
                    ins.then_inc(slab_used, 1 + extra)

                def b_product(b):
                    if b == 0:
                        pe.wait_ge(slots_ready, i * 4 + 4)
                    pe.wait_ge(rotated, i * 4 + b + 1)
                    for c in range(2):
                        for e in range(2):
                            q = 2 * (b % 2) + e
                            ins = mm(ps[:, BU + e, c * TOK:(c + 1) * TOK], bslot[32 * q:32 * q + 32, b // 2, c, :],
                                     uslot[32 * q:32 * q + 32, b // 2, :], start=True, stop=True)
                    ins.then_inc(bu_psum, 1)

                def c_product(b):
                    pe.wait_ge(states_ready, i * 4 + b + 1)
                    if b % 2 == 0:
                        pe.wait_ge(y_free, i * 2 + b // 2 + 1)
                    for c in range(2):
                        for e in range(2):
                            q = 2 * (b % 2) + e
                            ins = mm(ps[32 * q:32 * q + 32, YP, 0:TOK], cslot[:, 2 * b + e, c, :],
                                     states[:, c, e * TOK:(e + 1) * TOK], start=(c == 0), stop=(c == 1))
                    ins.then_inc(c_done, 1)

                def score(h):
                    if h == 0:
                        pe.wait_ge(qk_ready, i + 1)
                    else:
                        pe.wait_ge(max_ready, i * 4 + h)
                    r = 64 * (h % 2)
                    for q, (c0, n) in enumerate(((0, P), (P, 2 * P))):
                        o_ = ps[:, SC, c0:c0 + n]
                        mm(o_, qT[:, h, q * P:(q + 1) * P], kT[:, h, 0:n], start=True, stop=False)
                        ins = mm(o_, qr[r:r + 64, h // 2, q * P:(q + 1) * P], zT[r:r + 64, 8, 0:n], start=False, stop=True)
                    ins.then_inc(scores, 1)

                def turn_probs(h):
                    pe.wait_ge(prob_ready, i * 4 + h + 1)
                    nc.tensor.transpose(ps[:, PT, 0:P], prob[:, 0:P], ident)
                    nc.tensor.transpose(ps[:, PT, P:2 * P], prob[:, P:2 * P], ident)
                    nc.tensor.transpose(ps[:, PT, 2 * P:3 * P], prob[:, 2 * P:3 * P], ident).then_inc(pt_psum, 1)

                def values(h):
                    pe.wait_ge(pt_copied, i * 4 + h + 1)
                    if h == 0:
                        pe.wait_ge(gemm_free, m0 + 12)
                    pe.wait_ge(o_read, i * 4 + h + 1)
                    mm(ps[:, OP, 0:TOK], vT[:, 0, h * P:(h + 1) * P], probT[:, 0:TOK], start=True, stop=False)
                    mm(ps[:, OP, P:TOK], vT[:, 1, h * P:(h + 1) * P], probT[:, TOK:384], start=False,
                       stop=True).then_inc(o_psum, 1)

                def gate_tile(g, between=None):
                    bank_free(m0 + 12 + g)
                    for h in range(2):
                        k = 8 + 2 * g + h
                        if h == 1 and between is not None:
                            b_product(between)
                        weights_in(v0 + k)
                        ins = feature_tile(g % 2, k % RING, 0, xT, range(8 * h, 8 * h + 8), h == 0, h == 1)
                        ins.then_inc(slab_used, 1)

                pe.wait_ge(c_lo, 8)
                latent_tiles(0, 0, 2, 0)
                latent_tiles(1, 2, 2, 0)
                b_product(0)
                latent_tiles(2, 4, 2, CT)
                latent_tiles(3, 6, 2, CT)
                latent_tiles(4, 8, 2, 0, extra=1)
                for h in range(2):
                    weights_in(v0 + 6 + h)
                    for t in range(2):
                        if h == 0:
                            bank_free(m0 + 10 + t)
                        ins = row_tile(t, (6 + h) % RING, t, cT, range(CT + 2 * h, CT + 2 * h + 2), h == 0, h == 1)
                        if h == 1 and t == 0:
                            ins.then_inc(half_done, 1)
                    ins.then_inc(slab_used, 1)
                score(0)
                gate_tile(0, between=1)
                turn_probs(0)
                score(1)
                c_product(0)
                gate_tile(1)
                values(0)
                turn_probs(1)
                score(2)
                gate_tile(2)
                values(1)
                turn_probs(2)
                score(3)
                gate_tile(3)
                c_product(1)
                values(2)
                turn_probs(3)
                b_product(2)
                gate_tile(4)
                values(3)
                b_product(3)
                gate_tile(5)
                gate_tile(6)
                c_product(2)
                gate_tile(7)
                c_product(3)

            for half in (0, 1):
                for e in range(2):
                    if half == 0:
                        bank_free(98 + e)
                        weights_in(GLU0 + e)
                    for n in range(4 * half, 4 * half + 4):
                        pe.wait_ge(y_lo, n + 1)
                        ins = feature_tile(e, e, Y_ORDER[n], yT, (Y_ORDER[n],), n == 0, n == UT - 1)
                    if half == 1:
                        ins.then_inc(slab_used, 1)

            def glu_tiles(i, e0):
                for e in range(e0, 4):
                    bank_free(i * 4 + (98 + e))
                    weights_in(i * GLU_PER + (GLU0 + e))
                    feature_tile(e % 2, e, 0, yT, range(UT), True, True).then_inc(slab_used, 1)
            glu_tiles(0, 2)
            with pe.Fori(1, 8) as i:
                glu_tiles(i, 0)

            def panel(src, src_ready, n_slabs, slot0, v, m):
                def part(k, t):
                    if t == 0:
                        pe.wait_ge(src_ready, 2 * k + 2)
                        weights_in(v + k)
                    if k == 0:
                        bank_free(m + t)
                    ins = row_tile(t, (slot0 + k) % RING, t, src, (2 * k, 2 * k + 1), k == 0, k == n_slabs - 1)
                    if t == 0 and k == n_slabs - 1:
                        ins.then_inc(half_done, 1)
                    if t == 1:
                        ins.then_inc(slab_used, 1)

                for k in range(n_slabs - RING):
                    part(k, 0)
                    part(k, 1)
                for t in range(2):
                    for k in range(n_slabs - RING, n_slabs):
                        part(k, t)

            with pe.Fori(0, 4) as i:
                panel(mixT, mix_lo, OUT_PER, 0, i * OUT_PER + OUT0, i * 2 + 130)

            def turn_h(k, t):
                for a in range(2):
                    ins = nc.tensor.transpose(ps[:, 2 + k % 6, a * TOK + t * P:a * TOK + (t + 1) * P],
                                              rows[:, t, (2 * k + a) * P:(2 * k + a + 1) * P], ident)
                if t == 1:
                    ins.then_inc(h_psum, 1)
            for t in range(2):
                for k in range(6):
                    pe.wait_ge(normed, 2 * t + k // 4 + 1)
                    turn_h(k, t)
            for k in (6, 7):
                pe.wait_ge(h_f32, 2 * (k - 6) + 2)
                for t in range(2):
                    turn_h(k, t)

            for k in range(KT):
                h, n = k // 8, k % 8
                if k == 0:
                    bank_free(138)
                    bank_free(139)
                wait_h_low(pe, k)
                for e in range(2):
                    if n == 0:
                        weights_in(FFN0 + 2 * e + h)
                    ins = feature_tile(e, 2 * e + h, n, hT, (k,), k == 0, k == KT - 1)
                    if e == 0 and n == 7:
                        ins.then_inc(slab_used, 1)
                    if e == 1 and k == KT - 1:
                        ins.then_inc(slab_used, 2)

            def ffn_tiles(i, e0):
                for e in range(e0, 4):
                    bank_free(i * 4 + 138 + e)
                    for h in range(2):
                        k = 2 * e + h
                        weights_in(i * FFN_PER + FFN0 + k)
                        feature_tile(e % 2, k % RING, 0, hT, range(8 * h, 8 * h + 8), h == 0, h == 1
                                     ).then_inc(slab_used, 1)
            ffn_tiles(0, 2)
            with pe.Fori(1, FFN_TURNS) as i:
                ffn_tiles(i, 0)

            with pe.Fori(0, 2) as i:
                for p in range(2):
                    panel(act, act_lo, DOWN_PER, DOWN_PER * p, i * (2 * DOWN_PER) + DOWN0 + DOWN_PER * p,
                          i * 4 + (138 + 2 * FT) + 2 * p)

        @block.vector
        def _(ve):
            st = Steps(ve, dve_step)
            V = nc.vector

            def tile_sum(out_, bank, slab=None, half=None):
                if slab is not None:
                    ve.wait_ge(slab_used, slab + 1)
                else:
                    ve.wait_ge(half_done, half + 1)
                V.tensor_reduce(out_, ps[:, bank, :].rearrange("p (a t) -> p t a", a=2), mybir.AxisListType.X, ALU.add
                                ).then_inc(gemm_free, 1)

            for k in range(8):
                ve.wait_ge(xt_hi, k + 1)
                V.tensor_tensor(xT[:, 2 * k:2 * k + 2, 1, :], ps[:, 2 + k % 6, :].rearrange("p (a t) -> p a t", a=2),
                                xT[:, 2 * k:2 * k + 2, 0, :].bitcast(F32), ALU.subtract).then_inc(xt_lo, 1)
                if k == 3:
                    low_part(ve, V, 0, 0)
            low_part(ve, V, 1, 1)

            def front_sums(i, e):
                tile_sum(zT[:, i * 2 + e + 1, :], e, i * 4 + 2 * e + 1)

            re, im, dt = sp[:, 0, :], sp[:, 1, :], sp[:, 2, :]
            mag, theta, sn, cs = sp[:, 3, :], sp[:, 4, :], sp[:, 5, :], sp[:, 6, :]
            w = [sp[:, 7 + n, :] for n in range(5)]

            def s5_angle():
                ve.wait_ge(ssm_exp, 1)
                V.tensor_tensor(mag, re, dt, ALU.mult).then_inc(ssm_phase, 1)
                st(V.tensor_tensor(w[0], im, dt, ALU.mult)); st.wait()
                st(V.tensor_scalar(w[0], w[0], INV_2PI, None, ALU.mult)); st.wait()
                st(V.tensor_scalar(w[1], w[0], MAGIC, None, ALU.add)); st.wait()
                st(V.tensor_scalar(w[1], w[1], MAGIC, None, ALU.subtract)); st.wait()
                V.tensor_tensor(theta, w[0], w[1], ALU.subtract).then_inc(ssm_phase, 1)
                st(V.tensor_tensor(w[2], re, re, ALU.mult))
                st(V.tensor_tensor(w[3], im, im, ALU.mult)); st.wait()
                st(V.tensor_tensor(w[2], w[2], w[3], ALU.add)); st.wait()
                st(V.reciprocal(w[2], w[2]))

            def s5_coefficient():
                ve.wait_ge(ssm_trig, 2)
                st(V.tensor_tensor(cs, mag, cs, ALU.mult))
                st(V.tensor_tensor(sn, mag, sn, ALU.mult)); st.wait()
                st(V.tensor_scalar(cs, cs, -1.0, None, ALU.add)); st.wait()
                st(V.tensor_tensor(w[0], cs, re, ALU.mult))
                st(V.tensor_tensor(w[1], sn, im, ALU.mult)); st.wait()
                st(V.tensor_tensor(w[0], w[0], w[1], ALU.add))
                st(V.tensor_tensor(w[4], sn, re, ALU.mult))
                st(V.tensor_tensor(w[3], cs, im, ALU.mult)); st.wait()
                st(V.tensor_tensor(w[1], w[4], w[3], ALU.subtract))
                st(V.tensor_tensor(w[0], w[0], w[2], ALU.mult)); st.wait()
                st(V.tensor_tensor(w[1], w[1], w[2], ALU.mult))

            def wide(a):
                return a.rearrange("p (n o) -> p n o", o=1).to_broadcast([P, PAIRS, GROUP])
            pr = [bprod[:, n, :].rearrange("p (a b) -> p a b", a=PAIRS) for n in range(4)]

            def bbar_products():
                st.wait()
                ve.wait_ge(in_small, 64)
                st(V.tensor_tensor(pr[0], bpar[:, 0], wide(w[0]), ALU.mult))
                st(V.tensor_tensor(pr[1], bpar[:, 1], wide(w[1]), ALU.mult))
                st(V.tensor_tensor(pr[2], bpar[:, 1], wide(w[0]), ALU.mult))
                st(V.tensor_tensor(pr[3], bpar[:, 0], wide(w[1]), ALU.mult))

            def bbar():
                st.wait()
                ve.wait_ge(b_padded, 2)
                for g in range(2):
                    half = slice(64 * g, 64 * g + 64)
                    for c, (one, two, op) in enumerate(((0, 1, ALU.subtract), (2, 3, ALU.add))):
                        V.tensor_tensor(bpad[half, c].rearrange("p (a b) -> p a b", a=PAIRS)[:, :, g * GROUP:(g + 1) * GROUP],
                                        pr[one][half], pr[two][half], op).then_inc(b_padded, 1)
                st(V.tensor_scalar(cP[:, :, 1, :], cP[:, :, 1, :], -1.0, None, ALU.mult))

            def rope_angle():
                st(V.tensor_copy(ang[:, 0, :], posi[:])); st.wait()
                st(V.tensor_scalar(ang[:, 0, :], ang[:, 0, :], cst[:, C_INVF:C_INVF + 1], None, ALU.mult)); st.wait()
                st(V.tensor_scalar(ang[:, 1, :], ang[:, 0, :], INV_2PI, MAGIC, ALU.mult, ALU.add)); st.wait()
                st(V.tensor_scalar(ang[:, 1, :], ang[:, 1, :], MAGIC, None, ALU.subtract)); st.wait()
                for part in (PI_A, PI_B, PI_C):
                    st(V.scalar_tensor_tensor(ang[:, 0, :], ang[:, 1, :], -part, ang[:, 0, :], ALU.mult, ALU.add)); st.wait()
                V.tensor_scalar(ang[:, 0, :], ang[:, 0, :], 3.1415925, -3.1415925, ALU.min, ALU.max).then_inc(rope_phase, 1)

            for n, set_up in enumerate((s5_angle, s5_coefficient, bbar_products, bbar, rope_angle)):
                tile_sum(zT[:, n, :], n % 2, 2 * n + 1)
                set_up()
            for n in (5, 6, 7, 8):
                tile_sum(zT[:, n, :], n % 2, 2 * n + 1)

            front_sums(4, 1)
            front_sums(5, 0)
            front_sums(5, 1)
            cosr, sinr = ropecs[:, 0, :], ropecs[:, 1, :]

            def rotate(t1, t2, moves, signal):
                a, b, c, d = gsum[:, 0, :], gsum[:, 1, :], states[:, 1, 0:TOK], states[:, 1, TOK:]
                st(V.tensor_tensor(a, t1, cosr, ALU.mult))
                st(V.tensor_tensor(b, t2, sinr, ALU.mult))
                st(V.tensor_tensor(c, t1, sinr, ALU.mult))
                st(V.tensor_tensor(d, t2, cosr, ALU.mult)); st.wait()
                for second, r, to in moves:
                    one, two = (c, d) if second else (a, b)
                    ins = V.tensor_tensor(to, one[r:r + 32], two[r:r + 32], ALU.add if second else ALU.subtract)
                ins.then_inc(signal, 1)

            for c in range(2):
                for q in range(2):
                    ve.wait_ge(bt_psum, 2 * c + q + 1)
                    st(V.tensor_copy(bT[:, 4 * q:4 * q + 4, c, :],
                                     ps[:, BT_BANKS[2 * c + q], :].rearrange("p (a b) -> p a b", a=4)))
            for n in range(2):
                ve.wait_ge(rms_root, n + 1)
                st(V.reciprocal(rinv[:, n, :], rinv[:, n, :])); st.wait()
                for m in range(CT * n, CT * n + CT):
                    V.scalar_tensor_tensor(zT[:, m, :], zT[:, m, :], col[:, P_CG + m:P_CG + m + 1], rinv[:, n, :],
                                           ALU.mult, ALU.mult).then_inc(c_ready, 1)
            front_sums(6, 0)
            for m in range(8):
                ve.wait_ge(c_hi, m + 1)
                V.tensor_tensor(cT[:, m, 1, :], zT[:, m, :], cT[:, m, 0, :].bitcast(F32), ALU.subtract).then_inc(c_lo, 1)
            ve.wait_ge(gemm_free, 9)
            for r in range(0, P, 32):
                other = r + 32 if r % 64 == 0 else r - 32
                st(V.tensor_copy(zT[r:r + 32, 9, :], zT[other:other + 32, 8, :]))
            ve.wait_ge(rope_trig, 2)
            st(V.tensor_tensor(gsum[:, 0, :], zT[:, 8, :], cosr, ALU.mult)); st.wait()
            st(V.tensor_tensor(gsum[:, 1, :], zT[:, 9, :], sinr, ALU.mult)); st.wait()
            for r in range(0, P, 32):
                op = ALU.subtract if r % 64 == 0 else ALU.add
                st(V.tensor_tensor(zT[r:r + 32, 8, :], gsum[r:r + 32, 0, :], gsum[r:r + 32, 1, :], op))
            st.wait()
            front_sums(6, 1)

            def phases(i, n, part):
                if part == 0:
                    for e in range(4):
                        st(V.tensor_scalar(sinT[:, e, :], tvals, theta_of(i, 4 * n + e), MAGIC, ALU.mult, ALU.add))
                elif part == 1:
                    st.wait()
                    st(V.tensor_scalar(sinT[:], sinT[:], MAGIC, None, ALU.subtract))
                else:
                    if part == 2:
                        st.wait()
                    for e in (0, 1) if part == 2 else (2, 3):
                        ins = V.scalar_tensor_tensor(cosT[:, e, :], tvals, theta_of(i, 4 * n + e), sinT[:, e, :],
                                                     ALU.mult, ALU.subtract)
                        if e == 3:
                            ins.then_inc(phase_ready, 1)
                        else:
                            st(ins)

            def theta_of(i, pair):
                return sp[:, 4, bass.ds(i * 8 + pair, 1)]

            for e in range(2):
                front_sums(7, e)
            for n, s_ in enumerate((c_done, rotated, o_read, y_free)):
                V.memset(start[:, n:n + 1], 0.0).then_inc(s_, 1)
            ve.wait_ge(slab_used, HEAD0)
            V.tensor_reduce(zT[:, 9 + UT, :], ps[:, 0, :].rearrange("p (a t) -> p t a", a=2), mybir.AxisListType.X, ALU.add
                            ).then_inc(gemm_free, 2)

            with ve.Fori(0, HG) as i:
                st.enter(i, DVE_HEAD_STEPS)
                v0, m0 = i * HEAD_PER + HEAD0, i * 20 + 18
                xR, xI = scan[:, 0], scan[:, 1]
                sR, sI = states[:, 0], states[:, 1]

                def trig_of(b):
                    return cosT[:, 2 * (b % 2):2 * (b % 2) + 2, :], sinT[:, 2 * (b % 2):2 * (b % 2) + 2, :]

                def of_pairs(a):
                    return a.rearrange("p (a t) -> p a t", a=2)

                def turn_back(b, half):
                    c_, s_ = trig_of(b)
                    uR, uI = ps[:, BU:BU + 2, 0:TOK], ps[:, BU:BU + 2, TOK:512]
                    if half == 0:
                        if b % 2 == 0:
                            ve.wait_ge(trig_ready, i * 6 + 3 * (b // 2) + 3)
                        else:
                            ve.wait_ge(states_ready, i * 4 + b)
                        ve.wait_ge(bu_psum, i * 4 + b + 1)
                        st(V.tensor_tensor(of_pairs(prod[:, 0]), uR, c_, ALU.mult))
                        st(V.tensor_tensor(of_pairs(prod[:, 1]), uI, s_, ALU.mult))
                    else:
                        st(V.tensor_tensor(of_pairs(prod[:, 2]), uI, c_, ALU.mult))
                        V.tensor_tensor(of_pairs(prod[:, 3]), uR, s_, ALU.mult).then_inc(rotated, 1)

                def combine(b):
                    ve.wait_ge(rotated, i * 4 + b + 2)
                    st(V.tensor_tensor(prod[:, 0], prod[:, 0], prod[:, 1], ALU.add))
                    st(V.tensor_tensor(prod[:, 2], prod[:, 2], prod[:, 3], ALU.subtract))

                def recur(b, e):
                    if e == 0:
                        st.wait()
                    a_ = sp[:, 3, bass.ds(i * 8 + (2 * b + e), 1)].to_broadcast([P, TOK])
                    cut = slice(e * TOK, (e + 1) * TOK)
                    st(V.tensor_tensor_scan(xR[:, cut], a_, prod[:, 0, cut], 0.0, ALU.mult, ALU.add))
                    st(V.tensor_tensor_scan(xI[:, cut], a_, prod[:, 2, cut], 0.0, ALU.mult, ALU.add))

                def turn_forward(b, half):
                    c_, s_ = trig_of(b)
                    if half == 0:
                        st.wait()
                        st(V.tensor_tensor(of_pairs(prod[:, 0]), of_pairs(xR), c_, ALU.mult))
                        st(V.tensor_tensor(of_pairs(prod[:, 1]), of_pairs(xI), s_, ALU.mult))
                        st(V.tensor_tensor(of_pairs(prod[:, 2]), of_pairs(xI), c_, ALU.mult))
                    else:
                        st(V.tensor_tensor(of_pairs(prod[:, 3]), of_pairs(xR), s_, ALU.mult)); st.wait()
                        ve.wait_ge(c_done, i * 4 + b + 1)
                        st(V.tensor_tensor(sR, prod[:, 0], prod[:, 1], ALU.subtract))
                        V.tensor_tensor(sI, prod[:, 2], prod[:, 3], ALU.add).then_inc(states_ready, 1)

                def y_tile(n):
                    ve.wait_ge(c_done, i * 4 + 2 * n + 3)
                    ins = V.scalar_tensor_tensor(zT[:, bass.ds(i * 2 + (10 + n), 1), :].rearrange("p a t -> p (a t)"),
                                                 uslot[:, n, :], col[:, bass.ds(i * 2 + (P_D + n), 1)],
                                                 ps[:, YP, 0:TOK], ALU.mult, ALU.add)
                    ins.then_inc(y_free, 1)

                def softmax_max(h):
                    ve.wait_ge(scores, i * 4 + h + 1)
                    V.memset(start[:, 4:5], 0.0)
                    st(V.tensor_tensor_reduce(prob[:, 0:P], ps[:, SC, 0:P], cst[:, C_MASK + P:C_MASK + 2 * P], 1.0,
                                              NEG, ALU.add, ALU.max, sm[:, 0:1]))
                    st(V.tensor_tensor_reduce(prob[:, P:384], ps[:, SC, P:384], cst[:, C_MASK:C_MASK + 2 * P], 1.0,
                                              NEG, ALU.add, ALU.max, sm[:, 1:2])); st.wait()
                    V.tensor_scalar(sm[:, 2:4], sm[:, 0:2], -SM_SCALE, None, ALU.mult).then_inc(max_ready, 1)

                def normalise(h):
                    ve.wait_ge(exp_done, i * 8 + 2 * h + 2)
                    st(V.reciprocal(sm[:, 4:6], sm[:, 4:6])); st.wait()
                    st(V.tensor_scalar(prob[:, 0:P], prob[:, 0:P], sm[:, 4:5], None, ALU.mult))
                    V.tensor_scalar(prob[:, P:384], prob[:, P:384], sm[:, 5:6], None, ALU.mult).then_inc(prob_ready, 1)

                def gate_sum(g):
                    if g >= 2:
                        ve.wait_ge(gate_done, i * 8 + g - 1)
                    tile_sum(gsum[:, g % 2, :], g % 2, v0 + 9 + 2 * g)

                def head_out(h):
                    ve.wait_ge(o_psum, i * 4 + h + 1)
                    ve.wait_ge(gate_done, i * 8 + h + 1)
                    g_ = mla[:, bass.ds(i * 4 + h, 1), :].rearrange("p a t -> p (a t)")
                    V.scalar_tensor_tensor(g_, g_, 1.0, ps[:, OP, 0:TOK], ALU.add, ALU.mult).then_inc(o_read, 1)

                def latent_sum(k, to, h):
                    if h % 2 == 0:
                        tile_sum(to[:, h, :], 0, half=i * 6 + k + h // 2)
                    else:
                        tile_sum(to[:, h, :], 1, slab=v0 + k + h // 2)

                latent_sum(0, qT, 0)
                latent_sum(0, qT, 1)
                phases(i, 0, 0)
                latent_sum(0, qT, 2)
                phases(i, 0, 1)
                latent_sum(0, qT, 3)
                phases(i, 0, 2)
                latent_sum(2, kT, 0)
                phases(i, 0, 3)
                latent_sum(2, kT, 1)
                latent_sum(2, kT, 2)
                latent_sum(2, kT, 3)
                tile_sum(states[:, 0, 0:TOK], 0, half=i * 6 + 4)
                tile_sum(states[:, 0, TOK:], 1, slab=v0 + 4)
                ve.wait_ge(gemm_free, m0 + 10)
                rotate(states[:, 0, 0:TOK], states[:, 0, TOK:],
                       [(second, 32 * h, qr[64 * (h % 2) + 32 * second:64 * (h % 2) + 32 * second + 32, h // 2, :])
                        for h in range(4) for second in range(2)], qk_ready)
                turn_back(0, 0)
                turn_back(0, 1)
                combine(0)
                recur(0, 0)
                recur(0, 1)
                softmax_max(0)
                turn_forward(0, 0)
                normalise(0)
                turn_forward(0, 1)
                gate_sum(0)
                softmax_max(1)
                turn_back(1, 0)
                turn_back(1, 1)
                normalise(1)
                combine(1)
                gate_sum(1)
                recur(1, 0)
                head_out(0)
                softmax_max(2)
                recur(1, 1)
                normalise(2)
                turn_forward(1, 0)
                gate_sum(2)
                turn_forward(1, 1)
                head_out(1)
                softmax_max(3)
                for part in range(4):
                    phases(i, 1, part)
                normalise(3)
                gate_sum(3)
                y_tile(0)
                head_out(2)
                turn_back(2, 0)
                turn_back(2, 1)
                combine(2)
                recur(2, 0)
                gate_sum(4)
                recur(2, 1)
                turn_forward(2, 0)
                head_out(3)
                turn_forward(2, 1)
                gate_sum(5)
                turn_back(3, 0)
                turn_back(3, 1)
                combine(3)
                gate_sum(6)
                recur(3, 0)
                recur(3, 1)
                turn_forward(3, 0)
                turn_forward(3, 1)
                gate_sum(7)
                y_tile(1)
            st.leave(HG, DVE_HEAD_STEPS)

            for n, m in enumerate(Y_ORDER):
                ve.wait_ge(y_hi, n + 1)
                V.tensor_tensor(yT[:, m, 1, :], zT[:, 10 + m, :], yT[:, m, 0, :].bitcast(F32), ALU.subtract).then_inc(y_lo, 1)

            def mix_tile(kt, e):
                ve.wait_ge(glu_tanh, kt + 1)
                st(V.scalar_tensor_tensor(tmpB[:, 4, :], tmpB[:, 2 * e + 1, :], 1.0, tmpB[:, 2 * e, :], ALU.add, ALU.mult)); st.wait()
                st(V.scalar_tensor_tensor(tmpB[:, 5:6, :], gate[:, bass.ds(kt, 1), :], 1.0, tmpB[:, 4:5, :],
                                          ALU.add, ALU.mult)); st.wait()
                V.scalar_tensor_tensor(tmpB[:, 6:7, :], tmpB[:, 5:6, :], 0.5, mla[:, bass.ds(kt, 1), :],
                                       ALU.mult, ALU.add).then_inc(mix_sum, 1)
                ve.wait_ge(mix_hi, kt + 1)
                V.scalar_tensor_tensor(mixT[:, bass.ds(kt, 1), 1, :], tmpB[:, 6:7, :], 0.5,
                                       mixT[:, bass.ds(kt, 1), 0, :].bitcast(F32), ALU.mult, ALU.subtract
                                       ).then_inc(mix_lo, 1)
                ve.wait_ge(mix_lo, kt + 1)

            def glu_turn(i, first):
                v = i * GLU_PER + GLU0
                tile_sum(tmpB[:, 0, :], 0, v)
                if not first:
                    mix_tile(i * 2 - 1, 1)
                tile_sum(tmpB[:, 1, :], 1, v + 1)
                tile_sum(tmpB[:, 2, :], 0, v + 2)
                mix_tile(i * 2, 0)
                tile_sum(tmpB[:, 3, :], 1, v + 3)
            glu_turn(0, True)
            with ve.Fori(1, 8) as i:
                st.enter(i - 1, DVE_GLU_STEPS)
                glu_turn(i, False)
            st.leave(7, DVE_GLU_STEPS)
            mix_tile(KT - 1, 1)

            def residual(n, t, m, half, v_last):
                if t == 0:
                    ve.wait_ge(half_done, half + 1)
                else:
                    ve.wait_ge(slab_used, v_last + 1)
                r_ = rows[:, t, bass.ds(n * 512, 512)]
                V.scalar_tensor_tensor(r_, r_, ALPHA, ps[:, t, :], ALU.mult, ALU.add).then_inc(gemm_free, 1)
                ve.wait_ge(gemm_free, m + t + 1)
                st(V.bn_stats(stats[:, t, bass.ds(n, 1), :].rearrange("p a b -> p (a b)"), r_))

            def statistics(t):
                st.wait()
                V.bn_aggr(moments[:, t, :], stats[:, t, :, :].rearrange("p a b -> p (a b)")).then_inc(var_ready, 1)

            def inverse_root(t, count):
                ve.wait_ge(root_ready, count)
                st(V.reciprocal(rstd[:, t:t + 1], rstd[:, t:t + 1])); st.wait()

            ve.wait_ge(in_rows, 64)
            ve.wait_ge(lo_ready, OUT0 + RING)

            def out_low(i, k):
                low_part(ve, V, i * OUT_PER + OUT0 + RING + k, k % RING)

            def out_residual(i, t):
                residual(i, t, i * 2 + 130, i + 6 * HG, i * OUT_PER + OUT0 + OUT_PER - 1)

            with ve.Fori(0, 3) as i:
                st.enter(i, DVE_OUT_STEPS)
                for k in range(RING):
                    out_low(i, k)
                out_residual(i, 0)
                out_low(i, 4)
                out_low(i, 5)
                out_residual(i, 1)
                out_low(i, 6)
                out_low(i, 7)
            st.leave(3, DVE_OUT_STEPS)
            for k in range(RING):
                out_low(3, k)
            for t in range(2):
                out_residual(3, t)
                statistics(t)
                inverse_root(t, 1 + t)
                for h in range(2):
                    r_ = rows[:, t, h * 1024:(h + 1) * 1024]
                    V.tensor_scalar(r_, r_, moments[:, t, 0:1], rstd[:, t:t + 1], ALU.subtract, ALU.mult
                                    ).then_inc(normed, 1)

            def h_low(k):
                if k in H_POOL:
                    return
                ve.wait_ge(h_hi, k + 1)
                V.tensor_tensor(hT[:, k, 1, :], tmp[:, k % 4, :], hT[:, k, 0, :].bitcast(F32), ALU.subtract).then_inc(h_lo, 1)

            for k in range(KT):
                if k % 2 == 0:
                    ve.wait_ge(h_psum, k // 2 + 1)
                if k >= 4:
                    wait_h_low(ve, k - 4)
                V.tensor_scalar(tmp[:, k % 4, :], ps[:, 2 + (k // 2) % 6, (k % 2) * TOK:(k % 2 + 1) * TOK],
                                col[:, P_G1 + k:P_G1 + k + 1], col[:, P_B1 + k:P_B1 + k + 1], ALU.mult, ALU.add
                                ).then_inc(h_f32, 1)
                if k >= 2:
                    h_low(k - 2)
            h_low(KT - 2)
            h_low(KT - 1)

            def ffn_turn(i, first):
                for e in range(2):
                    n = i * 2 + e
                    m = i * 4 + 138 + 2 * e
                    v = i * FFN_PER + FFN0 + 4 * e

                    def lows(*ks):
                        if first and e == 0:
                            return
                        if first and ks[0] == 0:
                            ve.wait_ge(lo_ready, FFN0 + 2 * RING)
                        for k in ks:
                            low_part(ve, V, i * FFN_PER + FFN0 + RING + 4 * e + k, k)
                    lows(0, 1)
                    tile_sum(tmp[:, 0, :], 0, v + 1)
                    lows(2)
                    tile_sum(tmp[:, 2, :], 1, v + 3)
                    lows(3)
                    ve.wait_ge(gemm_free, m + 2)
                    ve.wait_ge(ffn_silu, n + 1)
                    V.tensor_tensor(tmp[:, 3, :], tmp[:, 1, :], tmp[:, 2, :], ALU.mult).then_inc(ffn_prod, 1)
                    ve.wait_ge(act_hi, n + 1)
                    V.tensor_tensor(act[:, bass.ds(n, 1), 1, :], tmp[:, 3:4, :],
                                    act[:, bass.ds(n, 1), 0, :].bitcast(F32), ALU.subtract).then_inc(act_lo, 1)
                    ve.wait_ge(act_lo, n + 1)
            ffn_turn(0, True)
            with ve.Fori(1, FFN_TURNS) as i:
                ffn_turn(i, False)

            ve.wait_ge(h_rows, 4)

            def down_low(n, k):
                low_part(ve, V, DOWN0 + n * DOWN_PER + k, (n * DOWN_PER + k) % RING)

            def down_residual(n, t):
                residual(n, t, n * 2 + (138 + 2 * FT), n + 6 * HG + 4, n * DOWN_PER + DOWN0 + DOWN_PER - 1)

            for n in range(4):
                for k in range(RING, DOWN_PER):
                    down_low(n, k)
                if n < 3:
                    down_residual(n, 0)
                    down_low(n + 1, 0)
                    down_low(n + 1, 1)
                    down_residual(n, 1)
                    down_low(n + 1, 2)
                    down_low(n + 1, 3)
            for t in range(2):
                down_residual(3, t)
                statistics(t)
                inverse_root(t, 3 + t)
                if t == 0:
                    ve.wait_ge(in_gb, 80)
                V.scalar_tensor_tensor(sm[:, t:t + 1], moments[:, t, 0:1], -1.0, rstd[:, t:t + 1], ALU.mult, ALU.mult
                                       ).then_inc(shift_ready, 1)
                for c0, c1 in zip(OUT_CUT[t], OUT_CUT[t][1:]):
                    r_ = rows[:, t, c0:c1]
                    st(V.scalar_tensor_tensor(r_, r_, moments[:, t, 0:1], gb[:, 0, c0:c1], ALU.subtract, ALU.mult)); st.wait()
                    V.scalar_tensor_tensor(r_, r_, rstd[:, t:t + 1], gb[:, 1, c0:c1], ALU.mult, ALU.add).then_inc(out_ready, 1)


def blocks_for_features(w):
    k, m = w.shape
    t = w.reshape(k // P, P, m // P, P).transpose(2, 1, 0, 3).reshape(m // P, P, k)
    if k >= SLAB:
        return t.reshape(m // P, P, k // SLAB, SLAB).transpose(0, 2, 1, 3).reshape(-1, P, SLAB)
    n = SLAB // k
    return t.reshape(m // P // n, n, P, k).transpose(0, 2, 1, 3).reshape(-1, P, SLAB)


def blocks_for_rows(w):
    return w.reshape(-1, 2, P, 512).transpose(0, 2, 1, 3).reshape(-1, P, SLAB)


def pack_slabs(w_in, w_uq, w_ukv, w_glu, w_out, w_gate, w_up, w_down):
    o_q, o_kv = SSM_W, SSM_W + LORA
    o_kr = o_kv + LORA
    o_gs = o_kr + ROPE
    o_gm = o_gs + D
    half = ROPE // 2
    k_rope = w_in[:, o_kr:o_gs]
    parts = [blocks_for_features(np.concatenate([w_in[:, o_q:o_kr], k_rope, k_rope, w_in[:, :SSM_W]], axis=1))]
    uq = w_uq.reshape(LORA, HEADS, P + ROPE)
    ukv = w_ukv.reshape(LORA, HEADS, 2 * P)
    for g in range(HG):
        hs = slice(4 * g, 4 * g + 4)
        parts.append(blocks_for_features(uq[:, hs, :P].reshape(LORA, 512)))
        parts.append(blocks_for_features(ukv[:, hs, :P].reshape(LORA, 512)))
        parts.append(blocks_for_features(np.concatenate([uq[:, hs, P:P + half].reshape(LORA, P),
                                                         uq[:, hs, P + half:].reshape(LORA, P)], axis=1)))
        parts.append(blocks_for_rows(ukv[:, hs, P:].reshape(LORA, 512)))
        parts.append(blocks_for_features(w_in[:, o_gm + 512 * g:o_gm + 512 * (g + 1)]))
        parts.append(blocks_for_features(w_in[:, o_gs + 512 * g:o_gs + 512 * (g + 1)]))

    def alternate(a, b):
        k, m = a.shape
        return np.stack([a.reshape(k, m // P, P), b.reshape(k, m // P, P)], axis=2).reshape(k, 2 * m)
    parts.append(blocks_for_features(alternate(w_glu[:, :D], w_glu[:, D:])))
    for n in range(4):
        parts.append(blocks_for_rows(w_out[:, 512 * n:512 * (n + 1)]))
    parts.append(blocks_for_features(alternate(w_gate, w_up)))
    for n in range(4):
        parts.append(blocks_for_rows(w_down[:, 512 * n:512 * (n + 1)]))
    return np.concatenate(parts, axis=0)


def shape_constants():
    c = np.zeros((P, C_N), np.float32)
    c[:, C_ID:C_ID + P] = np.eye(P)
    c[:, C_MASK + P:C_MASK + 2 * P] = np.where(np.arange(P)[None, :] <= np.arange(P)[:, None], 0.0, NEG)
    c[:, C_T:C_T + TOK] = np.arange(TOK)[None, :]
    c[:, C_ONES:C_ONES + P] = 1.0
    inv = (1.0 / (np.float32(10000.0) ** (np.arange(0, ROPE, 2, dtype=np.float32) / ROPE))).astype(np.float32)
    c[:, C_INVF] = np.tile(inv, 4)
    c[:, C_HALFPI] = np.float32(np.pi / 2)
    c[:, C_RMSEPS] = RMS_EPS
    c[:, C_LNEPS] = LN_EPS
    return c


def kernel(**inputs):
    import concourse.bacc as _bacc
    from concourse.bass_utils import run_bass_kernel_spmd as _run

    a = {k: np.asarray(v)[0] for k, v in inputs.items()}

    def by_state(v):
        v = v.reshape(PAIRS, P, *v.shape[2:])
        return np.moveaxis(v, 0, 1)

    log_dt = np.broadcast_to(a["ssm_log_dt"][:, None], (2 * PAIRS, STATE))
    c_of = [by_state(a[n].transpose(0, 2, 1)) for n in ("ssm_c_re", "ssm_c_im")]
    arrays = {
        "slabs": pack_slabs(a["w_in"], a["w_uq"], a["w_ukv"], a["w_glu"], a["w_out"], a["w_ffn_gate"],
                            a["w_ffn_up"], a["w_ffn_down"]),
        "x": a["x"],
        "pos": a["positions"][None, :],
        "consts": shape_constants(),
        "cols": np.concatenate([a[n].reshape(-1, P).T for n in ("q_norm_g", "kv_norm_g", "ssm_d", "ln1_g", "ln1_b")],
                               axis=1),
        "ssm": np.stack([by_state(v) for v in (a["ssm_lambda_re"], a["ssm_lambda_im"], log_dt)], axis=1),
        "ssm_b": np.stack([by_state(a[n]) for n in ("ssm_b_re", "ssm_b_im")], axis=1),
        "ssm_c": np.stack(c_of, axis=2),
        "ln_rows": np.stack([np.stack([a["ln1_g"], a["ln1_b"]]), np.stack([a["ln2_g"], a["ln2_b"]])]),
    }
    nc = _bacc.Bacc("TRN2", target_bir_lowering=False, num_devices=1)
    args, given = [], {}
    for name, v in arrays.items():
        v = np.ascontiguousarray(v)
        given[name] = v
        args.append(nc.dram_tensor(name, v.shape, mybir.dt.from_np(v.dtype), kind="ExternalInput").ap())
    out = nc.dram_tensor("out", (TOK, D), F32, kind="ExternalOutput").ap()
    build(nc, *args, out)
    r = _run(nc, [given], core_ids=[0])
    return r.results[0]["out"].reshape(1, TOK, D)
```
